# Optimizing a Trainium2 kernel written in Bass

```python
import jax, jax.numpy as jnp
from jax import lax
import numpy as np

D_MODEL = 2048
BATCH = 1
SEQ = 256
DEPTH = 1

CHUNK = 64
HEAD_DIM = 128
N_MIX_HEADS = D_MODEL // HEAD_DIM
SB_HEADS = N_MIX_HEADS // 2
RET_HEADS = N_MIX_HEADS - SB_HEADS
SB_WIDTH = SB_HEADS * HEAD_DIM
RET_WIDTH = RET_HEADS * HEAD_DIM
MIX_WIDTH = SB_WIDTH + RET_WIDTH
IN_WIDTH = 3 * SB_WIDTH + 4 * RET_WIDTH
Q_BLOCK = 128
ROPE_THETA = 10000.0
PEER_HEADS = 8
PEER_KEYS = 128
PEER_EXPERTS = PEER_KEYS * PEER_KEYS
PEER_KEY_DIM = 256
PEER_HALF = PEER_KEY_DIM // 2
PEER_TOPK = 16
PEER_TOKEN_BLOCK = 128
LN_EPS = 1e-5
NORM_EPS = 1e-6
DEEPNORM_ALPHA = (2.0 * DEPTH) ** 0.25
DEEPNORM_BETA = (8.0 * DEPTH) ** -0.25

kernel_name = 'hybrid_sb_retention_peer_block'

def layer_norm(x, w, b):
    xf = x.astype(jnp.float32)
    mu = jnp.mean(xf, -1, keepdims=True)
    var = jnp.mean(jnp.square(xf - mu), -1, keepdims=True)
    y = (xf - mu) * lax.rsqrt(var + LN_EPS) * w.astype(jnp.float32) + b.astype(jnp.float32)
    return y.astype(x.dtype)

def to_heads(t, n_heads):
    b, s, _ = t.shape
    return t.reshape(b, s, n_heads, HEAD_DIM).transpose(0, 2, 1, 3).astype(jnp.float32)

def from_heads(t):
    b, h, s, d = t.shape
    return t.transpose(0, 2, 1, 3).reshape(b, s, h * d)

def rotary(t):
    s, d = t.shape[2], t.shape[3]
    inv_freq = ROPE_THETA ** (-jnp.arange(0, d, 2, dtype=jnp.float32) / d)
    ang = jnp.arange(s, dtype=jnp.float32)[:, None] * inv_freq[None, :]
    ang = jnp.concatenate([ang, ang], -1)
    t1, t2 = jnp.split(t, 2, axis=-1)
    return t * jnp.cos(ang) + jnp.concatenate([-t2, t1], -1) * jnp.sin(ang)

def stick_breaking_attention(q, k, v):
    b, h, s, d = q.shape
    scale = d ** -0.5
    outs = []
    for blk in range(s // Q_BLOCK):
        q0 = blk * Q_BLOCK
        kv_len = q0 + Q_BLOCK
        z = jnp.einsum('bhqd,bhkd->bhqk', q[:, :, q0:kv_len], k[:, :, :kv_len]) * scale
        q_pos = q0 + jnp.arange(Q_BLOCK)[:, None]
        k_pos = jnp.arange(kv_len)[None, :]
        mask = k_pos < q_pos
        log_1mb = jnp.where(mask, jax.nn.log_sigmoid(-z), 0.0)
        incl = jnp.cumsum(log_1mb, axis=-1)
        log_a = jax.nn.log_sigmoid(z) + incl[..., -1:] - incl
        a = jnp.where(mask, jnp.exp(log_a), 0.0)
        outs.append(jnp.einsum('bhqk,bhkd->bhqd', a, v[:, :, :kv_len]))
    return jnp.concatenate(outs, axis=2)

def retention(q, k, v):
    b, h, s, d = q.shape
    nc = s // CHUNK
    log_g = jnp.log1p(-(2.0 ** (-5.0 - jnp.arange(h, dtype=jnp.float32))))
    idx = jnp.arange(CHUNK, dtype=jnp.float32)
    intra_decay = jnp.exp(log_g[:, None, None] * jnp.abs(idx[:, None] - idx[None, :]))
    xi = jnp.exp(log_g[:, None] * (idx + 1.0))
    zeta = jnp.exp(log_g[:, None] * (CHUNK - 1.0 - idx))
    chunk_decay = jnp.exp(log_g * CHUNK)
    qc = q.reshape(b, h, nc, CHUNK, d)
    kc = (k * d ** -0.5).reshape(b, h, nc, CHUNK, d)
    vc = v.reshape(b, h, nc, CHUNK, v.shape[-1])
    scores = jnp.einsum('bhnid,bhnjd->bhnij', qc, kc) * intra_decay[None, :, None]
    intra = jnp.einsum('bhnij,bhnjv->bhniv', scores, vc)
    kv = jnp.einsum('bhnjd,bhnjv->nbhdv', kc * zeta[None, :, None, :, None], vc)

    def step(state, kv_n):
        return state * chunk_decay[None, :, None, None] + kv_n, state

    _, prev = lax.scan(step, jnp.zeros(kv.shape[1:], kv.dtype), kv)
    inter = jnp.einsum('bhnid,nbhdv->bhniv', qc, prev) * xi[None, :, None, :, None]
    return (intra + inter).reshape(b, h, s, -1)

def token_mixer(x, w_in, sb_norm_w, ret_norm_w, w_out):
    b, s, _ = x.shape
    proj = x @ w_in
    cuts = [SB_WIDTH, 2 * SB_WIDTH, 3 * SB_WIDTH, 3 * SB_WIDTH + RET_WIDTH,
            3 * SB_WIDTH + 2 * RET_WIDTH, 3 * SB_WIDTH + 3 * RET_WIDTH]
    sb_q, sb_k, sb_v, r_q, r_k, r_v, r_g = jnp.split(proj, cuts, axis=-1)
    sb = stick_breaking_attention(to_heads(sb_q, SB_HEADS), to_heads(sb_k, SB_HEADS), to_heads(sb_v, SB_HEADS))
    sb = sb * lax.rsqrt(jnp.mean(jnp.square(sb), -1, keepdims=True) + NORM_EPS)
    sb = from_heads(sb) * sb_norm_w.astype(jnp.float32)
    ret = retention(rotary(to_heads(r_q, RET_HEADS)), rotary(to_heads(r_k, RET_HEADS)), to_heads(r_v, RET_HEADS))
    mu = jnp.mean(ret, -1, keepdims=True)
    var = jnp.mean(jnp.square(ret - mu), -1, keepdims=True)
    ret = from_heads((ret - mu) * lax.rsqrt(var + NORM_EPS)) * ret_norm_w.astype(jnp.float32)
    ret = jax.nn.silu(r_g.astype(jnp.float32)) * ret
    mixed = jnp.concatenate([sb, ret], axis=-1).astype(x.dtype)
    return mixed @ w_out

def peer_ffn(x, w_pq, sub_keys, expert_u, expert_v):
    b, s, d = x.shape
    n_tok = b * s
    xt = x.reshape(n_tok, d)
    q = (xt @ w_pq).reshape(n_tok, PEER_HEADS, 2, PEER_HALF).astype(jnp.float32)
    scores = jnp.einsum('thcd,hckd->thck', q, sub_keys.astype(jnp.float32))
    s_top, i_top = lax.top_k(scores, PEER_TOPK)
    cand = (s_top[:, :, 0, :, None] + s_top[:, :, 1, None, :]).reshape(n_tok, PEER_HEADS, PEER_TOPK * PEER_TOPK)
    cand_idx = (i_top[:, :, 0, :, None] * PEER_KEYS + i_top[:, :, 1, None, :]).reshape(n_tok, PEER_HEADS, PEER_TOPK * PEER_TOPK)
    best, pos = lax.top_k(cand, PEER_TOPK)
    expert_idx = jnp.take_along_axis(cand_idx, pos, axis=-1)
    gate = jax.nn.softmax(best, axis=-1)
    nb = n_tok // PEER_TOKEN_BLOCK

    def block(args):
        xb, idx_b, g_b = args
        u = jnp.take(expert_u, idx_b, axis=0)
        act = jax.nn.gelu(jnp.einsum('thkd,td->thk', u, xb).astype(jnp.float32), approximate=False)
        v = jnp.take(expert_v, idx_b, axis=0)
        return jnp.einsum('thk,thkd->td', (g_b * act).astype(v.dtype), v)

    out = lax.map(block, (xt.reshape(nb, PEER_TOKEN_BLOCK, d),
                          expert_idx.reshape(nb, PEER_TOKEN_BLOCK, PEER_HEADS, PEER_TOPK),
                          gate.reshape(nb, PEER_TOKEN_BLOCK, PEER_HEADS, PEER_TOPK)))
    return out.reshape(b, s, d).astype(x.dtype)

def setup_inputs(seed: int = 0) -> dict:
    key = jax.random.key(seed)
    ks = jax.random.split(key, 14)
    f32 = jnp.float32

    def nrm(k, shape, scale):
        return scale * jax.random.normal(k, shape, f32)

    return {
        'x': jax.random.normal(ks[0], (BATCH, SEQ, D_MODEL), f32),
        'w_in': nrm(ks[1], (DEPTH, D_MODEL, IN_WIDTH), D_MODEL ** -0.5),
        'sb_norm_w': 1.0 + nrm(ks[2], (DEPTH, SB_WIDTH), 0.02),
        'ret_norm_w': 1.0 + nrm(ks[3], (DEPTH, RET_WIDTH), 0.02),
        'w_out': nrm(ks[4], (DEPTH, MIX_WIDTH, D_MODEL), DEEPNORM_BETA * MIX_WIDTH ** -0.5),
        'ln1_w': 1.0 + nrm(ks[5], (DEPTH, D_MODEL), 0.02),
        'ln1_b': nrm(ks[6], (DEPTH, D_MODEL), 0.02),
        'w_pq': nrm(ks[7], (DEPTH, D_MODEL, PEER_HEADS * PEER_KEY_DIM), D_MODEL ** -0.5),
        'sub_keys': nrm(ks[8], (DEPTH, PEER_HEADS, 2, PEER_KEYS, PEER_HALF), PEER_HALF ** -0.5),
        'expert_u': nrm(ks[9], (DEPTH, PEER_EXPERTS, D_MODEL), D_MODEL ** -0.5),
        'expert_v': nrm(ks[10], (DEPTH, PEER_EXPERTS, D_MODEL), DEEPNORM_BETA),
        'ln2_w': 1.0 + nrm(ks[11], (DEPTH, D_MODEL), 0.02),
        'ln2_b': nrm(ks[12], (DEPTH, D_MODEL), 0.02),
    }

def reference(x, w_in, sb_norm_w, ret_norm_w, w_out, ln1_w, ln1_b, w_pq, sub_keys,
              expert_u, expert_v, ln2_w, ln2_b):
    for layer in range(DEPTH):
        mix = token_mixer(x, w_in[layer], sb_norm_w[layer], ret_norm_w[layer], w_out[layer])
        x = layer_norm(DEEPNORM_ALPHA * x + mix, ln1_w[layer], ln1_b[layer])
        ffn = peer_ffn(x, w_pq[layer], sub_keys[layer], expert_u[layer], expert_v[layer])
        x = layer_norm(DEEPNORM_ALPHA * x + ffn, ln2_w[layer], ln2_b[layer])
    return x


_drawn_inputs = setup_inputs


def setup_inputs(seed=0):
    import zlib

    import numpy as np

    out = dict(_drawn_inputs(seed))
    spreads = {}
    factors = {'ret_norm_w': 3.145, 'ln2_w': 8.46, 'ln2_b': 8.457, 'sb_norm_w': 2.842}
    for name, (base, spread) in spreads.items():
        noise = np.random.default_rng([zlib.crc32(name.encode()), seed]).standard_normal(out[name].shape)
        drawn = base * np.exp(spread * noise) if base else spread * noise
        out[name] = __import__('jax').numpy.asarray(drawn.astype(out[name].dtype))
    for name, factor in factors.items():
        out[name] = (out[name] * factor).astype(out[name].dtype)
    return out
```

```python
from contextlib import ExitStack

import numpy as np

import concourse.bass as bass
from concourse import mybir

P = 128
SEQ, D = 256, 2048
TB = SEQ // P
KT = D // P
HD = 128
SBH, RTH = 8, 8
INW = 3 * SBH * HD + 4 * RTH * HD
CHUNK = 64
PH, PKEYS, TOPK = 8, 128, 16
SETS = 2 * PH
EXPERTS = PKEYS * PKEYS
NT = EXPERTS // P
COLS = 512
ALPHA = 2.0 ** 0.25
LN_EPS, NORM_EPS = 1e-5, 1e-6
SCALE = HD ** -0.5
BIG = 1e30
LOWEST = -3.4e38

G_IN, G_OUT, G_PQ = INW // COLS, D // COLS, D // COLS
Q_OUT = G_IN * KT
Q_PQ = Q_OUT + G_OUT * KT
Q_U = Q_PQ + G_PQ * KT
Q_V = Q_U + NT * 4
RAWS, SPLITS = 4, 4
F_X, F_MIX, F_KEYS, F_X1, F_Q = 0, 8, 16, 20, 28


def layer_kernel(nc, x, w_in, sb_norm_w, ret_norm_w, w_out, ln1_w, ln1_b, w_pq, sub_keys,
                 expert_u, expert_v, ln2_w, ln2_b, tables, small_tables, out):
    f32, f32r, u32 = mybir.dt.float32, mybir.dt.float32r, mybir.dt.uint32
    ACT, ALU, AX = mybir.ActivationFunctionType, mybir.AluOpType, mybir.AxisListType
    ctx = ExitStack()
    with ctx:
        base = 16512

        def at(name, shape, dt, offset):
            return nc.alloc_sbuf_tensor_at(name, [P, *shape], dt, offset=offset)

        A_HI, A_LO = base, base + 16384
        RAW, SPL = base + 32768, base + 49152
        KEEP = base + 65536
        W0 = 98272
        act_hi = at("act_hi", [KT, SEQ], f32r, A_HI)
        act_lo = at("act_lo", [KT, SEQ], f32r, A_LO)
        raw = at("raw", [RAWS, 2, COLS], f32, RAW)
        split_hi = at("split_hi", [SPLITS, COLS], f32r, SPL)
        split_lo = at("split_lo", [SPLITS, COLS], f32r, SPL + 8192)
        small = at("small", [2, P], f32, KEEP)
        picks_t = at("picks_t", [3, SEQ], f32, KEEP + 1024)
        stats = at("stats", [512], f32, KEEP + 4096)
        soft_a = at("soft_a", [2, 384], f32, KEEP + 6144)
        pick_n = at("pick_n", [3, TB, P], f32, KEEP + 6144)
        whalf_hi = at("whalf_hi", [2, SEQ], f32r, KEEP + 9216)
        whalf_lo = at("whalf_lo", [2, SEQ], f32r, KEEP + 11264)
        wexp = at("wexp", [NT, SEQ], f32, W0)
        proj = at("proj", [TB, INW], f32, W0)
        x_nat = at("x_nat", [TB, D], f32, W0 + 57344)
        mixed = at("mixed", [TB, D], f32, W0 + 73728)
        cst = at("cst", [4608], f32, W0 + 90112)
        norm_w = at("norm_w", [D], f32, W0 + 108544)
        qk_t = at("qk_t", [2, 2, SEQ], f32, W0 + 116736)
        z_sb = at("z_sb", [2, 384], f32, W0 + 120832)
        soft_l = at("soft_l", [2, 384], f32, W0 + 123904)
        soft_p = at("soft_p", [2, 384], f32, W0 + 126976)
        ln_w = at("ln_w", [D], f32, W0)
        ln_b = at("ln_b", [D], f32, W0 + 8192)
        q_nat = at("q_nat", [TB, D], f32, W0 + 16384)
        q_t = at("q_t", [KT, SEQ], f32, W0 + 32768)
        keys_t = at("keys_t", [SETS, PKEYS], f32, W0 + 49152)
        keys_nat = at("keys_nat", [SETS, HD], f32, W0 + 90112)
        scores = at("scores", [TB, SETS, PKEYS], f32, W0 + 98304)
        T0 = W0 + 114688
        idx_u = at("idx_u", [TB * PH, 2, TOPK], u32, T0)
        idx_f = at("idx_f", [TB * PH, 2, TOPK], f32, T0 + 2048)
        best = at("best", [TB * PH, TOPK], f32, T0 + 4096)
        pos_u = at("pos_u", [TB * PH, TOPK], u32, T0 + 5120)
        pos_f = at("pos_f", [2, TB * PH, TOPK], f32, T0 + 6144)
        pos_i = at("pos_i", [2, TB * PH, TOPK], u32, T0 + 8192)
        cand = at("cand", [TOPK, TOPK], f32, T0 + 10240)
        top_v = at("top_v", [2, TOPK], f32, T0 + 11264)
        rest = at("rest", [256], f32, T0 + 11392)
        onehot = at("onehot", [2 * TOPK, TOPK], f32, T0 + 12416)
        gsum = at("gsum", [2, TB * PH], f32, T0 + 14464)
        head_s = at("head_s", [2, PKEYS], f32, T0 + 14592)
        head_i = at("head_i", [2, TOPK], u32, T0 + 15616)
        head_b = at("head_b", [TOPK], f32, T0 + 15744)
        head_p = at("head_p", [TOPK], u32, T0 + 15808)
        rot_v = at("rot_v", [2, RTH, HD], f32, A_HI)
        rot_g = at("rot_g", [2, RTH, HD], f32, A_HI + 8192)
        square = at("square", [TB, D], f32, A_LO)
        key2_hot = at("key2_hot", [2, 4, P], f32, A_HI)
        key1_hot = at("key1_hot", [2, 4, P], f32, A_HI + 4096)
        ln2w = at("ln2w", [D], f32, A_HI)
        ln2b = at("ln2b", [D], f32, A_HI + 8192)
        x1_back = at("x1_back", [TB, D], f32, A_LO)
        y_out = at("y_out", [TB, D], f32, W0)

        ps = ctx.enter_context(nc.psum_tensor("ps", [P, 8, COLS], f32))
        x1_dram = nc.dram_tensor("x1_dram", (P, TB, D), f32, kind="Internal").ap()

        ident, iota = small[:, 0, :], small[:, 1, :]
        cos_t = cst[:, 0:256].rearrange("p (b d) -> p b d", b=TB)
        sin_t = cst[:, 256:512].rearrange("p (b d) -> p b d", b=TB)
        decay = cst[:, 512:3584].rearrange("p (h q) -> p h q", h=RTH)
        tri = cst[:, 3584:3712]
        ones = cst[:, 3712:3840]
        causal = cst[:, 3840:4224]
        masked = cst[:, 4224:4608]

        def sem(name):
            return ctx.enter_context(nc.semaphore(name))

        raw_ready = [sem(f"raw_ready{i}") for i in range(RAWS)]
        hi_ready = sem("hi_ready")
        lo_ready = sem("lo_ready")
        split_free = sem("split_free")
        acc_free = sem("acc_free")
        turned = sem("turned")
        turn_hi = sem("turn_hi")
        turn_done = sem("turn_done")
        u_turned = sem("u_turned")
        score_free = sem("score_free")
        x_in, tab_in, keys_in, ln1_in, ln2_in = (sem(n) for n in ("x_in", "tab_in", "keys_in", "ln1_in", "ln2_in"))
        norms_in, x1_out, x1_in, y_stored = (sem(n) for n in ("norms_in", "x1_out", "x1_in", "y_stored"))
        rot_q, rot_k = sem("rot_q"), sem("rot_k")
        qk_turned, q_out, k_out = sem("qk_turned"), sem("q_out"), sem("k_out")
        z_ready, c_ready, o_ready, o_out = sem("z_ready"), sem("c_ready"), sem("o_ready"), sem("o_out")
        z_copied, soft_ready, spm_ready, la_ready, a_ready = (
            sem(n) for n in ("z_copied", "soft_ready", "spm_ready", "la_ready", "a_ready"))
        gated = sem("gated")
        mixed_ready, x1_ready = sem("mixed_ready"), sem("x1_ready")
        var_ready, rstd_ready = sem("var_ready"), sem("rstd_ready")
        sc_ready, sc_out = sem("sc_ready"), sem("sc_out")
        best_ready, exp_ready, topk_done = sem("best_ready"), sem("exp_ready"), sem("topk_done")
        picks_turned, picks_ready = sem("picks_turned"), sem("picks_ready")
        dist_ready, hot1_ready, hot2_ready, gate_ready, gate_used = (
            sem(n) for n in ("dist_ready", "hot1_ready", "hot2_ready", "gate_ready", "gate_used"))
        abs_ready, carried = sem("abs_ready"), sem("carried")
        w_hi, w_lo = sem("w_hi"), sem("w_lo")
        halfexp = sem("halfexp")
        y_ready = sem("y_ready")
        v_chain, a_chain, g_chain = sem("v_chain"), sem("a_chain"), sem("g_chain")

        MEAN, VAR, RSTD, NHALF, SUMS = 0, 16, 48, 80, 112

        class Chain:

            def __init__(self, eng, s):
                self.eng, self.sem, self.n = eng, s, 0

            def step(self, instruction):
                self.n += 1
                instruction.then_inc(self.sem, 1)
                self.eng.wait_ge(self.sem, self.n)

        w_in_v = w_in.rearrange("l (k p) n -> (l p) k n", p=P)
        w_out_v = w_out.rearrange("l (k p) n -> (l p) k n", p=P)
        w_pq_v = w_pq.rearrange("l (k p) n -> (l p) k n", p=P)
        u_v = expert_u.rearrange("l e d -> (l e) d")
        v_v = expert_v.rearrange("l e d -> (l e) d")
        block = ctx.enter_context(nc.Block())

        @block.sync
        def _(sp):
            def dense(view, first_q, g, wait):
                for kk in range(KT // 2):
                    if wait or kk >= RAWS:
                        sp.wait_ge(lo_ready, g * KT + first_q + 2 * kk + 2 - 2 * RAWS)
                    sp.dma_start(raw[:, kk % RAWS, :, :], view[:, 2 * kk:2 * kk + 2, bass.ds(g * COLS, COLS)]
                                 ).then_inc(raw_ready[kk % RAWS], 16)

            def expert_half(view, j, hf, slot):
                sp.dma_start(raw[:, slot, :, :].rearrange("p a b -> p (a b)"),
                             view[bass.ds(j * P, P), hf * 1024:hf * 1024 + 1024]).then_inc(raw_ready[slot], 16)

            sp.dma_start(x_nat[:, :, :], x.rearrange("a (b p) d -> (a p) b d", p=P)).then_inc(x_in, 16)
            sp.dma_start(small[:, :, :], small_tables).then_inc(x_in, 16)
            dense(w_in_v, 0, 0, False)
            sp.dma_start(cst[:, :], tables).then_inc(tab_in, 16)
            sp.dma_start(norm_w[:, 0:SBH * HD], sb_norm_w.partition_broadcast(P)).then_inc(norms_in, 16)
            sp.dma_start(norm_w[:, SBH * HD:D], ret_norm_w.partition_broadcast(P)).then_inc(norms_in, 16)
            with sp.Fori(1, G_IN) as g:
                dense(w_in_v, 0, g, True)
            dense(w_out_v, Q_OUT, 0, True)
            sp.wait_ge(mixed_ready, TB)
            sp.dma_start(keys_nat[:, :, :], sub_keys.rearrange("l h c k d -> k (l h c) d")).then_inc(keys_in, 16)
            sp.dma_start(ln_w[:, :], ln1_w.partition_broadcast(P)).then_inc(ln1_in, 16)
            sp.dma_start(ln_b[:, :], ln1_b.partition_broadcast(P)).then_inc(ln1_in, 16)
            with sp.Fori(1, G_OUT) as g:
                dense(w_out_v, Q_OUT, g, True)
            dense(w_pq_v, Q_PQ, 0, True)
            sp.wait_ge(x1_ready, TB)
            sp.dma_start(x1_dram, x_nat[:, :, :]).then_inc(x1_out, 16)
            with sp.Fori(1, G_PQ) as g:
                dense(w_pq_v, Q_PQ, g, True)
            for n in range(RAWS):
                sp.wait_ge(lo_ready, Q_U - 2 * RAWS + 2 * n + 2)
                expert_half(u_v, n // 2, n % 2, n)
            with sp.Fori(1, NT // 2) as i:
                for n in range(RAWS):
                    sp.wait_ge(u_turned, i * 8 + (2 * n + 2 - 2 * RAWS))
                    expert_half(u_v, i * 2 + n // 2, n % 2, n)
            for n in range(RAWS):
                sp.wait_ge(u_turned, NT * 4 + 2 * n + 2 - 2 * RAWS)
                expert_half(v_v, n // 2, n % 2, n)
            sp.wait_ge(gate_used, SEQ // 4)
            sp.dma_start(ln2w[:, :], ln2_w.partition_broadcast(P)).then_inc(ln2_in, 16)
            sp.dma_start(ln2b[:, :], ln2_b.partition_broadcast(P)).then_inc(ln2_in, 16)
            sp.wait_ge(x1_out, 16)
            sp.dma_start(x1_back[:, :, :], x1_dram).then_inc(x1_in, 16)
            with sp.Fori(1, NT // 2) as i:
                for n in range(RAWS):
                    sp.wait_ge(lo_ready, i * 8 + (Q_V + 2 * n + 2 - 2 * RAWS))
                    expert_half(v_v, i * 2 + n // 2, n % 2, n)
            for b in range(TB):
                sp.wait_ge(y_ready, b + 1)
                sp.dma_start(out[0, b * P:(b + 1) * P, :], y_out[:, b, :]).then_inc(y_stored, 16)
            sp.wait_ge(y_stored, 16 * TB)

        @block.tensor
        def _(pe):
            pe.sem_inc(split_free, SPLITS)

            def turn(fill, sources):
                if fill >= 4:
                    pe.wait_ge(turn_done, fill - 3)
                for i, s in enumerate(sources):
                    last = nc.tensor.transpose(ps[:, 4 + fill % 4, i * P:(i + 1) * P], s, ident)
                last.then_inc(turned, 1)

            def three(acc, l_hi, l_lo, r_hi, r_lo, first, last):
                nc.tensor.matmul(acc, l_hi, r_hi, start=first, stop=False)
                nc.tensor.matmul(acc, l_hi, r_lo, start=False, stop=False)
                return nc.tensor.matmul(acc, l_lo, r_hi, start=False, stop=last)

            def dense(g, parity, first_q):
                pe.wait_ge(acc_free, g + 1)
                for k in range(KT):
                    pe.wait_ge(lo_ready, g * KT + (k + 1))
                    for b in range(TB):
                        c = slice(b * P, (b + 1) * P)
                        last = three(ps[:, 2 * parity + b, :], act_hi[:, k, c], act_lo[:, k, c],
                                     split_hi[:, k % SPLITS, :], split_lo[:, k % SPLITS, :], k == 0, k == KT - 1)
                    last.then_inc(split_free, 1)

            pe.wait_ge(x_in, 32)
            for f in range(8):
                turn(F_X + f, [x_nat[:, f // 4, (f % 4 * 4 + i) * P:(f % 4 * 4 + i + 1) * P] for i in range(4)])
            pe.wait_ge(turn_done, F_X + 8)
            with pe.Fori(0, G_IN // 2) as i:
                for s in range(2):
                    dense(i * 2 + s, s, 0)

            pe.wait_ge(tab_in, 16)
            pe.wait_ge(acc_free, G_IN + 2)
            heads = SBH + RTH

            def head_cols(it, kind):
                first = (0 if it < SBH else 3 * SBH * HD) + kind * SBH * HD + (it % SBH) * HD
                return slice(first, first + HD)

            def turn_qk(it):
                if it == SBH:
                    pe.wait_ge(rot_q, 1)
                    pe.wait_ge(rot_k, 1)
                if it >= 2:
                    pe.wait_ge(q_out, it - 1)
                    pe.wait_ge(k_out, it - 1)
                for n in range(4):
                    last = nc.tensor.transpose(ps[:, it % 2 * 4, n * P:(n + 1) * P],
                                               proj[:, n % 2, head_cols(it, n // 2)], ident)
                last.then_inc(qk_turned, 1)

            def z_product(it):
                bank, p = it % 2 * 4 + 1, it % 2
                pe.wait_ge(q_out, it + 1)
                pe.wait_ge(k_out, it + 1)
                if it >= 2:
                    pe.wait_ge(z_copied, it - 1) if it - 2 < SBH else pe.wait_ge(a_ready, it - 1)
                nc.tensor.matmul(ps[:, bank, 0:256], qk_t[:, p, 1, 0:P], qk_t[:, p, 0, :], start=True, stop=True)
                nc.tensor.matmul(ps[:, bank, 256:384], qk_t[:, p, 1, P:SEQ], qk_t[:, p, 0, P:SEQ],
                                 start=True, stop=True).then_inc(z_ready, 1)

            def suffix_sums(it):
                bank, p = it % 2 * 4 + 2, it % 2
                pe.wait_ge(spm_ready, it + 1)
                if it >= 2:
                    pe.wait_ge(la_ready, it - 1)
                nc.tensor.matmul(ps[:, bank, 0:256], tri, soft_p[:, p, 0:256], start=True, stop=False)
                nc.tensor.matmul(ps[:, bank, P:256], ones, soft_p[:, p, 256:384], start=False, stop=False)
                nc.tensor.matmul(ps[:, bank, 0:256], ident, masked[:, 0:256], start=False, stop=True)
                nc.tensor.matmul(ps[:, bank, 256:384], tri, soft_p[:, p, 256:384], start=True, stop=False)
                nc.tensor.matmul(ps[:, bank, 256:384], ident, masked[:, 256:384], start=False, stop=True
                                 ).then_inc(c_ready, 1)

            def values(it):
                bank, p = it % 2 * 4 + 3, it % 2
                pe.wait_ge(a_ready, it + 1)
                if it >= 2:
                    pe.wait_ge(o_out, it - 1)
                v = head_cols(it, 2)
                nc.tensor.matmul(ps[:, bank, 0:P], soft_a[:, p, 0:P], proj[:, 0, v], start=True, stop=True)
                nc.tensor.matmul(ps[:, bank, P:256], soft_a[:, p, P:256], proj[:, 0, v], start=True, stop=False)
                nc.tensor.matmul(ps[:, bank, P:256], soft_a[:, p, 256:384], proj[:, 1, v], start=False, stop=True
                                 ).then_inc(o_ready, 1)

            for s in range(heads + 3):
                if s < heads:
                    turn_qk(s)
                if 0 <= s - 1 < heads:
                    z_product(s - 1)
                if 0 <= s - 2 < SBH:
                    suffix_sums(s - 2)
                if 0 <= s - 3 < heads:
                    values(s - 3)

            for f in range(8):
                if f % 4 == 0:
                    pe.wait_ge(mixed_ready, f // 4 + 1)
                turn(F_MIX + f, [mixed[:, f // 4, (f % 4 * 4 + i) * P:(f % 4 * 4 + i + 1) * P] for i in range(4)])
            pe.wait_ge(turn_done, F_MIX + 8)
            with pe.Fori(0, G_OUT // 2) as i:
                for s in range(2):
                    dense(i * 2 + (G_IN + s), s, Q_OUT)

            pe.wait_ge(keys_in, 16)
            for f in range(4):
                turn(F_KEYS + f, [keys_nat[:, 4 * f + i, :] for i in range(4)])
            for f in range(8):
                if f % 4 == 0:
                    pe.wait_ge(x1_ready, f // 4 + 1)
                turn(F_X1 + f, [x_nat[:, f // 4, (f % 4 * 4 + i) * P:(f % 4 * 4 + i + 1) * P] for i in range(4)])
            pe.wait_ge(turn_done, F_X1 + 8)
            with pe.Fori(0, G_PQ // 2) as i:
                for s in range(2):
                    dense(i * 2 + (G_IN + G_OUT + s), s, Q_PQ)
            pe.wait_ge(acc_free, G_IN + G_OUT + G_PQ + 2)
            for f in range(8):
                turn(F_Q + f, [q_nat[:, f // 4, (f % 4 * 4 + i) * P:(f % 4 * 4 + i + 1) * P] for i in range(4)])
            pe.wait_ge(turn_done, F_Q + 8)
            for f in range(8):
                if f >= 2:
                    pe.wait_ge(sc_out, f - 1)
                for i in range(4):
                    s, b = f % 4 * 4 + i, f // 4
                    last = nc.tensor.matmul(ps[:, 2 + f % 2, i * P:(i + 1) * P], q_t[:, s, b * P:(b + 1) * P],
                                            keys_t[:, s, :], start=True, stop=True)
                last.then_inc(sc_ready, 1)

            def turn_u(n, q):
                if q % 2 == 0:
                    slot = q // 2 % RAWS
                    pe.wait_ge(raw_ready[slot], n * 2 + (16 * (Q_U // 8 + 1) - 2 * q))
                for i in range(4):
                    last = nc.tensor.transpose(ps[:, 4 + q % 4, i * P:(i + 1) * P],
                                               raw[:, q // 2 % RAWS, q % 2, i * P:(i + 1) * P], ident)
                last.then_inc(u_turned, 1)

            LEAD = 3

            def score_pair(n0, ahead):
                for q in range(8):
                    if q % 4 == 0:
                        pe.wait_ge(score_free, (n0 // 4 + q // 4 + 1) if isinstance(n0, int) else n0 // 4 + (q // 4 + 1))
                    if q + LEAD < ahead:
                        turn_u(n0 + (q + LEAD), (q + LEAD) % 8)
                    pe.wait_ge(lo_ready, n0 + (Q_U + q + 1))
                    for i in range(4):
                        last = three(ps[:, q // 4, 0:SEQ], split_hi[:, q % SPLITS, i * P:(i + 1) * P],
                                     split_lo[:, q % SPLITS, i * P:(i + 1) * P], act_hi[:, q % 4 * 4 + i, :],
                                     act_lo[:, q % 4 * 4 + i, :], q % 4 == 0 and i == 0, q % 4 == 3 and i == 3)
                    last.then_inc(split_free, 1)

            for q in range(LEAD):
                turn_u(q, q)
            with pe.Fori(0, NT // 2 - 1) as i:
                score_pair(i * 8, 99)
            score_pair(NT * 4 - 8, 8)

            pe.wait_ge(topk_done, 1)
            for a in range(3):
                for b in range(TB):
                    last = nc.tensor.transpose(ps[:, 2 + a % 2, b * P:(b + 1) * P], pick_n[:, a, b, :], ident) \
                        if a < 2 else nc.tensor.transpose(ps[:, 2, 256 + b * P:256 + (b + 1) * P], pick_n[:, a, b, :], ident)
            last.then_inc(picks_turned, 1)

            def gate_group(n, parity, wait):
                pe.wait_ge(hot1_ready, n + 1)
                pe.wait_ge(hot2_ready, n + 1)
                if wait:
                    pe.wait_ge(gate_used, n - 1)
                for i in range(4):
                    last = nc.tensor.matmul(ps[:, 4 + parity, i * P:(i + 1) * P], key2_hot[:, parity, i, :],
                                            key1_hot[:, parity, i, :], start=True, stop=True)
                last.then_inc(gate_ready, 1)

            for n in range(2):
                gate_group(n, n, False)
            with pe.Fori(1, SEQ // 8) as i:
                for s in range(2):
                    gate_group(i * 2 + s, s, True)

            def value_pair(n0, first, last_pair):
                for q in range(8):
                    t = q // 4
                    if q % 4 == 0:
                        pe.wait_ge(w_lo, (n0 // 4 + t + 1) if isinstance(n0, int) else n0 // 4 + (t + 1))
                    pe.wait_ge(lo_ready, n0 + (Q_V + q + 1))
                    for b in range(TB):
                        c = slice(b * P, (b + 1) * P)
                        last = three(ps[:, b * 4 + q % 4, :], whalf_hi[:, t, c], whalf_lo[:, t, c],
                                     split_hi[:, q % SPLITS, :], split_lo[:, q % SPLITS, :],
                                     first and t == 0, last_pair and t == 1)
                    last.then_inc(split_free, 1)

            pe.wait_ge(gate_used, SEQ // 4)
            value_pair(0, True, False)
            with pe.Fori(1, NT // 2 - 1) as i:
                value_pair(i * 8, False, False)
            value_pair(NT * 4 - 8, False, True)

        @block.scalar
        def _(act):
            chain = Chain(act, a_chain)
            act.sem_inc(acc_free, 2)
            act.sem_inc(score_free, 2)

            def split(n, q):
                if q % 2 == 0:
                    act.wait_ge(raw_ready[q // 2], n * 2 + 16)
                act.wait_ge(split_free, n + (q + 1))
                nc.scalar.activation(split_hi[:, q % SPLITS, :], raw[:, q // 2, q % 2, :], ACT.Copy
                                     ).then_inc(hi_ready, 1)

            def dense_group(g, parity, evacuate):
                for q in range(4, 20):
                    split(g * KT + q // 8 * 8, q % 8)
                evacuate(g, parity)

            def turned_hi(first):
                for f in range(first, first + 8):
                    act.wait_ge(turned, f + 1)
                    fb, k = (f - first) // 4, (f - first) % 4 * 4
                    nc.scalar.activation(act_hi[:, k:k + 4, fb * P:(fb + 1) * P],
                                         ps[:, 4 + f % 4, :].rearrange("p (k t) -> p k t", k=4), ACT.Copy
                                         ).then_inc(turn_hi, 1)

            turned_hi(F_X)
            for q in range(4):
                split(0, q)

            def to_proj(g, parity):
                act.wait_ge(split_free, g * KT + (KT + SPLITS))
                nc.scalar.activation(proj[:, :, bass.ds(g * COLS, COLS)], ps[:, 2 * parity:2 * parity + 2, :],
                                     ACT.Copy).then_inc(acc_free, 1)

            with act.Fori(0, G_IN // 2) as i:
                for s in range(2):
                    dense_group(i * 2 + s, s, to_proj)

            heads = SBH + RTH
            act.wait_ge(acc_free, G_IN + 2)

            def queries_out(it):
                act.wait_ge(qk_turned, it + 1)
                if it >= 2:
                    act.wait_ge(z_ready, it - 1)
                nc.scalar.activation(qk_t[:, it % 2, 0, :], ps[:, it % 2 * 4, 0:256], ACT.Copy,
                                     scale=SCALE if it < SBH else 1.0).then_inc(q_out, 1)

            def softplus_tail(it):
                p = it % 2
                act.wait_ge(z_ready, it + 1)
                if it >= 2:
                    act.wait_ge(la_ready, it - 1)
                z = ps[:, p * 4 + 1, 0:384]
                nc.scalar.activation(z_sb[:, p, :], z, ACT.Copy).then_inc(z_copied, 1)
                if it >= 2:
                    act.wait_ge(spm_ready, it - 1)
                act.wait_ge(z_copied, it + 1)
                chain.step(nc.scalar.activation(soft_l[:, p, :], z_sb[:, p, :], ACT.Abs))
                chain.step(nc.scalar.activation(soft_l[:, p, :], soft_l[:, p, :], ACT.Exp, scale=-1.0))
                nc.scalar.activation(soft_l[:, p, :], soft_l[:, p, :], ACT.Ln, bias=1.0).then_inc(soft_ready, 1)

            def weights(it):
                act.wait_ge(la_ready, it + 1)
                nc.scalar.activation(soft_a[:, it % 2, :], soft_p[:, it % 2, :], ACT.Exp).then_inc(a_ready, 1)

            def result_out(it):
                act.wait_ge(o_ready, it + 1)
                nc.scalar.activation(mixed[:, :, it * HD:(it + 1) * HD],
                                     ps[:, it % 2 * 4 + 3, 0:256].rearrange("p (b d) -> p b d", b=TB), ACT.Copy
                                     ).then_inc(o_out, 1)

            for s in range(heads + 3):
                if s < heads:
                    queries_out(s)
                if 0 <= s - 1 < SBH:
                    softplus_tail(s - 1)
                if 0 <= s - 2 < SBH:
                    weights(s - 2)
                if 0 <= s - 3 < heads:
                    result_out(s - 3)
            gate_cols = slice(INW - RTH * HD, INW)
            nc.scalar.activation(proj[:, :, gate_cols], proj[:, :, gate_cols], ACT.Silu).then_inc(gated, 1)

            turned_hi(F_MIX)
            with act.Fori(0, G_OUT) as i:
                dense_group(i + G_IN, 0, lambda g, parity: None)

            turned_hi(F_X1)

            def to_q(g, parity):
                n = g - G_IN - G_OUT
                act.wait_ge(split_free, g * KT + KT + SPLITS)
                nc.scalar.activation(q_nat[:, :, n * COLS:(n + 1) * COLS], ps[:, 2 * parity:2 * parity + 2, :],
                                     ACT.Copy).then_inc(acc_free, 1)

            for g in range(G_IN + G_OUT, G_IN + G_OUT + G_PQ - 1):
                dense_group(g, g % 2, to_q)
            g = G_IN + G_OUT + G_PQ - 1
            for q in range(4, 16):
                split(g * KT + q // 8 * 8, q % 8)
            to_q(g, g % 2)
            for f in range(8):
                act.wait_ge(sc_ready, f + 1)
                nc.scalar.activation(scores[:, f // 4, f % 4 * 4:f % 4 * 4 + 4, :].rearrange("p s k -> p (s k)"),
                                     ps[:, 2 + f % 2, :], ACT.Copy).then_inc(sc_out, 1)

            def split_u(n, q):
                act.wait_ge(u_turned, n + (q + 1))
                act.wait_ge(split_free, n + (Q_U + q + 1))
                nc.scalar.activation(split_hi[:, q % SPLITS, :], ps[:, 4 + q % 4, :], ACT.Copy).then_inc(hi_ready, 1)

            def gelu(n, t):
                act.wait_ge(split_free, n + (Q_U + SPLITS + 4 * t + 4))
                nc.scalar.activation(wexp[:, bass.ds(n // 4 + t, 1), :].rearrange("p a t -> p (a t)"),
                                     ps[:, t, 0:SEQ], ACT.Gelu).then_inc(score_free, 1)

            act.wait_ge(x1_out, 16)
            for q in range(4):
                split_u(0, q)

            def u_pair(n):
                for q in range(4, 8):
                    split_u(n, q)
                gelu(n, 0)
                for q in range(8, 12):
                    split_u(n, q)
                gelu(n, 1)

            with act.Fori(0, 20) as i:
                u_pair(i * 8)
            act.wait_ge(best_ready, 1)
            nc.scalar.activation(best[:, :, :], best[:, :, :], ACT.Exp).then_inc(exp_ready, 1)
            with act.Fori(20, 46) as i:
                u_pair(i * 8)
            act.wait_ge(topk_done, 1)
            with act.Fori(46, NT // 2 - 1) as i:
                u_pair(i * 8)
            n = NT * 4 - 8
            for q in range(4, 8):
                split_u(n, q)
            gelu(n, 0)
            gelu(n, 1)

            def split_w(n, t, static=False):
                act.wait_ge(split_free, n + (Q_V + SPLITS + 4 * t - 4) if static or t > 0 else n + (Q_V + SPLITS - 4))
                nc.scalar.activation(whalf_hi[:, t % 2, :],
                                     wexp[:, bass.ds(n // 4 + t, 1), :].rearrange("p a t -> p (a t)"), ACT.Copy
                                     ).then_inc(w_hi, 1)

            for q in range(4):
                split(Q_V, q)

            def hot1(n, parity):
                act.wait_ge(dist_ready, n + 1)
                d = key1_hot[:, parity, :, :]
                nc.scalar.activation(d, d, ACT.Abs).then_inc(abs_ready, 1)
                act.wait_ge(abs_ready, n + 1)
                nc.scalar.activation(d, d, ACT.Relu, scale=-1.0, bias=1.0).then_inc(hot1_ready, 1)

            with act.Fori(0, SEQ // 8) as i:
                for s in range(2):
                    hot1(i * 2 + s, s)
            act.wait_ge(gate_used, SEQ // 4)
            split_w(0, 0)

            with act.Fori(0, NT // 2 - 1) as i:
                split_w(i * 8, 1)
                for q in range(4, 8):
                    split(i * 8 + Q_V, q)
                split_w(i * 8, 2)
                for q in range(4):
                    split(i * 8 + (Q_V + 8), q)
            n = NT * 4 - 8
            split_w(n, 1)
            for q in range(4, 8):
                split(n + Q_V, q)

        @block.vector
        def _(dve):
            chain = Chain(dve, v_chain)
            vec = nc.vector

            def split(n, q):
                dve.wait_ge(hi_ready, n + (q + 1))
                vec.tensor_tensor(split_lo[:, q % SPLITS, :], raw[:, q // 2, q % 2, :],
                                  split_hi[:, q % SPLITS, :].bitcast(f32), ALU.subtract).then_inc(lo_ready, 1)

            def dense_group(g):
                for q in range(4, 20):
                    split(g * KT + q // 8 * 8, q % 8)

            def turned_lo(first, order):
                for f in range(first, first + 8):
                    dve.wait_ge(turn_hi, order * 8 + f - first + 1)
                    fb, k = (f - first) // 4, (f - first) % 4 * 4
                    vec.tensor_tensor(act_lo[:, k:k + 4, fb * P:(fb + 1) * P],
                                      ps[:, 4 + f % 4, :].rearrange("p (k t) -> p k t", k=4),
                                      act_hi[:, k:k + 4, fb * P:(fb + 1) * P].bitcast(f32), ALU.subtract
                                      ).then_inc(turn_done, 1)

            turned_lo(F_X, 0)
            for q in range(4):
                split(0, q)
            with dve.Fori(0, G_IN) as i:
                dense_group(i)

            dve.wait_ge(tab_in, 16)
            dve.wait_ge(acc_free, G_IN + 2)

            def rotary(eng, own, first_col, tmp, b):
                xs = proj[:, b, first_col:first_col + RTH * HD].rearrange("p (h d) -> p h d", h=RTH)
                half = HD // 2
                eng.tensor_tensor(tmp[:, 1, :, 0:half], xs[:, :, half:HD],
                                  sin_t[:, b:b + 1, 0:half].to_broadcast([P, RTH, half]), ALU.mult)
                eng.tensor_tensor(tmp[:, 1, :, half:HD], xs[:, :, 0:half],
                                  sin_t[:, b:b + 1, half:HD].to_broadcast([P, RTH, half]), ALU.mult)
                own.step(eng.tensor_tensor(tmp[:, 0, :, :], xs, cos_t[:, b:b + 1, :].to_broadcast([P, RTH, HD]),
                                           ALU.mult))
                ins = eng.tensor_tensor(xs, tmp[:, 0, :, :], tmp[:, 1, :, :], ALU.add)
                own.step(ins)

            heads = SBH + RTH

            def keys_out(it):
                dve.wait_ge(q_out, it + 1)
                if it >= 2:
                    dve.wait_ge(z_ready, it - 1)
                vec.tensor_copy(qk_t[:, it % 2, 1, :], ps[:, it % 2 * 4, 256:512]).then_inc(k_out, 1)

            def softplus(it):
                p = it % 2
                dve.wait_ge(soft_ready, it + 1)
                if it >= 2:
                    dve.wait_ge(a_ready, it - 1)
                chain.step(vec.scalar_tensor_tensor(out=soft_p[:, p, :], in0=z_sb[:, p, :], scalar=0.0,
                                                    in1=soft_l[:, p, :], op0=ALU.max, op1=ALU.add))
                vec.tensor_tensor(soft_p[:, p, :], soft_p[:, p, :], causal, ALU.mult).then_inc(spm_ready, 1)

            def log_weights(it):
                p = it % 2
                dve.wait_ge(c_ready, it + 1)
                if it >= 2:
                    dve.wait_ge(o_ready, it - 1)
                vec.tensor_tensor(soft_p[:, p, :], z_sb[:, p, :], ps[:, p * 4 + 2, 0:384], ALU.subtract
                                  ).then_inc(la_ready, 1)

            def decayed(it):
                p = it % 2
                dve.wait_ge(z_ready, it + 1)
                dve.wait_ge(o_ready, it - 1)
                vec.tensor_tensor(soft_a[:, p, :], ps[:, p * 4 + 1, 0:384], decay[:, it - SBH, :], ALU.mult
                                  ).then_inc(a_ready, 1)

            for s in range(heads + 3):
                if s < heads:
                    keys_out(s)
                if 0 <= s - 1 < SBH:
                    softplus(s - 1)
                if 0 <= s - 2 < SBH:
                    log_weights(s - 2)
                elif SBH <= s - 2 < heads:
                    decayed(s - 2)
                if s in (2, 3):
                    rotary(vec, chain, 3 * SBH * HD, rot_v, s - 2)
                    if s == 3:
                        vec.engine_nop().then_inc(rot_q, 1)

            dve.wait_ge(o_out, heads)
            dve.wait_ge(norms_in, 32)
            dve.wait_ge(halfexp, 1)
            m4 = mixed[:, :, :].rearrange("p b (h d) -> p b h d", h=heads)
            s4 = square[:, :, :].rearrange("p b (h d) -> p b h d", h=heads)
            sums = stats[:, SUMS:SUMS + 32].rearrange("p (b h) -> p b h", b=TB)
            for b in range(TB):
                chain.step(vec.tensor_reduce(sums[:, b, SBH:], m4[:, b, SBH:, :], AX.X, ALU.add))
                chain.step(vec.tensor_scalar(sums[:, b, SBH:], sums[:, b, SBH:], 1.0 / HD, None, ALU.mult))
                chain.step(vec.tensor_tensor(m4[:, b, SBH:, :], m4[:, b, SBH:, :],
                                             sums[:, b, SBH:].unsqueeze(2).to_broadcast([P, RTH, HD]), ALU.subtract))
                chain.step(vec.tensor_tensor(square[:, b, :], mixed[:, b, :], mixed[:, b, :], ALU.mult))
                chain.step(vec.tensor_reduce(stats[:, VAR + 16 * b:VAR + 16 * b + 16], s4[:, b, :, :], AX.X, ALU.add))
                vec.tensor_scalar(stats[:, VAR + 16 * b:VAR + 16 * b + 16], stats[:, VAR + 16 * b:VAR + 16 * b + 16],
                                  1.0 / HD, NORM_EPS, ALU.mult, ALU.add).then_inc(var_ready, 1)
            dve.wait_ge(gated, 1)
            ret = slice(SBH * HD, D)
            for b in range(TB):
                dve.wait_ge(rstd_ready, b + 1)
                chain.step(vec.tensor_tensor(m4[:, b, :, :], m4[:, b, :, :],
                                             stats[:, RSTD + 16 * b:RSTD + 16 * b + 16].unsqueeze(2)
                                             .to_broadcast([P, heads, HD]), ALU.mult))
                chain.step(vec.tensor_tensor(mixed[:, b, :], mixed[:, b, :], norm_w[:, :], ALU.mult))
                vec.tensor_tensor(mixed[:, b, ret], mixed[:, b, ret], proj[:, b, INW - RTH * HD:INW], ALU.mult
                                  ).then_inc(mixed_ready, 1)

            turned_lo(F_MIX, 1)
            with dve.Fori(0, G_OUT // 2) as i:
                for s in range(2):
                    dense_group(i * 2 + (G_IN + s))
                    dve.wait_ge(split_free, (i * 2 + (G_IN + s)) * KT + (KT + SPLITS))
                    part = x_nat[:, :, bass.ds((i * 2 + s) * COLS, COLS)]
                    vec.scalar_tensor_tensor(out=part, in0=part, scalar=ALPHA, in1=ps[:, 2 * s:2 * s + 2, :],
                                             op0=ALU.mult, op1=ALU.add).then_inc(acc_free, 1)

            def layer_norm(buf, w, b_, blk, n_var):
                st = stats[:, 160:184].rearrange("p (c s) -> p c s", c=4)
                for c in range(4):
                    chain.step(vec.bn_stats(st[:, c, :], buf[:, blk, c * COLS:(c + 1) * COLS]))
                chain.step(vec.bn_aggr(stats[:, MEAN:MEAN + 2], stats[:, 160:184]))
                vec.tensor_scalar(stats[:, VAR:VAR + 1], stats[:, MEAN + 1:MEAN + 2], LN_EPS, None, ALU.add
                                  ).then_inc(var_ready, 1)
                dve.wait_ge(rstd_ready, n_var)
                row = buf[:, blk, :]
                chain.step(vec.tensor_scalar(row, row, stats[:, MEAN:MEAN + 1], stats[:, RSTD:RSTD + 1],
                                             ALU.subtract, ALU.mult))
                chain.step(vec.tensor_tensor(row, row, w[:, :], ALU.mult))
                return vec.tensor_tensor(row, row, b_[:, :], ALU.add)

            dve.wait_ge(acc_free, G_IN + G_OUT + 2)
            dve.wait_ge(ln1_in, 32)
            for b in range(TB):
                layer_norm(x_nat, ln_w, ln_b, b, TB + b + 1).then_inc(x1_ready, 1)

            for f in range(4):
                dve.wait_ge(turned, F_KEYS + f + 1)
                vec.tensor_copy(keys_t[:, 4 * f:4 * f + 4, :].rearrange("p s k -> p (s k)"),
                                ps[:, 4 + (F_KEYS + f) % 4, :]).then_inc(turn_done, 1)
            turned_lo(F_X1, 2)
            with dve.Fori(0, G_PQ - 1) as i:
                dense_group(i + (G_IN + G_OUT))
            g = G_IN + G_OUT + G_PQ - 1
            for q in range(4, 16):
                split(g * KT + q // 8 * 8, q % 8)
            for f in range(8):
                dve.wait_ge(turned, F_Q + f + 1)
                vec.tensor_copy(q_t[:, f % 4 * 4:f % 4 * 4 + 4, f // 4 * P:(f // 4 + 1) * P],
                                ps[:, 4 + f % 4, :].rearrange("p (k t) -> p k t", k=4)).then_inc(turn_done, 1)

            def split_u(n, q):
                dve.wait_ge(hi_ready, n + (Q_U + q + 1))
                vec.tensor_tensor(split_lo[:, q % SPLITS, :], ps[:, 4 + q % 4, :],
                                  split_hi[:, q % SPLITS, :].bitcast(f32), ALU.subtract).then_inc(lo_ready, 1)

            class LoopChain:

                def __init__(self, i, first, steps):
                    self.i, self.first, self.steps, self.n = i, first, steps, 0

                def step(self, instruction):
                    self.n += 1
                    instruction.then_inc(v_chain, 1)
                    dve.wait_ge(v_chain, self.i * self.steps + (self.first + self.n))
                    dve.sem_inc(carried, 1)

            def flat(ap, pattern="p a b -> p (a b)"):
                return ap.rearrange(pattern)

            def top16(lc, values_in, scratch, out_v, out_i):
                lc.step(vec.max(out_v[:, 0:8], values_in))
                lc.step(vec.max_index(out_i[:, 0:8], out_v[:, 0:8], values_in))
                lc.step(vec.match_replace(scratch, out_v[:, 0:8], values_in, LOWEST))
                lc.step(vec.max(out_v[:, 8:16], scratch))
                lc.step(vec.max_index(out_i[:, 8:16], out_v[:, 8:16], scratch))

            sc3 = flat(scores[:, :, :, :], "p b s k -> p (b s) k")
            TOP_STEPS = 18
            dve.wait_ge(sc_out, 8)
            c0 = chain.n
            for q in range(4):
                split_u(0, q)
            with dve.Fori(0, TB * PH) as i:
                lc = LoopChain(i, c0, TOP_STEPS)
                for q in range(4, 8):
                    split_u(i * 8, q)
                lc.step(vec.tensor_copy(head_s[:, :, :], sc3[:, bass.ds(i * 2, 2), :]))
                for c in range(2):
                    top16(lc, head_s[:, c, :], rest[:, 0:PKEYS], top_v[:, c, :], head_i[:, c, :])
                for q in range(8, 12):
                    split_u(i * 8, q)
                lc.step(vec.tensor_tensor(cand[:, :, :], top_v[:, 0, :].unsqueeze(2).to_broadcast([P, TOPK, TOPK]),
                                          top_v[:, 1, :].unsqueeze(1).to_broadcast([P, TOPK, TOPK]), ALU.add))
                top16(lc, flat(cand[:, :, :]), rest[:, :], head_b, head_p)
                vec.tensor_copy(idx_u[:, bass.ds(i, 1), :, :].rearrange("p a c k -> p (a c) k"), head_i[:, :, :])
                vec.tensor_copy(best[:, bass.ds(i, 1), :].rearrange("p a k -> p (a k)"), head_b[:, :])
                lc.step(vec.tensor_copy(pos_u[:, bass.ds(i, 1), :].rearrange("p a k -> p (a k)"), head_p[:, :]))
                assert lc.n == TOP_STEPS
            chain.n += TB * PH * TOP_STEPS

            def u_pair(n, between):
                for q in range(4, 8):
                    split_u(n, q)
                for q in range(8, 12):
                    split_u(n, q)
                between()

            def softmax_start():
                chain.step(vec.tensor_copy(gsum[:, 0, :], best[:, :, 0]))
                vec.tensor_tensor(best[:, :, :], best[:, :, :], gsum[:, 0, :].unsqueeze(2)
                                  .to_broadcast([P, TB * PH, TOPK]), ALU.subtract).then_inc(best_ready, 1)
                chain.step(vec.tensor_scalar(pos_i[:, 0, :, :], pos_u[:, :, :], 4, None, ALU.logical_shift_right))
                chain.step(vec.tensor_scalar(pos_i[:, 1, :, :], pos_u[:, :, :], TOPK - 1, None, ALU.bitwise_and))
                chain.step(vec.tensor_copy(flat(pos_f[:, :, :, :], "p a b c -> p (a b c)"),
                                           flat(pos_i[:, :, :, :], "p a b c -> p (a b c)")))
                chain.step(vec.tensor_copy(flat(idx_f[:, :, :, :], "p a b c -> p (a b c)"),
                                           flat(idx_u[:, :, :, :], "p a b c -> p (a b c)")))

            u_pair(TB * PH * 8, softmax_start)

            PAIRS_DONE = TB * PH + 1
            DEC_STEPS = 6
            c1 = chain.n
            with dve.Fori(0, TB * PH // 2) as i:
                lc = LoopChain(i, c1, DEC_STEPS)
                for q in range(4, 8):
                    split_u(i * 8 + PAIRS_DONE * 8, q)
                for h in range(2):
                    if h == 1:
                        for q in range(8, 12):
                            split_u(i * 8 + PAIRS_DONE * 8, q)
                    for k in range(2) if h == 0 else ():
                        pass
                    row = pos_f[:, h, bass.ds(i * 2, 2), :].rearrange("p a k -> p (a k)")
                    lc.step(vec.tensor_tensor(onehot[:, :, :], row.unsqueeze(2).to_broadcast([P, 2 * TOPK, TOPK]),
                                              iota[:, 0:TOPK].unsqueeze(1).to_broadcast([P, 2 * TOPK, TOPK]),
                                              ALU.is_equal))
                    o4 = onehot[:, :, :].rearrange("p (a k) j -> p a k j", a=2)
                    lc.step(vec.tensor_tensor(o4, o4, idx_f[:, bass.ds(i * 2, 2), h, :].unsqueeze(2)
                                              .to_broadcast([P, 2, TOPK, TOPK]), ALU.mult))
                    dst = pick_n[:, h, :, :].rearrange("p b k -> p (b k)")
                    lc.step(vec.tensor_reduce(dst[:, bass.ds(i * 2 * TOPK, 2 * TOPK)], onehot[:, :, :], AX.X, ALU.add))
                assert lc.n == DEC_STEPS
            chain.n += TB * PH // 2 * DEC_STEPS

            def softmax_end():
                dve.wait_ge(exp_ready, 1)
                chain.step(vec.tensor_reduce(gsum[:, 0, :], best[:, :, :], AX.X, ALU.add))
                chain.step(vec.reciprocal(gsum[:, 1, :], gsum[:, 0, :]))
                vec.tensor_tensor(pick_n[:, 2, :, :].rearrange("p b (h k) -> p (b h) k", k=TOPK), best[:, :, :],
                                  gsum[:, 1, :].unsqueeze(2).to_broadcast([P, TB * PH, TOPK]), ALU.mult
                                  ).then_inc(topk_done, 1)

            done = PAIRS_DONE + TB * PH // 2
            u_pair(done * 8, softmax_end)
            with dve.Fori(done + 1, NT // 2 - 1) as i:
                u_pair(i * 8, lambda: None)
            for q in range(4, 8):
                split_u(NT * 4 - 8, q)

            dve.wait_ge(picks_turned, 1)
            chain.step(vec.tensor_copy(picks_t[:, 0, :], ps[:, 2, 0:256]))
            chain.step(vec.tensor_copy(picks_t[:, 1, :], ps[:, 3, 0:256]))
            vec.tensor_copy(picks_t[:, 2, :], ps[:, 2, 256:512]).then_inc(picks_ready, 1)
            dve.wait_ge(picks_ready, 1)
            dve.wait_ge(score_free, NT + 2)

            def hot2(n, parity, wait):
                if wait:
                    dve.wait_ge(gate_ready, n - 1)
                for i in range(4):
                    last = vec.tensor_scalar(key2_hot[:, parity, i, :], iota,
                                             picks_t[:, 1, bass.ds(n * 4 + i, 1)], picks_t[:, 2, bass.ds(n * 4 + i, 1)],
                                             ALU.is_equal, ALU.mult)
                last.then_inc(hot2_ready, 1)

            def apply_gates(n, parity):
                dve.wait_ge(gate_ready, n + 1)
                part = wexp[:, :, bass.ds(n * 4, 4)]
                vec.tensor_tensor(part, part, ps[:, 4 + parity, :].rearrange("p (t j) -> p j t", t=4), ALU.mult
                                  ).then_inc(gate_used, 1)

            for q in range(4):
                split(Q_V, q)
            hot2(0, 0, False)
            hot2(1, 1, False)
            with dve.Fori(0, SEQ // 8 - 1) as i:
                for s in range(2):
                    apply_gates(i * 2 + s, s)
                    hot2(i * 2 + (2 + s), s, True)
            apply_gates(SEQ // 4 - 2, 0)
            apply_gates(SEQ // 4 - 1, 1)

            def split_w(n, t):
                dve.wait_ge(w_hi, (n // 4 + t + 1) if isinstance(n, int) else n // 4 + (t + 1))
                vec.tensor_tensor(whalf_lo[:, t % 2, :], wexp[:, bass.ds(n // 4 + t, 1), :].rearrange("p a t -> p (a t)"),
                                  whalf_hi[:, t % 2, :].bitcast(f32), ALU.subtract).then_inc(w_lo, 1)

            dve.wait_ge(gate_used, SEQ // 4)
            split_w(0, 0)
            with dve.Fori(0, NT // 2 - 1) as i:
                split_w(i * 8, 1)
                for q in range(4, 8):
                    split(i * 8 + Q_V, q)
                split_w(i * 8, 2)
                for q in range(4):
                    split(i * 8 + (Q_V + 8), q)
            n = NT * 4 - 8
            split_w(n, 1)
            for q in range(4, 8):
                split(n + Q_V, q)

            dve.wait_ge(split_free, Q_V + NT * 4 + SPLITS)
            dve.wait_ge(x1_in, 16)
            dve.wait_ge(ln2_in, 32)
            for b in range(TB):
                chain.step(vec.scalar_tensor_tensor(out=y_out[:, b, :], in0=x1_back[:, b, :], scalar=ALPHA,
                                                    in1=ps[:, 4 * b:4 * b + 4, :].rearrange("p n c -> p (n c)"),
                                                    op0=ALU.mult, op1=ALU.add))
                layer_norm(y_out, ln2w, ln2b, b, 2 * TB + b + 1).then_inc(y_ready, 1)

        @block.gpsimd
        def _(pool):
            chain = Chain(pool, g_chain)
            eng = nc.gpsimd
            eng.memset(stats[:, NHALF:NHALF + 32], -0.5).then_inc(halfexp, 1)

            pool.wait_ge(tab_in, 16)
            pool.wait_ge(acc_free, G_IN + 2)
            for b in range(TB):
                first_col = (3 * SBH + RTH) * HD
                xs = proj[:, b, first_col:first_col + RTH * HD].rearrange("p (h d) -> p h d", h=RTH)
                half = HD // 2
                eng.tensor_tensor(rot_g[:, 1, :, 0:half], xs[:, :, half:HD],
                                  sin_t[:, b:b + 1, 0:half].to_broadcast([P, RTH, half]), ALU.mult)
                eng.tensor_tensor(rot_g[:, 1, :, half:HD], xs[:, :, 0:half],
                                  sin_t[:, b:b + 1, half:HD].to_broadcast([P, RTH, half]), ALU.mult)
                chain.step(eng.tensor_tensor(rot_g[:, 0, :, :], xs, cos_t[:, b:b + 1, :].to_broadcast([P, RTH, HD]),
                                             ALU.mult))
                last = eng.tensor_tensor(xs, rot_g[:, 0, :, :], rot_g[:, 1, :, :], ALU.add)
                if b == 0:
                    chain.step(last)
                else:
                    last.then_inc(rot_k, 1)

            pool.wait_ge(halfexp, 1)
            for n in range(3 * TB):
                pool.wait_ge(var_ready, n + 1)
                o, w = (16 * n, 16) if n < TB else (0, 1)
                eng.tensor_tensor(stats[:, RSTD + o:RSTD + o + w], stats[:, VAR + o:VAR + o + w],
                                  stats[:, NHALF:NHALF + w], ALU.pow).then_inc(rstd_ready, 1)
                if n == 2 * TB - 1:
                    pool.wait_ge(picks_ready, 1)
                    pool.wait_ge(score_free, NT + 2)

                    def dist1(n, parity, wait):
                        if wait:
                            pool.wait_ge(gate_ready, n - 1)
                        eng.tensor_tensor(key1_hot[:, parity, :, :],
                                          iota.unsqueeze(1).to_broadcast([P, 4, P]),
                                          picks_t[:, 0, bass.ds(n * 4, 4)].unsqueeze(2).to_broadcast([P, 4, P]),
                                          ALU.subtract).then_inc(dist_ready, 1)

                    dist1(0, 0, False)
                    dist1(1, 1, False)
                    with pool.Fori(1, SEQ // 8) as i:
                        for s in range(2):
                            dist1(i * 2 + s, s, True)


def constant_tables():
    inv = 10000.0 ** (-np.arange(0, HD, 2, dtype=np.float32) / HD)
    ang = np.arange(SEQ, dtype=np.float32)[:, None] * inv.astype(np.float32)[None, :]
    ang = np.concatenate([ang, ang], -1).astype(np.float32)
    cos, sin = np.cos(ang), np.sin(ang)
    sin[:, :HD // 2] *= -1
    by_block = lambda a: a.reshape(TB, P, HD).transpose(1, 0, 2).reshape(P, TB * HD)
    log_g = np.log1p(-(2.0 ** (-5.0 - np.arange(RTH, dtype=np.float64))))
    j, i = np.arange(P)[:, None], np.arange(SEQ)[None, :]
    seen = (i // CHUNK) >= (j // CHUNK)
    dist = np.abs(i - j)
    decay = np.where(seen[None], np.exp(log_g[:, None, None] * dist[None]), 0.0) * SCALE
    decay = np.concatenate([decay, decay[:, :, :P]], -1).transpose(1, 0, 2).reshape(P, RTH * 384)
    r, c = np.arange(P)[:, None], np.arange(P)[None, :]
    causal = np.concatenate([j < i, r < c], -1)
    cst = np.concatenate([by_block(cos), by_block(sin), decay, (r >= c), np.ones((P, P)), causal,
                          np.where(causal, 0.0, BIG)], -1).astype(np.float32)
    small = np.stack([np.eye(P), np.broadcast_to(np.arange(P), (P, P))], 1).astype(np.float32)
    return np.ascontiguousarray(cst), np.ascontiguousarray(small)


_INS = ["x", "w_in", "sb_norm_w", "ret_norm_w", "w_out", "ln1_w", "ln1_b", "w_pq", "sub_keys",
        "expert_u", "expert_v", "ln2_w", "ln2_b"]


def kernel(**inputs):
    import concourse.bacc as _bacc
    from concourse.bass_utils import run_bass_kernel_spmd as _run

    nc = _bacc.Bacc("TRN2", target_bir_lowering=False, num_devices=1)
    cst, small = constant_tables()
    arrays, args = {}, []
    named = [(n, np.ascontiguousarray(inputs[n])) for n in _INS] + [("tables", cst), ("small_tables", small)]
    for name, a in named:
        arrays[f"in_{name}"] = a
        args.append(nc.dram_tensor(f"in_{name}", a.shape, mybir.dt.from_np(a.dtype), kind="ExternalInput").ap())
    args.append(nc.dram_tensor("out_y", (1, SEQ, D), mybir.dt.float32, kind="ExternalOutput").ap())
    layer_kernel(nc, *args)
    r = _run(nc, [arrays], core_ids=[0])
    return r.results[0]["out_y"]
```

```python
from contextlib import ExitStack

import numpy as np

import concourse.bass as bass
from concourse import mybir

P = 128
SEQ, D = 256, 2048
TB = SEQ // P
KT = D // P
HD = 128
SBH, RTH = 8, 8
INW = 3 * SBH * HD + 4 * RTH * HD
CHUNK = 64
PH, PKEYS, TOPK = 8, 128, 16
SETS = 2 * PH
EXPERTS = PKEYS * PKEYS
NT = EXPERTS // P
COLS = 512
ALPHA = 2.0 ** 0.25
LN_EPS, NORM_EPS = 1e-5, 1e-6
SCALE = HD ** -0.5
BIG = 1e30
LOWEST = -3.4e38

G_IN, G_OUT, G_PQ = INW // COLS, D // COLS, D // COLS
Q_OUT = G_IN * KT
Q_PQ = Q_OUT + G_OUT * KT
Q_U = Q_PQ + G_PQ * KT
Q_V = Q_U + NT * 4
RAWS, SPLITS = 4, 4
PAIRS = NT // 2
PAIRS_A = 26
DVE_A, DVE_B = (3,), (0, 1, 2, 3)
SOFT = TB * PH
PICKS = PAIRS_A
GATE0 = PICKS + 2
GATES = SEQ // 4
LATE = 2 * PAIRS_A - 1
ROWS = 4
DMA1, DMA4 = 16, 16 * ROWS
F_X, F_MIX, F_KEYS, F_X1, F_Q = 0, 8, 16, 20, 28


def layer_kernel(nc, x, w_in, sb_norm_w, ret_norm_w, w_out, ln1_w, ln1_b, w_pq, sub_keys,
                 expert_u, expert_v, ln2_w, ln2_b, tables, small_tables, out):
    f32, f32r, u32 = mybir.dt.float32, mybir.dt.float32r, mybir.dt.uint32
    ACT, ALU, AX = mybir.ActivationFunctionType, mybir.AluOpType, mybir.AxisListType
    ctx = ExitStack()
    with ctx:
        base = 16512

        def at(name, shape, dt, offset):
            return nc.alloc_sbuf_tensor_at(name, [P, *shape], dt, offset=offset)

        A_HI, A_LO = base, base + 16384
        RAW, SPL = base + 32768, base + 49152
        KEEP = base + 65536
        W0 = 98272
        act_hi = at("act_hi", [KT, SEQ], f32r, A_HI)
        act_lo = at("act_lo", [KT, SEQ], f32r, A_LO)
        raw = at("raw", [RAWS, 2, COLS], f32, RAW)
        split_hi = at("split_hi", [SPLITS, COLS], f32r, SPL)
        split_lo = at("split_lo", [SPLITS, COLS], f32r, SPL + 8192)
        small = at("small", [2, P], f32, KEEP)
        picks_t = at("picks_t", [3, SEQ], f32, KEEP + 1024)
        stats = at("stats", [256], f32, KEEP + 4096)
        soft_a = at("soft_a", [2, 384], f32, KEEP + 5120)
        pick_n = at("pick_n", [3, TB, P], f32, KEEP + 5120)
        hot = at("hot", [2, 2, 4, P], f32, KEEP + 5120)
        late = at("late", [2, SEQ], f32, KEEP + 13312)
        whalf_hi = at("whalf_hi", [2, SEQ], f32r, KEEP + 5120)
        whalf_lo = at("whalf_lo", [2, SEQ], f32r, KEEP + 7168)
        wexp = at("wexp", [NT, SEQ], f32, W0)
        proj = at("proj", [TB, INW], f32, W0)
        x_nat = at("x_nat", [TB, D], f32, W0 + 57344)
        mixed = at("mixed", [TB, D], f32, W0 + 73728)
        cst = at("cst", [4608], f32, W0 + 90112)
        norm_w = at("norm_w", [D], f32, W0 + 108544)
        qk_t = at("qk_t", [2, 2, SEQ], f32, W0 + 116736)
        z_sb = at("z_sb", [2, 384], f32, W0 + 120832)
        soft_l = at("soft_l", [2, 384], f32, W0 + 123904)
        soft_p = at("soft_p", [2, 384], f32, W0 + 126976)
        ln_w = at("ln_w", [D], f32, W0)
        ln_b = at("ln_b", [D], f32, W0 + 8192)
        q_nat = at("q_nat", [TB, D], f32, W0 + 16384)
        q_t = at("q_t", [KT, SEQ], f32, W0 + 32768)
        keys_t = at("keys_t", [SETS, PKEYS], f32, W0 + 49152)
        keys_nat = at("keys_nat", [SETS, HD], f32, W0 + 90112)
        scores = at("scores", [TB, SETS, PKEYS], f32, W0 + 98304)
        T0 = W0 + 114688
        idx_u = at("idx_u", [TB * PH, 2, TOPK], u32, T0)
        idx_f = at("idx_f", [TB * PH, 2, TOPK], f32, T0 + 2048)
        best = at("best", [TB * PH, TOPK], f32, T0 + 4096)
        pos_u = at("pos_u", [TB * PH, TOPK], u32, T0 + 5120)
        pos_f = at("pos_f", [2, TB * PH, TOPK], f32, T0 + 6144)
        pos_i = at("pos_i", [2, TB * PH, TOPK], u32, T0 + 8192)
        cand = at("cand", [TOPK, TOPK], f32, T0 + 10240)
        top_v = at("top_v", [2, TOPK], f32, T0 + 11264)
        rest = at("rest", [256], f32, T0 + 11392)
        onehot = at("onehot", [2 * TOPK, TOPK], f32, T0 + 12416)
        gsum = at("gsum", [2, TB * PH], f32, T0 + 14464)
        head_s = at("head_s", [2, PKEYS], f32, T0 + 14592)
        head_i = at("head_i", [2, TOPK], u32, T0 + 15616)
        head_b = at("head_b", [TOPK], f32, T0 + 15744)
        head_p = at("head_p", [TOPK], u32, T0 + 15808)
        rot_v = at("rot_v", [2, RTH, HD], f32, A_HI)
        rot_g = at("rot_g", [2, RTH, HD], f32, A_HI + 8192)
        square = at("square", [TB, D], f32, A_LO)
        ln2w = at("ln2w", [D], f32, A_HI)
        ln2b = at("ln2b", [D], f32, A_HI + 8192)
        x1_back = at("x1_back", [TB, D], f32, A_LO)
        y_out = at("y_out", [TB, D], f32, W0)

        ps = ctx.enter_context(nc.psum_tensor("ps", [P, 8, COLS], f32))
        x1_dram = nc.dram_tensor("x1_dram", (P, TB, D), f32, kind="Internal").ap()

        ident, iota = small[:, 0, :], small[:, 1, :]
        cos_t = cst[:, 0:256].rearrange("p (b d) -> p b d", b=TB)
        sin_t = cst[:, 256:512].rearrange("p (b d) -> p b d", b=TB)
        decay = cst[:, 512:3584].rearrange("p (h q) -> p h q", h=RTH)
        tri = cst[:, 3584:3712]
        ones = cst[:, 3712:3840]
        causal = cst[:, 3840:4224]
        masked = cst[:, 4224:4608]

        def sem(name):
            return ctx.enter_context(nc.semaphore(name))

        raw_ready = [sem(f"raw_ready{i}") for i in range(RAWS)]
        hi_ready = sem("hi_ready")
        lo_ready = sem("lo_ready")
        split_free = sem("split_free")
        acc_free = sem("acc_free")
        turned = sem("turned")
        turn_hi = sem("turn_hi")
        turn_done = sem("turn_done")
        pe_turned = sem("pe_turned")
        dve_turned = sem("dve_turned")
        score_free = sem("score_free")
        x_in, tab_in, keys_in, ln1_in, ln2_in = (sem(n) for n in ("x_in", "tab_in", "keys_in", "ln1_in", "ln2_in"))
        norms_in, x1_out, x1_in, y_stored = (sem(n) for n in ("norms_in", "x1_out", "x1_in", "y_stored"))
        rot_q, rot_k = sem("rot_q"), sem("rot_k")
        qk_turned, q_out, k_out = sem("qk_turned"), sem("q_out"), sem("k_out")
        z_ready, c_ready, o_ready, o_out = sem("z_ready"), sem("c_ready"), sem("o_ready"), sem("o_out")
        z_copied, soft_ready, spm_ready, la_ready, a_ready = (
            sem(n) for n in ("z_copied", "soft_ready", "spm_ready", "la_ready", "a_ready"))
        gated = sem("gated")
        mixed_ready, x1_ready = sem("mixed_ready"), sem("x1_ready")
        var_ready, rstd_ready = sem("var_ready"), sem("rstd_ready")
        sc_ready, sc_out = sem("sc_ready"), sem("sc_out")
        best_ready, exp_ready, topk_done = sem("best_ready"), sem("exp_ready"), sem("topk_done")
        picks_turned, picks_ready = sem("picks_turned"), sem("picks_ready")
        dist_ready, hot_ready, weighted, gate_ready, gates_free = (
            sem(n) for n in ("dist_ready", "hot_ready", "weighted", "gate_ready", "gates_free"))
        ones_ready, late_used = sem("ones_ready"), sem("late_used")
        abs_ready, carried = sem("abs_ready"), sem("carried")
        w_hi, w_lo = sem("w_hi"), sem("w_lo")
        halfexp = sem("halfexp")
        y_ready = sem("y_ready")
        v_chain, a_chain, g_chain = sem("v_chain"), sem("a_chain"), sem("g_chain")

        MEAN, VAR, RSTD, NHALF, SUMS = 0, 16, 48, 80, 112

        class Chain:

            def __init__(self, eng, s):
                self.eng, self.sem, self.n = eng, s, 0

            def step(self, instruction):
                self.n += 1
                instruction.then_inc(self.sem, 1)
                self.eng.wait_ge(self.sem, self.n)

            def add(self, instruction):
                self.n += 1
                instruction.then_inc(self.sem, 1)

        w_in_v = w_in.rearrange("l (k p) n -> (l p) k n", p=P)
        w_out_v = w_out.rearrange("l (k p) n -> (l p) k n", p=P)
        w_pq_v = w_pq.rearrange("l (h m c) n -> (l h) m c n", h=2, c=8)
        u_pe = expert_u.rearrange("l e d -> (l e) d")
        u_dve = expert_u.rearrange("l (g i) (h r d) -> (l h) r i g d", i=32, h=2, r=ROWS)
        v_v = expert_v.rearrange("l e d -> (l e) d")
        def before(pair, a, b, part_a):
            return pair * a if part_a else pair * b + PAIRS_A * (a - b)

        def u_raw(slot, pair, part_a):
            a, b = (DMA4 if slot in s else DMA1 for s in (DVE_A, DVE_B))
            return before(pair, a, b, part_a) + (U_RAW + (a if part_a else b))

        def turned_at(half, pair, part_a):
            own = DVE_A if part_a else DVE_B
            if half in own:
                v = before(pair, len(DVE_A), len(DVE_B), part_a) + (own.index(half) + 1)
                return dve_turned, v, v
            v = before(pair, 8 - 2 * len(DVE_A), 8 - 2 * len(DVE_B), part_a)
            n = 2 * [h for h in range(4) if h not in own].index(half)
            return pe_turned, v + (n + 1), v + (n + 2)

        U_RAW = Q_U // 8 * DMA1
        V_RAW = [U_RAW + PAIRS_A * (DMA4 if k in DVE_A else DMA1)
                 + (PAIRS - PAIRS_A) * (DMA4 if k in DVE_B else DMA1) for k in range(RAWS)]
        block = ctx.enter_context(nc.Block())

        @block.sync
        def _(sp):
            def dense(view, first_q, g, wait):
                for kk in range(KT // 2):
                    if wait or kk >= RAWS:
                        sp.wait_ge(lo_ready, g * KT + first_q + 2 * kk + 2 - 2 * RAWS)
                    sp.dma_start(raw[:, kk % RAWS, :, :], view[:, 2 * kk:2 * kk + 2, bass.ds(g * COLS, COLS)]
                                 ).then_inc(raw_ready[kk % RAWS], 16)

            def by_rows(g, wait):
                for kk in range(KT // 2):
                    if wait or kk >= RAWS:
                        sp.wait_ge(lo_ready, g * KT + Q_PQ + 2 * kk + 2 - 2 * RAWS)
                    c = 2 * kk % 8
                    sp.dma_start(raw[:, kk % RAWS, :, :], w_pq_v[kk // 4, :, c:c + 2, bass.ds(g * COLS, COLS)]
                                 ).then_inc(raw_ready[kk % RAWS], 16)

            def u_half(i, k, own):
                j = i * 2 + k // 2
                if k in own:
                    for r in range(ROWS):
                        sp.dma_start(raw[32 * r:32 * r + 32, k, :, :].rearrange("p a (b d) -> p (a b) d", b=2),
                                     u_dve[k % 2, r, :, bass.ds(j * 4, 4), :]).then_inc(raw_ready[k], 16)
                else:
                    sp.dma_start(raw[:, k, :, :].rearrange("p a b -> p (a b)"),
                                 u_pe[bass.ds(j * P, P), k % 2 * 1024:k % 2 * 1024 + 1024]).then_inc(raw_ready[k], 16)

            def u_pair(i, own, part_a):
                for k in range(RAWS):
                    s, _, v = turned_at(k, i - 1, part_a)
                    sp.wait_ge(s, v)
                    u_half(i, k, own)

            def v_half(j, hf, slot):
                sp.dma_start(raw[:, slot, :, :].rearrange("p a b -> p (a b)"),
                             v_v[bass.ds(j * P, P), hf * 1024:hf * 1024 + 1024]).then_inc(raw_ready[slot], 16)

            sp.dma_start(x_nat[:, :, :], x.rearrange("a (b p) d -> (a p) b d", p=P)).then_inc(x_in, 16)
            sp.dma_start(small[:, :, :], small_tables).then_inc(x_in, 16)
            dense(w_in_v, 0, 0, False)
            sp.dma_start(cst[:, :], tables).then_inc(tab_in, 16)
            sp.dma_start(norm_w[:, 0:SBH * HD], sb_norm_w.partition_broadcast(P)).then_inc(norms_in, 16)
            sp.dma_start(norm_w[:, SBH * HD:D], ret_norm_w.partition_broadcast(P)).then_inc(norms_in, 16)
            with sp.Fori(1, G_IN) as g:
                dense(w_in_v, 0, g, True)
            dense(w_out_v, Q_OUT, 0, True)
            sp.wait_ge(mixed_ready, TB)
            sp.dma_start(keys_nat[:, :, :], sub_keys.rearrange("l h c k d -> k (l h c) d")).then_inc(keys_in, 16)
            sp.dma_start(ln_w[:, :], ln1_w.partition_broadcast(P)).then_inc(ln1_in, 16)
            sp.dma_start(ln_b[:, :], ln1_b.partition_broadcast(P)).then_inc(ln1_in, 16)
            with sp.Fori(1, G_OUT) as g:
                dense(w_out_v, Q_OUT, g, True)
            by_rows(0, True)
            sp.wait_ge(x1_ready, TB)
            sp.dma_start(x1_dram, x_nat[:, :, :]).then_inc(x1_out, 16)
            with sp.Fori(1, G_PQ) as g:
                by_rows(g, True)
            for k in range(RAWS):
                sp.wait_ge(lo_ready, Q_U - 2 * RAWS + 2 * k + 2)
                u_half(0, k, DVE_A)
            with sp.Fori(1, PAIRS_A) as i:
                u_pair(i, DVE_A, True)
            u_pair(PAIRS_A, DVE_B, True)
            with sp.Fori(PAIRS_A + 1, PAIRS) as i:
                u_pair(i, DVE_B, False)
            for k in range(RAWS):
                s, _, v = turned_at(k, PAIRS - 1, False)
                sp.wait_ge(s, v)
                v_half(k // 2, k % 2, k)
            sp.wait_ge(split_free, Q_V + SPLITS)
            sp.dma_start(ln2w[:, :], ln2_w.partition_broadcast(P)).then_inc(ln2_in, 16)
            sp.dma_start(ln2b[:, :], ln2_b.partition_broadcast(P)).then_inc(ln2_in, 16)
            sp.wait_ge(x1_out, 16)
            sp.dma_start(x1_back[:, :, :], x1_dram).then_inc(x1_in, 16)
            with sp.Fori(1, PAIRS) as i:
                for n in range(RAWS):
                    sp.wait_ge(lo_ready, i * 8 + (Q_V + 2 * n + 2 - 2 * RAWS))
                    v_half(i * 2 + n // 2, n % 2, n)
            for b in range(TB):
                sp.wait_ge(y_ready, b + 1)
                sp.dma_start(out[0, b * P:(b + 1) * P, :], y_out[:, b, :]).then_inc(y_stored, 16)
            sp.wait_ge(y_stored, 16 * TB)

        @block.tensor
        def _(pe):
            pe.sem_inc(split_free, SPLITS)

            def turn(fill, sources):
                if fill >= 4:
                    pe.wait_ge(turn_done, fill - 3)
                for i, s in enumerate(sources):
                    last = nc.tensor.transpose(ps[:, 4 + fill % 4, i * P:(i + 1) * P], s, ident)
                last.then_inc(turned, 1)

            def three(acc, l_hi, l_lo, r_hi, r_lo, first, last):
                nc.tensor.matmul(acc, l_hi, r_hi, start=first, stop=False)
                nc.tensor.matmul(acc, l_hi, r_lo, start=False, stop=False)
                return nc.tensor.matmul(acc, l_lo, r_hi, start=False, stop=last)

            def dense(g, parity, first_q):
                pe.wait_ge(acc_free, g + 1)
                for k in range(KT):
                    pe.wait_ge(lo_ready, g * KT + (k + 1))
                    for b in range(TB):
                        c = slice(b * P, (b + 1) * P)
                        last = three(ps[:, 2 * parity + b, :], act_hi[:, k, c], act_lo[:, k, c],
                                     split_hi[:, k % SPLITS, :], split_lo[:, k % SPLITS, :], k == 0, k == KT - 1)
                    last.then_inc(split_free, 1)

            pe.wait_ge(x_in, 32)
            for f in range(8):
                turn(F_X + f, [x_nat[:, f // 4, (f % 4 * 4 + i) * P:(f % 4 * 4 + i + 1) * P] for i in range(4)])
            pe.wait_ge(turn_done, F_X + 8)
            with pe.Fori(0, G_IN // 2) as i:
                for s in range(2):
                    dense(i * 2 + s, s, 0)

            pe.wait_ge(tab_in, 16)
            pe.wait_ge(acc_free, G_IN + 2)
            heads = SBH + RTH

            def head_cols(it, kind):
                first = (0 if it < SBH else 3 * SBH * HD) + kind * SBH * HD + (it % SBH) * HD
                return slice(first, first + HD)

            def turn_qk(it):
                if it == SBH:
                    pe.wait_ge(rot_q, 1)
                    pe.wait_ge(rot_k, 1)
                if it >= 2:
                    pe.wait_ge(q_out, it - 1)
                    pe.wait_ge(k_out, it - 1)
                for n in range(4):
                    last = nc.tensor.transpose(ps[:, it % 2 * 4, n * P:(n + 1) * P],
                                               proj[:, n % 2, head_cols(it, n // 2)], ident)
                last.then_inc(qk_turned, 1)

            def z_product(it):
                bank, p = it % 2 * 4 + 1, it % 2
                pe.wait_ge(q_out, it + 1)
                pe.wait_ge(k_out, it + 1)
                if it >= 2:
                    pe.wait_ge(z_copied, it - 1) if it - 2 < SBH else pe.wait_ge(a_ready, it - 1)
                nc.tensor.matmul(ps[:, bank, 0:256], qk_t[:, p, 1, 0:P], qk_t[:, p, 0, :], start=True, stop=True)
                nc.tensor.matmul(ps[:, bank, 256:384], qk_t[:, p, 1, P:SEQ], qk_t[:, p, 0, P:SEQ],
                                 start=True, stop=True).then_inc(z_ready, 1)

            def suffix_sums(it):
                bank, p = it % 2 * 4 + 2, it % 2
                pe.wait_ge(spm_ready, it + 1)
                if it >= 2:
                    pe.wait_ge(la_ready, it - 1)
                nc.tensor.matmul(ps[:, bank, 0:256], tri, soft_p[:, p, 0:256], start=True, stop=False)
                nc.tensor.matmul(ps[:, bank, P:256], ones, soft_p[:, p, 256:384], start=False, stop=False)
                nc.tensor.matmul(ps[:, bank, 0:256], ident, masked[:, 0:256], start=False, stop=True)
                nc.tensor.matmul(ps[:, bank, 256:384], tri, soft_p[:, p, 256:384], start=True, stop=False)
                nc.tensor.matmul(ps[:, bank, 256:384], ident, masked[:, 256:384], start=False, stop=True
                                 ).then_inc(c_ready, 1)

            def values(it):
                bank, p = it % 2 * 4 + 3, it % 2
                pe.wait_ge(a_ready, it + 1)
                if it >= 2:
                    pe.wait_ge(o_out, it - 1)
                v = head_cols(it, 2)
                nc.tensor.matmul(ps[:, bank, 0:P], soft_a[:, p, 0:P], proj[:, 0, v], start=True, stop=True)
                nc.tensor.matmul(ps[:, bank, P:256], soft_a[:, p, P:256], proj[:, 0, v], start=True, stop=False)
                nc.tensor.matmul(ps[:, bank, P:256], soft_a[:, p, 256:384], proj[:, 1, v], start=False, stop=True
                                 ).then_inc(o_ready, 1)

            for s in range(heads + 3):
                if s < heads:
                    turn_qk(s)
                if 0 <= s - 1 < heads:
                    z_product(s - 1)
                if 0 <= s - 2 < SBH:
                    suffix_sums(s - 2)
                if 0 <= s - 3 < heads:
                    values(s - 3)

            for f in range(8):
                if f % 4 == 0:
                    pe.wait_ge(mixed_ready, f // 4 + 1)
                turn(F_MIX + f, [mixed[:, f // 4, (f % 4 * 4 + i) * P:(f % 4 * 4 + i + 1) * P] for i in range(4)])
            pe.wait_ge(turn_done, F_MIX + 8)
            with pe.Fori(0, G_OUT // 2) as i:
                for s in range(2):
                    dense(i * 2 + (G_IN + s), s, Q_OUT)

            pe.wait_ge(keys_in, 16)
            for f in range(4):
                turn(F_KEYS + f, [keys_nat[:, 4 * f + i, :] for i in range(4)])
            for f in range(8):
                if f % 4 == 0:
                    pe.wait_ge(x1_ready, f // 4 + 1)
                dims = x_nat[:, f // 4, :].rearrange("p (h m c) -> p h c m", h=2, c=8)
                turn(F_X1 + f, [dims[:, f % 4 // 2, f % 2 * 4 + i, :] for i in range(4)])
            pe.wait_ge(turn_done, F_X1 + 8)
            with pe.Fori(0, G_PQ // 2) as i:
                for s in range(2):
                    dense(i * 2 + (G_IN + G_OUT + s), s, Q_PQ)
            pe.wait_ge(acc_free, G_IN + G_OUT + G_PQ + 2)
            for f in range(8):
                turn(F_Q + f, [q_nat[:, f // 4, (f % 4 * 4 + i) * P:(f % 4 * 4 + i + 1) * P] for i in range(4)])
            pe.wait_ge(turn_done, F_Q + 8)
            for f in range(8):
                if f >= 2:
                    pe.wait_ge(sc_out, f - 1)
                for i in range(4):
                    s, b = f % 4 * 4 + i, f // 4
                    last = nc.tensor.matmul(ps[:, 2 + f % 2, i * P:(i + 1) * P], q_t[:, s, b * P:(b + 1) * P],
                                            keys_t[:, s, :], start=True, stop=True)
                last.then_inc(sc_ready, 1)

            def turn_u(pair, q, own, part_a):
                k = q // 2
                if k in own:
                    return
                if q % 2 == 0:
                    pe.wait_ge(raw_ready[k], u_raw(k, pair, part_a))
                blocks = raw[:, k, :, :].rearrange("p a (m c) -> p c (a m)", c=8)
                for i in range(4):
                    last = nc.tensor.transpose(ps[:, 4 + q % 4, i * P:(i + 1) * P], blocks[:, q % 2 * 4 + i, :],
                                               ident)
                last.then_inc(pe_turned, 1)

            LEAD = 3

            def score_pair(pair, own, part_a, nxt=None, next_a=False, after=None):
                for q in range(8):
                    if q % 4 == 0:
                        pe.wait_ge(score_free, pair * 2 + (q // 4 + 1))
                    if q + LEAD < 8:
                        turn_u(pair, q + LEAD, own, part_a)
                    elif nxt is not None:
                        turn_u(pair + 1, q + LEAD - 8, nxt, next_a)
                    pe.wait_ge(lo_ready, pair * 8 + (Q_U + q + 1))
                    for i in range(4):
                        last = three(ps[:, q // 4, 0:SEQ], split_hi[:, q % SPLITS, i * P:(i + 1) * P],
                                     split_lo[:, q % SPLITS, i * P:(i + 1) * P], act_hi[:, q % 4 * 4 + i, :],
                                     act_lo[:, q % 4 * 4 + i, :], q % 4 == 0 and i == 0, q % 4 == 3 and i == 3)
                    last.then_inc(split_free, 1)
                    if after:
                        after(q)

            def picks_after(q):
                if q == 5:
                    pe.wait_ge(topk_done, 1)
                    for a, bank, col in ((0, 2, 0), (1, 3, 0), (2, 2, SEQ)):
                        for b in range(TB):
                            last = nc.tensor.transpose(ps[:, bank, col + b * P:col + (b + 1) * P],
                                                       pick_n[:, a, b, :], ident)
                    last.then_inc(picks_turned, 1)

            def gates_after(n0):
                def after(q):
                    if q % 4 == 1:
                        n, parity = n0 + q // 4, q // 4
                        pe.wait_ge(weighted, n + 1)
                        pe.wait_ge(gates_free, n + 1)
                        for i in range(4):
                            last = nc.tensor.matmul(ps[:, 2 + parity, i * P:(i + 1) * P], hot[:, parity, 1, i, :],
                                                    hot[:, parity, 0, i, :], start=True, stop=True)
                        last.then_inc(gate_ready, 1)
                return after

            for q in range(LEAD):
                turn_u(0, q, DVE_A, True)
            with pe.Fori(0, PAIRS_A - 1) as i:
                score_pair(i, DVE_A, True, DVE_A, True)
            score_pair(PAIRS_A - 1, DVE_A, True, DVE_B, False)
            score_pair(PICKS, DVE_B, False, DVE_B, False, picks_after)
            score_pair(PICKS + 1, DVE_B, False, DVE_B, False)
            with pe.Fori(GATE0, GATE0 + GATES // 2) as i:
                score_pair(i, DVE_B, False, DVE_B, False, gates_after(i * 2 - 2 * GATE0))
            with pe.Fori(GATE0 + GATES // 2, PAIRS - 1) as i:
                score_pair(i, DVE_B, False, DVE_B, False)
            score_pair(PAIRS - 1, DVE_B, False)

            def value_pair(n0, first, last_pair):
                for q in range(8):
                    t = q // 4
                    if q % 4 == 0:
                        pe.wait_ge(w_lo, (n0 // 4 + t + 1) if isinstance(n0, int) else n0 // 4 + (t + 1))
                    pe.wait_ge(lo_ready, n0 + (Q_V + q + 1))
                    for b in range(TB):
                        c = slice(b * P, (b + 1) * P)
                        last = three(ps[:, b * 4 + q % 4, :], whalf_hi[:, t, c], whalf_lo[:, t, c],
                                     split_hi[:, q % SPLITS, :], split_lo[:, q % SPLITS, :],
                                     first and t == 0, last_pair and t == 1)
                    last.then_inc(split_free, 1)

            pe.wait_ge(gates_free, GATES + 2)
            pe.wait_ge(score_free, NT + 2)
            value_pair(0, True, False)
            with pe.Fori(1, NT // 2 - 1) as i:
                value_pair(i * 8, False, False)
            value_pair(NT * 4 - 8, False, True)

        @block.scalar
        def _(act):
            chain = Chain(act, a_chain)
            act.sem_inc(acc_free, 2)
            act.sem_inc(score_free, 2)

            def split(n, q, values=False):
                if q % 2 == 0:
                    start = (V_RAW[q // 2] - Q_V * DMA1 // 8) if values else 0
                    act.wait_ge(raw_ready[q // 2], n * (DMA1 // 8) + (start + DMA1))
                act.wait_ge(split_free, n + (q + 1))
                nc.scalar.activation(split_hi[:, q % SPLITS, :], raw[:, q // 2, q % 2, :], ACT.Copy
                                     ).then_inc(hi_ready, 1)

            def dense_group(g, parity, evacuate):
                for q in range(4, 20):
                    split(g * KT + q // 8 * 8, q % 8)
                if evacuate:
                    evacuate(g, parity)

            def turned_hi(first):
                for f in range(first, first + 8):
                    act.wait_ge(turned, f + 1)
                    fb, k = (f - first) // 4, (f - first) % 4 * 4
                    nc.scalar.activation(act_hi[:, k:k + 4, fb * P:(fb + 1) * P],
                                         ps[:, 4 + f % 4, :].rearrange("p (k t) -> p k t", k=4), ACT.Copy
                                         ).then_inc(turn_hi, 1)

            turned_hi(F_X)
            for q in range(4):
                split(0, q)

            def to_proj(g, parity):
                act.wait_ge(split_free, g * KT + (KT + SPLITS))
                nc.scalar.activation(proj[:, :, bass.ds(g * COLS, COLS)], ps[:, 2 * parity:2 * parity + 2, :],
                                     ACT.Copy).then_inc(acc_free, 1)

            with act.Fori(0, G_IN // 2) as i:
                for s in range(2):
                    dense_group(i * 2 + s, s, to_proj)

            heads = SBH + RTH
            nc.scalar.preload_act_table_set("natural_log_exp_and_others")
            act.wait_ge(acc_free, G_IN + 2)

            def queries_out(it):
                act.wait_ge(qk_turned, it + 1)
                if it >= 2:
                    act.wait_ge(z_ready, it - 1)
                nc.scalar.activation(qk_t[:, it % 2, 0, :], ps[:, it % 2 * 4, 0:256], ACT.Copy,
                                     scale=SCALE if it < SBH else 1.0).then_inc(q_out, 1)

            def softplus_tail(it):
                p = it % 2
                act.wait_ge(z_ready, it + 1)
                if it >= 2:
                    act.wait_ge(la_ready, it - 1)
                z = ps[:, p * 4 + 1, 0:384]
                nc.scalar.activation(z_sb[:, p, :], z, ACT.Copy).then_inc(z_copied, 1)
                if it >= 2:
                    act.wait_ge(spm_ready, it - 1)
                act.wait_ge(z_copied, it + 1)
                chain.step(nc.scalar.activation(soft_l[:, p, :], z_sb[:, p, :], ACT.Abs))
                chain.step(nc.scalar.activation(soft_l[:, p, :], soft_l[:, p, :], ACT.Exp, scale=-1.0))
                nc.scalar.activation(soft_l[:, p, :], soft_l[:, p, :], ACT.Ln, bias=1.0).then_inc(soft_ready, 1)

            def weights(it):
                act.wait_ge(la_ready, it + 1)
                nc.scalar.activation(soft_a[:, it % 2, :], soft_p[:, it % 2, :], ACT.Exp).then_inc(a_ready, 1)

            def result_out(it):
                act.wait_ge(o_ready, it + 1)
                nc.scalar.activation(mixed[:, :, it * HD:(it + 1) * HD],
                                     ps[:, it % 2 * 4 + 3, 0:256].rearrange("p (b d) -> p b d", b=TB), ACT.Copy
                                     ).then_inc(o_out, 1)

            for s in range(heads + 3):
                if s < heads:
                    queries_out(s)
                if 0 <= s - 1 < SBH:
                    softplus_tail(s - 1)
                if 0 <= s - 2 < SBH:
                    weights(s - 2)
                if 0 <= s - 3 < heads:
                    result_out(s - 3)
            gate_cols = slice(INW - RTH * HD, INW)
            nc.scalar.activation(proj[:, :, gate_cols], proj[:, :, gate_cols], ACT.Silu).then_inc(gated, 1)

            turned_hi(F_MIX)
            with act.Fori(0, G_OUT) as i:
                dense_group(i + G_IN, 0, None)

            turned_hi(F_X1)

            def to_q(g, parity):
                n = g - G_IN - G_OUT
                act.wait_ge(split_free, g * KT + KT + SPLITS)
                nc.scalar.activation(q_nat[:, :, n * COLS:(n + 1) * COLS], ps[:, 2 * parity:2 * parity + 2, :],
                                     ACT.Copy).then_inc(acc_free, 1)

            for g in range(G_IN + G_OUT, G_IN + G_OUT + G_PQ - 1):
                dense_group(g, g % 2, to_q)
            g = G_IN + G_OUT + G_PQ - 1
            for q in range(4, 16):
                split(g * KT + q // 8 * 8, q % 8)
            to_q(g, g % 2)
            for f in range(8):
                act.wait_ge(sc_ready, f + 1)
                nc.scalar.activation(scores[:, f // 4, f % 4 * 4:f % 4 * 4 + 4, :].rearrange("p s k -> p (s k)"),
                                     ps[:, 2 + f % 2, :], ACT.Copy).then_inc(sc_out, 1)

            def split_u(pair, q, part_a):
                semaphore, first, second = turned_at(q // 2, pair, part_a)
                act.wait_ge(semaphore, second if q % 2 else first)
                act.wait_ge(split_free, pair * 8 + (Q_U + q + 1))
                nc.scalar.activation(split_hi[:, q % SPLITS, :], ps[:, 4 + q % 4, :], ACT.Copy).then_inc(hi_ready, 1)

            def gelu(pair, t, is_late):
                act.wait_ge(split_free, pair * 8 + (Q_U + SPLITS + 4 * t + 4))
                if is_late:
                    act.wait_ge(late_used, pair * 2 + (t + 1 - LATE))
                    dst = late[:, t, :]
                else:
                    dst = wexp[:, bass.ds(pair * 2 + t, 1), :].rearrange("p a t -> p (a t)")
                nc.scalar.activation(dst, ps[:, t, 0:SEQ], ACT.Gelu).then_inc(score_free, 1)

            def hot_rows(n, parity):
                act.wait_ge(dist_ready, n + 1)
                d = hot[:, parity, :, :, :].rearrange("p a t k -> p (a t k)")
                nc.scalar.activation(d, d, ACT.Abs).then_inc(abs_ready, 1)
                act.wait_ge(abs_ready, n + 1)
                nc.scalar.activation(d, d, ACT.Relu, scale=-1.0, bias=1.0).then_inc(hot_ready, 1)

            def u_pair(pair, part_a, next_a, late_tiles=(), groups=None):
                for q in range(4, 8):
                    split_u(pair, q, part_a)
                gelu(pair, 0, 0 in late_tiles)
                split_u(pair + 1, 0, next_a)
                if groups is not None:
                    hot_rows(groups, 0)
                for q in range(1, 4):
                    split_u(pair + 1, q, next_a)
                gelu(pair, 1, 1 in late_tiles)
                if groups is not None:
                    hot_rows(groups + 1, 1)

            act.wait_ge(x1_out, 16)
            act.sem_inc(late_used, 2)
            nc.scalar.preload_act_table_set("gelu_and_others")
            for q in range(4):
                split_u(0, q, True)
            with act.Fori(0, PAIRS_A - 6) as i:
                u_pair(i, True, True)
            act.wait_ge(best_ready, 1)
            nc.scalar.activation(best[:, :, :], best[:, :, :], ACT.Exp).then_inc(exp_ready, 1)
            nc.scalar.preload_act_table_set("gelu_and_others")
            with act.Fori(PAIRS_A - 6, PAIRS_A - 1) as i:
                u_pair(i, True, True)
            u_pair(PAIRS_A - 1, True, False, (1,))
            u_pair(PICKS, False, False, (0, 1))
            with act.Fori(GATE0 - 1, GATE0 - 1 + GATES // 2) as i:
                u_pair(i, False, False, (0, 1), i * 2 - (2 * GATE0 - 2))
            with act.Fori(GATE0 - 1 + GATES // 2, PAIRS - 1) as i:
                u_pair(i, False, False, (0, 1))
            for q in range(4, 8):
                split_u(PAIRS - 1, q, False)
            gelu(PAIRS - 1, 0, True)
            gelu(PAIRS - 1, 1, True)

            def split_w(n, t, static=False):
                act.wait_ge(split_free, n + (Q_V + SPLITS + 4 * t - 4) if static or t > 0 else n + (Q_V + SPLITS - 4))
                nc.scalar.activation(whalf_hi[:, t % 2, :],
                                     wexp[:, bass.ds(n // 4 + t, 1), :].rearrange("p a t -> p (a t)"), ACT.Copy
                                     ).then_inc(w_hi, 1)

            for q in range(4):
                split(Q_V, q, True)
            act.wait_ge(gates_free, GATES + 2)
            act.wait_ge(late_used, NT - LATE + 2)
            split_w(0, 0)

            with act.Fori(0, NT // 2 - 1) as i:
                split_w(i * 8, 1)
                for q in range(4, 8):
                    split(i * 8 + Q_V, q, True)
                split_w(i * 8, 2)
                for q in range(4):
                    split(i * 8 + (Q_V + 8), q, True)
            n = NT * 4 - 8
            split_w(n, 1)
            for q in range(4, 8):
                split(n + Q_V, q, True)

        @block.vector
        def _(dve):
            chain = Chain(dve, v_chain)
            vec = nc.vector

            def split(n, q):
                dve.wait_ge(hi_ready, n + (q + 1))
                vec.tensor_tensor(split_lo[:, q % SPLITS, :], raw[:, q // 2, q % 2, :],
                                  split_hi[:, q % SPLITS, :].bitcast(f32), ALU.subtract).then_inc(lo_ready, 1)

            def dense_group(g):
                for q in range(4, 20):
                    split(g * KT + q // 8 * 8, q % 8)

            def turned_lo(first, order):
                for f in range(first, first + 8):
                    dve.wait_ge(turn_hi, order * 8 + f - first + 1)
                    fb, k = (f - first) // 4, (f - first) % 4 * 4
                    vec.tensor_tensor(act_lo[:, k:k + 4, fb * P:(fb + 1) * P],
                                      ps[:, 4 + f % 4, :].rearrange("p (k t) -> p k t", k=4),
                                      act_hi[:, k:k + 4, fb * P:(fb + 1) * P].bitcast(f32), ALU.subtract
                                      ).then_inc(turn_done, 1)

            turned_lo(F_X, 0)
            for q in range(4):
                split(0, q)
            with dve.Fori(0, G_IN) as i:
                dense_group(i)

            dve.wait_ge(tab_in, 16)
            dve.wait_ge(acc_free, G_IN + 2)

            def rotary(eng, own, first_col, tmp, b):
                xs = proj[:, b, first_col:first_col + RTH * HD].rearrange("p (h d) -> p h d", h=RTH)
                half = HD // 2
                eng.tensor_tensor(tmp[:, 1, :, 0:half], xs[:, :, half:HD],
                                  sin_t[:, b:b + 1, 0:half].to_broadcast([P, RTH, half]), ALU.mult)
                eng.tensor_tensor(tmp[:, 1, :, half:HD], xs[:, :, 0:half],
                                  sin_t[:, b:b + 1, half:HD].to_broadcast([P, RTH, half]), ALU.mult)
                own.step(eng.tensor_tensor(tmp[:, 0, :, :], xs, cos_t[:, b:b + 1, :].to_broadcast([P, RTH, HD]),
                                           ALU.mult))
                ins = eng.tensor_tensor(xs, tmp[:, 0, :, :], tmp[:, 1, :, :], ALU.add)
                own.step(ins)

            heads = SBH + RTH

            def keys_out(it):
                dve.wait_ge(q_out, it + 1)
                if it >= 2:
                    dve.wait_ge(z_ready, it - 1)
                vec.tensor_copy(qk_t[:, it % 2, 1, :], ps[:, it % 2 * 4, 256:512]).then_inc(k_out, 1)

            def softplus(it):
                p = it % 2
                dve.wait_ge(soft_ready, it + 1)
                if it >= 2:
                    dve.wait_ge(a_ready, it - 1)
                chain.step(vec.scalar_tensor_tensor(out=soft_p[:, p, :], in0=z_sb[:, p, :], scalar=0.0,
                                                    in1=soft_l[:, p, :], op0=ALU.max, op1=ALU.add))
                vec.tensor_tensor(soft_p[:, p, :], soft_p[:, p, :], causal, ALU.mult).then_inc(spm_ready, 1)

            def log_weights(it):
                p = it % 2
                dve.wait_ge(c_ready, it + 1)
                if it >= 2:
                    dve.wait_ge(o_ready, it - 1)
                vec.tensor_tensor(soft_p[:, p, :], z_sb[:, p, :], ps[:, p * 4 + 2, 0:384], ALU.subtract
                                  ).then_inc(la_ready, 1)

            def decayed(it):
                p = it % 2
                dve.wait_ge(z_ready, it + 1)
                dve.wait_ge(o_ready, it - 1)
                vec.tensor_tensor(soft_a[:, p, :], ps[:, p * 4 + 1, 0:384], decay[:, it - SBH, :], ALU.mult
                                  ).then_inc(a_ready, 1)

            for s in range(heads + 3):
                if s < heads:
                    keys_out(s)
                if 0 <= s - 1 < SBH:
                    softplus(s - 1)
                if 0 <= s - 2 < SBH:
                    log_weights(s - 2)
                elif SBH <= s - 2 < heads:
                    decayed(s - 2)
                if s in (2, 3):
                    rotary(vec, chain, 3 * SBH * HD, rot_v, s - 2)
                    if s == 3:
                        vec.engine_nop().then_inc(rot_q, 1)

            dve.wait_ge(o_out, heads)
            dve.wait_ge(norms_in, 32)
            dve.wait_ge(halfexp, 1)
            m4 = mixed[:, :, :].rearrange("p b (h d) -> p b h d", h=heads)
            s4 = square[:, :, :].rearrange("p b (h d) -> p b h d", h=heads)
            sums = stats[:, SUMS:SUMS + 32].rearrange("p (b h) -> p b h", b=TB)
            for b in range(TB):
                chain.step(vec.tensor_reduce(sums[:, b, SBH:], m4[:, b, SBH:, :], AX.X, ALU.add))
                chain.step(vec.tensor_scalar(sums[:, b, SBH:], sums[:, b, SBH:], 1.0 / HD, None, ALU.mult))
                chain.step(vec.tensor_tensor(m4[:, b, SBH:, :], m4[:, b, SBH:, :],
                                             sums[:, b, SBH:].unsqueeze(2).to_broadcast([P, RTH, HD]), ALU.subtract))
                chain.step(vec.tensor_tensor(square[:, b, :], mixed[:, b, :], mixed[:, b, :], ALU.mult))
                chain.step(vec.tensor_reduce(stats[:, VAR + 16 * b:VAR + 16 * b + 16], s4[:, b, :, :], AX.X, ALU.add))
                vec.tensor_scalar(stats[:, VAR + 16 * b:VAR + 16 * b + 16], stats[:, VAR + 16 * b:VAR + 16 * b + 16],
                                  1.0 / HD, NORM_EPS, ALU.mult, ALU.add).then_inc(var_ready, 1)
            dve.wait_ge(gated, 1)
            ret = slice(SBH * HD, D)
            for b in range(TB):
                dve.wait_ge(rstd_ready, b + 1)
                chain.step(vec.tensor_tensor(m4[:, b, :, :], m4[:, b, :, :],
                                             stats[:, RSTD + 16 * b:RSTD + 16 * b + 16].unsqueeze(2)
                                             .to_broadcast([P, heads, HD]), ALU.mult))
                chain.step(vec.tensor_tensor(mixed[:, b, :], mixed[:, b, :], norm_w[:, :], ALU.mult))
                vec.tensor_tensor(mixed[:, b, ret], mixed[:, b, ret], proj[:, b, INW - RTH * HD:INW], ALU.mult
                                  ).then_inc(mixed_ready, 1)

            turned_lo(F_MIX, 1)
            with dve.Fori(0, G_OUT // 2) as i:
                for s in range(2):
                    dense_group(i * 2 + (G_IN + s))
                    dve.wait_ge(split_free, (i * 2 + (G_IN + s)) * KT + (KT + SPLITS))
                    part = x_nat[:, :, bass.ds((i * 2 + s) * COLS, COLS)]
                    vec.scalar_tensor_tensor(out=part, in0=part, scalar=ALPHA, in1=ps[:, 2 * s:2 * s + 2, :],
                                             op0=ALU.mult, op1=ALU.add).then_inc(acc_free, 1)

            def layer_norm(buf, w, b_, blk, n_var):
                st = stats[:, 160:184].rearrange("p (c s) -> p c s", c=4)
                for c in range(4):
                    chain.step(vec.bn_stats(st[:, c, :], buf[:, blk, c * COLS:(c + 1) * COLS]))
                chain.step(vec.bn_aggr(stats[:, MEAN:MEAN + 2], stats[:, 160:184]))
                vec.tensor_scalar(stats[:, VAR:VAR + 1], stats[:, MEAN + 1:MEAN + 2], LN_EPS, None, ALU.add
                                  ).then_inc(var_ready, 1)
                dve.wait_ge(rstd_ready, n_var)
                row = buf[:, blk, :]
                chain.step(vec.tensor_scalar(row, row, stats[:, MEAN:MEAN + 1], stats[:, RSTD:RSTD + 1],
                                             ALU.subtract, ALU.mult))
                chain.step(vec.tensor_tensor(row, row, w[:, :], ALU.mult))
                return vec.tensor_tensor(row, row, b_[:, :], ALU.add)

            dve.wait_ge(acc_free, G_IN + G_OUT + 2)
            dve.wait_ge(ln1_in, 32)
            for b in range(TB):
                layer_norm(x_nat, ln_w, ln_b, b, TB + b + 1).then_inc(x1_ready, 1)

            for f in range(4):
                dve.wait_ge(turned, F_KEYS + f + 1)
                vec.tensor_copy(keys_t[:, 4 * f:4 * f + 4, :].rearrange("p s k -> p (s k)"),
                                ps[:, 4 + (F_KEYS + f) % 4, :]).then_inc(turn_done, 1)
            turned_lo(F_X1, 2)
            with dve.Fori(0, G_PQ - 1) as i:
                dense_group(i + (G_IN + G_OUT))
            g = G_IN + G_OUT + G_PQ - 1
            for q in range(4, 16):
                split(g * KT + q // 8 * 8, q % 8)
            for f in range(8):
                dve.wait_ge(turned, F_Q + f + 1)
                vec.tensor_copy(q_t[:, f % 4 * 4:f % 4 * 4 + 4, f // 4 * P:(f // 4 + 1) * P],
                                ps[:, 4 + f % 4, :].rearrange("p (k t) -> p k t", k=4)).then_inc(turn_done, 1)

            def split_u(pair, q):
                dve.wait_ge(hi_ready, pair * 8 + (Q_U + q + 1))
                vec.tensor_tensor(split_lo[:, q % SPLITS, :], ps[:, 4 + q % 4, :],
                                  split_hi[:, q % SPLITS, :].bitcast(f32), ALU.subtract).then_inc(lo_ready, 1)

            def turn_u(pair, k, own, part_a):
                if k not in own:
                    return
                dve.wait_ge(raw_ready[k], u_raw(k, pair, part_a))
                dve.wait_ge(lo_ready, pair * 8 + (Q_U + 2 * k - 2))
                bank = 4 + k % 2 * 2
                vec.transpose(ps[:, bank:bank + 2, :].rearrange("p a (c g i) -> p g (a c) i", g=4, i=32),
                              raw[:, k, :, :].rearrange("p a (b q c) -> p (a b) c q", b=2, q=32)
                              ).then_inc(dve_turned, 1)

            def split_turn(pair, k, own, part_a, nxt=None, next_a=False, between=None, behind=None):
                split_u(pair, 2 * k)
                if between:
                    between()
                split_u(pair, 2 * k + 1)
                if behind:
                    behind()
                if nxt is not None:
                    turn_u(pair + 1, k - 2, nxt, next_a)

            class LoopChain:

                def __init__(self, i, first, steps):
                    self.i, self.first, self.steps, self.n = i, first, steps, 0

                def add(self, instruction):
                    self.n += 1
                    instruction.then_inc(v_chain, 1)

                def step(self, instruction):
                    self.add(instruction)
                    dve.wait_ge(v_chain, self.i * self.steps + (self.first + self.n))
                    dve.sem_inc(carried, 1)

            def flat(ap, pattern="p a b -> p (a b)"):
                return ap.rearrange(pattern)

            sc3 = flat(scores[:, :, :, :], "p b s k -> p (b s) k")
            TOP_STEPS = 18
            dve.wait_ge(sc_out, 8)
            c0 = chain.n
            dve.wait_ge(turn_done, F_Q + 8)
            for k in range(2):
                turn_u(0, k, DVE_A, True)
            for k in range(2):
                split_u(0, 2 * k)
                split_u(0, 2 * k + 1)
                turn_u(0, k + 2, DVE_A, True)
            with dve.Fori(0, TB * PH) as i:
                lc = LoopChain(i, c0, TOP_STEPS)
                halves = range(2)
                half_rest = [rest[:, c * PKEYS:(c + 1) * PKEYS] for c in halves]

                def largest():
                    lc.step(vec.tensor_copy(head_s[:, :, :], sc3[:, bass.ds(i * 2, 2), :]))
                    lc.add(vec.max(top_v[:, 0, 0:8], head_s[:, 0, :]))
                    lc.step(vec.max(top_v[:, 1, 0:8], head_s[:, 1, :]))

                def their_places():
                    for c in halves:
                        lc.add(vec.max_index(head_i[:, c, 0:8], top_v[:, c, 0:8], head_s[:, c, :]))
                    lc.add(vec.match_replace(half_rest[0], top_v[:, 0, 0:8], head_s[:, 0, :], LOWEST))
                    lc.step(vec.match_replace(half_rest[1], top_v[:, 1, 0:8], head_s[:, 1, :], LOWEST))

                def next_largest():
                    lc.add(vec.max(top_v[:, 0, 8:16], half_rest[0]))
                    lc.step(vec.max(top_v[:, 1, 8:16], half_rest[1]))
                    for c in halves:
                        lc.add(vec.max_index(head_i[:, c, 8:16], top_v[:, c, 8:16], half_rest[c]))

                def candidates():
                    lc.step(vec.tensor_tensor(cand[:, :, :], top_v[:, 0, :].unsqueeze(2).to_broadcast([P, TOPK, TOPK]),
                                              top_v[:, 1, :].unsqueeze(1).to_broadcast([P, TOPK, TOPK]), ALU.add))
                    lc.step(vec.max(head_b[:, 0:8], flat(cand[:, :, :])))

                def their_sums():
                    lc.add(vec.max_index(head_p[:, 0:8], head_b[:, 0:8], flat(cand[:, :, :])))
                    lc.step(vec.match_replace(rest[:, :], head_b[:, 0:8], flat(cand[:, :, :]), LOWEST))
                    lc.step(vec.max(head_b[:, 8:16], rest[:, :]))
                    lc.step(vec.max_index(head_p[:, 8:16], head_b[:, 8:16], rest[:, :]))

                def keep_picks():
                    vec.tensor_copy(idx_u[:, bass.ds(i, 1), :, :].rearrange("p a c k -> p (a c) k"), head_i[:, :, :])
                    vec.tensor_copy(best[:, bass.ds(i, 1), :].rearrange("p a k -> p (a k)"), head_b[:, :])
                    lc.step(vec.tensor_copy(pos_u[:, bass.ds(i, 1), :].rearrange("p a k -> p (a k)"), head_p[:, :]))

                split_turn(i, 2, DVE_A, True, DVE_A, True, between=largest, behind=their_places)
                split_turn(i, 3, DVE_A, True, DVE_A, True, between=next_largest)
                split_turn(i, 4, DVE_A, True, DVE_A, True, between=candidates, behind=their_sums)
                split_turn(i, 5, DVE_A, True, DVE_A, True, between=keep_picks)
                assert lc.n == TOP_STEPS
            chain.n += TB * PH * TOP_STEPS

            def late_tile(pair, t):
                dve.wait_ge(score_free, pair * 2 + (t + 3))
                row = wexp[:, bass.ds(pair * 2 + t, 1), :].rearrange("p a t -> p (a t)")
                vec.tensor_tensor(row, row, late[:, t % 2, :], ALU.mult).then_inc(late_used, 1)

            def apply_gates(n, parity):
                dve.wait_ge(gate_ready, n + 1)
                part = wexp[:, :, bass.ds(n * 4, 4)]
                dve.wait_ge(late_used, n + (2 * GATE0 - LATE + 2))
                vec.tensor_tensor(part, part, ps[:, 2 + parity, :].rearrange("p (t j) -> p j t", t=4), ALU.mult
                                  ).then_inc(gates_free, 1)

            def u_pair(pair, own, part_a, nxt, next_a, late_tiles=False, groups=None, between=None):
                for k in (2, 3):
                    split_turn(pair, k, own, part_a, nxt, next_a)
                    if late_tiles and k == 2:
                        if groups is not None and not isinstance(groups, int):
                            dve.wait_ge(gates_free, groups + 2)
                        late_tile(pair, -1)
                if groups is not None:
                    apply_gates(groups, 0)
                for k in (4, 5):
                    split_turn(pair, k, own, part_a, nxt, next_a)
                    if late_tiles and k == 4:
                        if groups is not None:
                            dve.wait_ge(gates_free, groups + 3)
                        late_tile(pair, 0)
                if groups is not None:
                    apply_gates(groups + 1, 1)
                if between:
                    between()

            def softmax_start():
                chain.step(vec.tensor_copy(gsum[:, 0, :], best[:, :, 0]))
                vec.tensor_tensor(best[:, :, :], best[:, :, :], gsum[:, 0, :].unsqueeze(2)
                                  .to_broadcast([P, TB * PH, TOPK]), ALU.subtract).then_inc(best_ready, 1)
                chain.step(vec.tensor_scalar(pos_i[:, 0, :, :], pos_u[:, :, :], 4, None, ALU.logical_shift_right))
                chain.step(vec.tensor_scalar(pos_i[:, 1, :, :], pos_u[:, :, :], TOPK - 1, None, ALU.bitwise_and))
                chain.step(vec.tensor_copy(flat(pos_f[:, :, :, :], "p a b c -> p (a b c)"),
                                           flat(pos_i[:, :, :, :], "p a b c -> p (a b c)")))
                chain.step(vec.tensor_copy(flat(idx_f[:, :, :, :], "p a b c -> p (a b c)"),
                                           flat(idx_u[:, :, :, :], "p a b c -> p (a b c)")))

            u_pair(SOFT, DVE_A, True, DVE_A, True, between=softmax_start)

            DEC_STEPS = 6
            c1 = chain.n
            with dve.Fori(0, TB * PH // 2) as i:
                lc = LoopChain(i, c1, DEC_STEPS)
                o4 = onehot[:, :, :].rearrange("p (a k) j -> p a k j", a=2)

                def compare(h):
                    row = pos_f[:, h, bass.ds(i * 2, 2), :].rearrange("p a k -> p (a k)")
                    lc.step(vec.tensor_tensor(onehot[:, :, :], row.unsqueeze(2).to_broadcast([P, 2 * TOPK, TOPK]),
                                              iota[:, 0:TOPK].unsqueeze(1).to_broadcast([P, 2 * TOPK, TOPK]),
                                              ALU.is_equal))

                def select(h):
                    lc.step(vec.tensor_tensor(o4, o4, idx_f[:, bass.ds(i * 2, 2), h, :].unsqueeze(2)
                                              .to_broadcast([P, 2, TOPK, TOPK]), ALU.mult))

                def collect(h):
                    dst = pick_n[:, h, :, :].rearrange("p b k -> p (b k)")
                    lc.step(vec.tensor_reduce(dst[:, bass.ds(i * 2 * TOPK, 2 * TOPK)], onehot[:, :, :], AX.X, ALU.add))

                for h in range(2):
                    split_turn(i + (SOFT + 1), 2 + 2 * h, DVE_A, True, DVE_A, True,
                               between=lambda: compare(h), behind=lambda: select(h))
                    split_turn(i + (SOFT + 1), 3 + 2 * h, DVE_A, True, DVE_A, True, between=lambda: collect(h))
                assert lc.n == DEC_STEPS
            chain.n += TB * PH // 2 * DEC_STEPS

            def softmax_end():
                dve.wait_ge(exp_ready, 1)
                chain.step(vec.tensor_reduce(gsum[:, 0, :], best[:, :, :], AX.X, ALU.add))
                chain.step(vec.reciprocal(gsum[:, 1, :], gsum[:, 0, :]))
                vec.tensor_tensor(pick_n[:, 2, :, :].rearrange("p b (h k) -> p (b h) k", k=TOPK), best[:, :, :],
                                  gsum[:, 1, :].unsqueeze(2).to_broadcast([P, TB * PH, TOPK]), ALU.mult
                                  ).then_inc(topk_done, 1)

            assert SOFT + 1 + TB * PH // 2 == PAIRS_A - 1
            u_pair(PAIRS_A - 1, DVE_A, True, DVE_B, False, between=softmax_end)

            def picks_out():
                dve.wait_ge(picks_turned, 1)
                chain.step(vec.tensor_copy(picks_t[:, 0, :], ps[:, 2, 0:SEQ]))
                chain.step(vec.tensor_copy(picks_t[:, 1, :], ps[:, 3, 0:SEQ]))
                vec.tensor_copy(picks_t[:, 2, :], ps[:, 2, SEQ:2 * SEQ]).then_inc(picks_ready, 1)
                dve.sem_inc(gates_free, 2)

            dve.wait_ge(ones_ready, 1)
            u_pair(PICKS, DVE_B, False, DVE_B, False, True, between=picks_out)
            dve.wait_ge(ones_ready, 2)
            u_pair(PICKS + 1, DVE_B, False, DVE_B, False, True)
            with dve.Fori(GATE0, GATE0 + GATES // 2) as i:
                u_pair(i, DVE_B, False, DVE_B, False, True, i * 2 - 2 * GATE0)
            dve.wait_ge(gates_free, GATES + 2)
            with dve.Fori(GATE0 + GATES // 2, PAIRS - 1) as i:
                u_pair(i, DVE_B, False, DVE_B, False, True)
            split_turn(PAIRS - 1, 2, DVE_B, False)
            late_tile(PAIRS - 1, -1)
            split_turn(PAIRS - 1, 3, DVE_B, False)
            late_tile(PAIRS - 1, 0)
            late_tile(PAIRS - 1, 1)
            for q in range(4):
                split(Q_V, q)

            def split_w(n, t):
                dve.wait_ge(w_hi, (n // 4 + t + 1) if isinstance(n, int) else n // 4 + (t + 1))
                vec.tensor_tensor(whalf_lo[:, t % 2, :], wexp[:, bass.ds(n // 4 + t, 1), :].rearrange("p a t -> p (a t)"),
                                  whalf_hi[:, t % 2, :].bitcast(f32), ALU.subtract).then_inc(w_lo, 1)

            split_w(0, 0)
            with dve.Fori(0, NT // 2 - 1) as i:
                split_w(i * 8, 1)
                for q in range(4, 8):
                    split(i * 8 + Q_V, q)
                split_w(i * 8, 2)
                for q in range(4):
                    split(i * 8 + (Q_V + 8), q)
            n = NT * 4 - 8
            split_w(n, 1)
            for q in range(4, 8):
                split(n + Q_V, q)

            dve.wait_ge(split_free, Q_V + NT * 4 + SPLITS)
            dve.wait_ge(x1_in, 16)
            dve.wait_ge(ln2_in, 32)
            for b in range(TB):
                chain.step(vec.scalar_tensor_tensor(out=y_out[:, b, :], in0=x1_back[:, b, :], scalar=ALPHA,
                                                    in1=ps[:, 4 * b:4 * b + 4, :].rearrange("p n c -> p (n c)"),
                                                    op0=ALU.mult, op1=ALU.add))
                layer_norm(y_out, ln2w, ln2b, b, 2 * TB + b + 1).then_inc(y_ready, 1)

        @block.gpsimd
        def _(pool):
            chain = Chain(pool, g_chain)
            eng = nc.gpsimd
            eng.memset(stats[:, NHALF:NHALF + 32], -0.5).then_inc(halfexp, 1)

            pool.wait_ge(tab_in, 16)
            pool.wait_ge(acc_free, G_IN + 2)
            for b in range(TB):
                first_col = (3 * SBH + RTH) * HD
                xs = proj[:, b, first_col:first_col + RTH * HD].rearrange("p (h d) -> p h d", h=RTH)
                half = HD // 2
                eng.tensor_tensor(rot_g[:, 1, :, 0:half], xs[:, :, half:HD],
                                  sin_t[:, b:b + 1, 0:half].to_broadcast([P, RTH, half]), ALU.mult)
                eng.tensor_tensor(rot_g[:, 1, :, half:HD], xs[:, :, 0:half],
                                  sin_t[:, b:b + 1, half:HD].to_broadcast([P, RTH, half]), ALU.mult)
                chain.step(eng.tensor_tensor(rot_g[:, 0, :, :], xs, cos_t[:, b:b + 1, :].to_broadcast([P, RTH, HD]),
                                             ALU.mult))
                last = eng.tensor_tensor(xs, rot_g[:, 0, :, :], rot_g[:, 1, :, :], ALU.add)
                if b == 0:
                    chain.step(last)
                else:
                    last.then_inc(rot_k, 1)

            pool.wait_ge(halfexp, 1)
            for n in range(3 * TB):
                pool.wait_ge(var_ready, n + 1)
                o, w = (16 * n, 16) if n < TB else (0, 1)
                eng.tensor_tensor(stats[:, RSTD + o:RSTD + o + w], stats[:, VAR + o:VAR + o + w],
                                  stats[:, NHALF:NHALF + w], ALU.pow).then_inc(rstd_ready, 1)
                if n == 2 * TB - 1:
                    pool.wait_ge(x1_out, 16)
                    pool.wait_ge(sc_ready, 8)
                    top = 96
                    eng.memset(wexp[:, LATE:top, :], 1.0).then_inc(ones_ready, 1)
                    pool.wait_ge(topk_done, 1)
                    eng.memset(wexp[:, top:NT, :], 1.0).then_inc(ones_ready, 1)
                    pool.wait_ge(picks_ready, 1)

                    def distances(n, parity, wait):
                        if wait:
                            pool.wait_ge(gate_ready, n - 1)
                        eng.tensor_tensor(hot[:, parity, :, :, :],
                                          iota.unsqueeze(1).unsqueeze(1).to_broadcast([P, 2, 4, P]),
                                          picks_t[:, 0:2, bass.ds(n * 4, 4)].unsqueeze(3).to_broadcast([P, 2, 4, P]),
                                          ALU.subtract).then_inc(dist_ready, 1)

                    def weigh(n, parity):
                        pool.wait_ge(hot_ready, n + 1)
                        rows = hot[:, parity, 1, :, :]
                        eng.tensor_tensor(rows, rows, picks_t[:, 2, bass.ds(n * 4, 4)].unsqueeze(2)
                                          .to_broadcast([P, 4, P]), ALU.mult).then_inc(weighted, 1)

                    distances(0, 0, False)
                    distances(1, 1, False)
                    with pool.Fori(0, GATES // 2 - 1) as i:
                        for s in range(2):
                            weigh(i * 2 + s, s)
                            distances(i * 2 + (s + 2), s, True)
                    weigh(GATES - 2, 0)
                    weigh(GATES - 1, 1)


def constant_tables():
    inv = 10000.0 ** (-np.arange(0, HD, 2, dtype=np.float32) / HD)
    ang = np.arange(SEQ, dtype=np.float32)[:, None] * inv.astype(np.float32)[None, :]
    ang = np.concatenate([ang, ang], -1).astype(np.float32)
    cos, sin = np.cos(ang), np.sin(ang)
    sin[:, :HD // 2] *= -1
    by_block = lambda a: a.reshape(TB, P, HD).transpose(1, 0, 2).reshape(P, TB * HD)
    log_g = np.log1p(-(2.0 ** (-5.0 - np.arange(RTH, dtype=np.float64))))
    j, i = np.arange(P)[:, None], np.arange(SEQ)[None, :]
    seen = (i // CHUNK) >= (j // CHUNK)
    dist = np.abs(i - j)
    decay = np.where(seen[None], np.exp(log_g[:, None, None] * dist[None]), 0.0) * SCALE
    decay = np.concatenate([decay, decay[:, :, :P]], -1).transpose(1, 0, 2).reshape(P, RTH * 384)
    r, c = np.arange(P)[:, None], np.arange(P)[None, :]
    causal = np.concatenate([j < i, r < c], -1)
    cst = np.concatenate([by_block(cos), by_block(sin), decay, (r >= c), np.ones((P, P)), causal,
                          np.where(causal, 0.0, BIG)], -1).astype(np.float32)
    small = np.stack([np.eye(P), np.broadcast_to(np.arange(P), (P, P))], 1).astype(np.float32)
    return np.ascontiguousarray(cst), np.ascontiguousarray(small)


_INS = ["x", "w_in", "sb_norm_w", "ret_norm_w", "w_out", "ln1_w", "ln1_b", "w_pq", "sub_keys",
        "expert_u", "expert_v", "ln2_w", "ln2_b"]


def kernel(**inputs):
    import concourse.bacc as _bacc
    from concourse.bass_utils import run_bass_kernel_spmd as _run

    nc = _bacc.Bacc("TRN2", target_bir_lowering=False, num_devices=1)
    cst, small = constant_tables()
    arrays, args = {}, []
    named = [(n, np.ascontiguousarray(inputs[n])) for n in _INS] + [("tables", cst), ("small_tables", small)]
    for name, a in named:
        arrays[f"in_{name}"] = a
        args.append(nc.dram_tensor(f"in_{name}", a.shape, mybir.dt.from_np(a.dtype), kind="ExternalInput").ap())
    args.append(nc.dram_tensor("out_y", (1, SEQ, D), mybir.dt.float32, kind="ExternalOutput").ap())
    layer_kernel(nc, *args)
    r = _run(nc, [arrays], core_ids=[0])
    return r.results[0]["out_y"]
```

```python
from contextlib import ExitStack

import numpy as np

import concourse.bass as bass
from concourse import mybir

P = 128
SEQ, D = 256, 2048
TB = SEQ // P
KT = D // P
HD = 128
SBH, RTH = 8, 8
INW = 3 * SBH * HD + 4 * RTH * HD
CHUNK = 64
PH, PKEYS, TOPK = 8, 128, 16
SETS = 2 * PH
EXPERTS = PKEYS * PKEYS
NT = EXPERTS // P
COLS = 512
ALPHA = 2.0 ** 0.25
LN_EPS, NORM_EPS = 1e-5, 1e-6
SCALE = HD ** -0.5
BIG = 1e30
LOWEST = -3.4e38

G_IN, G_OUT, G_PQ = INW // COLS, D // COLS, D // COLS
Q_OUT = G_IN * KT
Q_PQ = Q_OUT + G_OUT * KT
Q_U = Q_PQ + G_PQ * KT
Q_V = Q_U + NT * 4
RAWS, SPLITS = 4, 4
PAIRS = NT // 2
PAIRS_A = 26
DVE_A, DVE_B = (3,), (0, 1, 2, 3)
SOFT = TB * PH
PICKS = PAIRS_A
GATE0 = PICKS + 2
TABLE_PIECES, PIECE = 4, 1152
SB_GROUP = 3 * SBH * HD // COLS
AT_TURN, AT_Z, AT_SUMS, AT_VALUES = 2, 4, 9, 13
GATES = SEQ // 4
LATE = 2 * PAIRS_A - 1
RT_FIRST = 5
HALF = KT // 2
ROWS = 4
DMA1, DMA4 = 16, 16 * ROWS
F_X, F_MIX, F_X1, F_Q = 0, 8, 16, 24


def layer_kernel(nc, x, w_in, sb_norm_w, ret_norm_w, w_out, ln1_w, ln1_b, w_pq, sub_keys,
                 expert_u, expert_v, ln2_w, ln2_b, tables, small_tables, out):
    f32, f32r, u32 = mybir.dt.float32, mybir.dt.float32r, mybir.dt.uint32
    ACT, ALU, AX = mybir.ActivationFunctionType, mybir.AluOpType, mybir.AxisListType
    ctx = ExitStack()
    with ctx:
        base = 16512

        def at(name, shape, dt, offset):
            return nc.alloc_sbuf_tensor_at(name, [P, *shape], dt, offset=offset)

        A_HI, A_LO = base, base + 16384
        RAW, SPL = base + 32768, base + 49152
        KEEP = base + 65536
        W0 = 98272
        act_hi = at("act_hi", [KT, SEQ], f32r, A_HI)
        act_lo = at("act_lo", [KT, SEQ], f32r, A_LO)
        raw = at("raw", [RAWS, 2, COLS], f32, RAW)
        split_hi = at("split_hi", [SPLITS, COLS], f32r, SPL)
        split_lo = at("split_lo", [SPLITS, COLS], f32r, SPL + 8192)
        small = at("small", [2, P], f32, KEEP)
        picks_t = at("picks_t", [3, SEQ], f32, KEEP + 1024)
        stats = at("stats", [256], f32, KEEP + 4096)
        moments = at("moments", [TB, RTH, 2], f32, W0 + 127616)
        soft_a = at("soft_a", [2, 384], f32, KEEP + 5120)
        pick_n = at("pick_n", [3, TB, P], f32, KEEP + 5120)
        hot = at("hot", [2, 2, 4, P], f32, KEEP + 5120)
        late = at("late", [2, SEQ], f32, KEEP + 13312)
        whalf_hi = at("whalf_hi", [2, SEQ], f32r, KEEP + 5120)
        whalf_lo = at("whalf_lo", [2, SEQ], f32r, KEEP + 7168)
        wexp = at("wexp", [NT, SEQ], f32, W0)
        proj = at("proj", [TB, INW], f32, W0)
        x_nat = at("x_nat", [TB, D], f32, W0 + 57344)
        mixed = at("mixed", [TB, D], f32, W0 + 73728)
        cst = at("cst", [4608], f32, W0 + 90112)
        norm_w = at("norm_w", [D], f32, W0 + 108544)
        qk_t = at("qk_t", [2, 2, SEQ], f32, W0 + 116736)
        z_sb = at("z_sb", [384], f32, W0 + 120832)
        soft_l = at("soft_l", [384], f32, W0 + 122368)
        soft_p = at("soft_p", [384], f32, W0 + 123904)
        stage = at("stage", [2, TB, HD], f32, W0 + 125440)
        scales = at("scales", [2], f32, W0 + 127488)
        bn_sb = at("bn_sb", [TB, SBH * 6], f32, W0 + 127744)
        moments_sb = at("moments_sb", [TB, SBH, 2], f32, W0 + 128128)
        ln_w = at("ln_w", [D], f32, W0)
        ln_b = at("ln_b", [D], f32, W0 + 8192)
        q_nat = at("q_nat", [TB, D], f32, W0 + 16384)
        q_t = at("q_t", [KT, SEQ], f32, W0 + 32768)
        keys_t = at("keys_t", [SETS, PKEYS], f32, W0 + 49152)
        keys_nat = at("keys_nat", [SETS, HD], f32, W0 + 90112)
        scores = at("scores", [TB, SETS, PKEYS], f32, W0 + 98304)
        T0 = W0 + 114688
        idx_u = at("idx_u", [TB * PH, 2, TOPK], u32, T0)
        idx_f = at("idx_f", [TB * PH, 2, TOPK], f32, T0 + 2048)
        best = at("best", [TB * PH, TOPK], f32, T0 + 4096)
        pos_u = at("pos_u", [TB * PH, TOPK], u32, T0 + 5120)
        pos_f = at("pos_f", [2, TB * PH, TOPK], f32, T0 + 6144)
        pos_i = at("pos_i", [2, TB * PH, TOPK], u32, T0 + 8192)
        cand = at("cand", [TOPK, TOPK], f32, T0 + 10240)
        top_v = at("top_v", [2, TOPK], f32, T0 + 11264)
        rest = at("rest", [256], f32, T0 + 11392)
        onehot = at("onehot", [2 * TOPK, TOPK], f32, T0 + 12416)
        gsum = at("gsum", [2, TB * PH], f32, T0 + 14464)
        head_s = at("head_s", [2, PKEYS], f32, T0 + 14592)
        head_i = at("head_i", [2, TOPK], u32, T0 + 15616)
        head_b = at("head_b", [TOPK], f32, T0 + 15744)
        head_p = at("head_p", [TOPK], u32, T0 + 15808)
        ln2w = at("ln2w", [D], f32, A_HI)
        ln2b = at("ln2b", [D], f32, A_HI + 8192)
        x1_back = at("x1_back", [TB, D], f32, A_LO)
        y_out = at("y_out", [TB, D], f32, W0)

        ps = ctx.enter_context(nc.psum_tensor("ps", [P, 8, COLS], f32))
        x1_dram = nc.dram_tensor("x1_dram", (P, TB, D), f32, kind="Internal").ap()

        ident, iota = small[:, 0, :], small[:, 1, :]
        cos_t = cst[:, 0:256].rearrange("p (b d) -> p b d", b=TB)
        sin_t = cst[:, 256:512].rearrange("p (b d) -> p b d", b=TB)
        decay = cst[:, 512:3584].rearrange("p (h q) -> p h q", h=RTH)
        tri = cst[:, 3584:3712]
        ones = cst[:, 3712:3840]
        causal = cst[:, 3840:4224]
        masked = cst[:, 4224:4608]

        def sem(name):
            return ctx.enter_context(nc.semaphore(name))

        raw_ready = [sem(f"raw_ready{i}") for i in range(RAWS)]
        hi_ready = sem("hi_ready")
        lo_ready = sem("lo_ready")
        split_free = sem("split_free")
        acc_free = sem("acc_free")
        turned = sem("turned")
        turn_hi = sem("turn_hi")
        turn_done = sem("turn_done")
        pe_turned = sem("pe_turned")
        dve_turned = sem("dve_turned")
        score_free = sem("score_free")
        x_in = [sem(f"x_in{i}") for i in range(4)]
        small_in, tab_in, keys_in, ln1_in, ln2_in = (sem(n) for n in ("small_in", "tab_in", "keys_in", "ln1_in", "ln2_in"))
        norms_in, x1_out, x1_in, y_stored = (sem(n) for n in ("norms_in", "x1_out", "x1_in", "y_stored"))
        rot_ready = sem("rot_ready")
        scales_ready, staged, qk_out = sem("scales_ready"), sem("staged"), sem("qk_out")
        soft_abs, soft_exp, soft_max, gate_weighted = (
            sem(n) for n in ("soft_abs", "soft_exp", "soft_max", "gate_weighted"))
        keys_turned, keys_out = sem("keys_turned"), sem("keys_out")
        qk_turned, q_out, k_out = sem("qk_turned"), sem("q_out"), sem("k_out")
        z_ready, c_ready, o_ready, o_out = sem("z_ready"), sem("c_ready"), sem("o_ready"), sem("o_out")
        z_masked, soft_ready, spm_ready, la_ready, a_ready = (
            sem(n) for n in ("z_masked", "soft_ready", "spm_ready", "la_ready", "a_ready"))
        gated = sem("gated")
        sb_ready, mixed_ready = sem("sb_ready"), sem("mixed_ready")
        x1_ready = sem("x1_ready")
        var_ready, rstd_ready = sem("var_ready"), sem("rstd_ready")
        sc_ready, sc_out = sem("sc_ready"), sem("sc_out")
        best_ready, exp_ready, topk_done = sem("best_ready"), sem("exp_ready"), sem("topk_done")
        picks_turned, picks_ready = sem("picks_turned"), sem("picks_ready")
        dist_ready, hot_ready, weighted, gate_ready, gates_free = (
            sem(n) for n in ("dist_ready", "hot_ready", "weighted", "gate_ready", "gates_free"))
        ones_ready, late_used = sem("ones_ready"), sem("late_used")
        abs_ready, carried = sem("abs_ready"), sem("carried")
        w_hi, w_lo = sem("w_hi"), sem("w_lo")
        halfexp = sem("halfexp")
        sb_bn_ready = sem("sb_bn_ready")
        bn_ready = sem("bn_ready")
        values_ready = sem("values_ready")
        y_ready = sem("y_ready")
        v_chain, a_chain, g_chain = sem("v_chain"), sem("a_chain"), sem("g_chain")

        MEAN, VAR, RSTD, NHALF, SUMS, BN = 0, 16, 48, 80, 112, 160

        class Chain:

            def __init__(self, eng, s):
                self.eng, self.sem, self.n = eng, s, 0

            def step(self, instruction):
                self.n += 1
                instruction.then_inc(self.sem, 1)
                self.eng.wait_ge(self.sem, self.n)

            def add(self, instruction):
                self.n += 1
                instruction.then_inc(self.sem, 1)

        w_in_v = w_in.rearrange("l (k p) n -> (l p) k n", p=P)
        w_out_v = w_out.rearrange("l (k p) n -> (l p) k n", p=P)
        w_pq_v = w_pq.rearrange("l (h m c) n -> (l h) m c n", h=2, c=8)
        u_pe = expert_u.rearrange("l e d -> (l e) d")
        u_dve = expert_u.rearrange("l (g i) (h r d) -> (l h) r i g d", i=32, h=2, r=ROWS)
        v_v = expert_v.rearrange("l e d -> (l e) d")

        def x_piece(ap, n):
            return ap[:, n // 2, n % 2 * 1024:n % 2 * 1024 + 1024]

        def before(pair, a, b, part_a):
            return pair * a if part_a else pair * b + PAIRS_A * (a - b)

        def u_raw(slot, pair, part_a):
            a, b = (DMA4 if slot in s else DMA1 for s in (DVE_A, DVE_B))
            return before(pair, a, b, part_a) + (U_RAW + (a if part_a else b))

        def turned_at(half, pair, part_a):
            own = DVE_A if part_a else DVE_B
            if half in own:
                v = before(pair, len(DVE_A), len(DVE_B), part_a) + (own.index(half) + 1)
                return dve_turned, v, v
            v = before(pair, 8 - 2 * len(DVE_A), 8 - 2 * len(DVE_B), part_a)
            n = 2 * [h for h in range(4) if h not in own].index(half)
            return pe_turned, v + (n + 1), v + (n + 2)

        U_RAW = Q_U // 8 * DMA1
        V_RAW = [U_RAW + PAIRS_A * (DMA4 if k in DVE_A else DMA1)
                 + (PAIRS - PAIRS_A) * (DMA4 if k in DVE_B else DMA1) for k in range(RAWS)]
        block = ctx.enter_context(nc.Block())

        @block.sync
        def _(sp):
            def dense(view, first_q, g, wait):
                for kk in range(KT // 2):
                    if wait or kk >= RAWS:
                        sp.wait_ge(lo_ready, g * KT + first_q + 2 * kk + 2 - 2 * RAWS)
                    sp.dma_start(raw[:, kk % RAWS, :, :], view[:, 2 * kk:2 * kk + 2, bass.ds(g * COLS, COLS)]
                                 ).then_inc(raw_ready[kk % RAWS], 16)

            def out_pair(pair):
                for n in range(4 * HALF // 2):
                    kind, g, k = n // HALF, n % HALF // (HALF // 2), n % (HALF // 2)
                    sp.wait_ge(lo_ready, Q_OUT + pair * 4 * HALF + 2 * n + 2 - 2 * RAWS)
                    sp.dma_start(raw[:, n % RAWS, :, :],
                                 w_out_v[:, kind * HALF + 2 * k:kind * HALF + 2 * k + 2,
                                         (2 * pair + g) * COLS:(2 * pair + g + 1) * COLS]
                                 ).then_inc(raw_ready[n % RAWS], 16)

            def by_rows(g, wait):
                for kk in range(KT // 2):
                    if wait or kk >= RAWS:
                        sp.wait_ge(lo_ready, g * KT + Q_PQ + 2 * kk + 2 - 2 * RAWS)
                    c = 2 * kk % 8
                    sp.dma_start(raw[:, kk % RAWS, :, :], w_pq_v[kk // 4, :, c:c + 2, bass.ds(g * COLS, COLS)]
                                 ).then_inc(raw_ready[kk % RAWS], 16)

            def u_half(i, k, own):
                j = i * 2 + k // 2
                if k in own:
                    for r in range(ROWS):
                        sp.dma_start(raw[32 * r:32 * r + 32, k, :, :].rearrange("p a (b d) -> p (a b) d", b=2),
                                     u_dve[k % 2, r, :, bass.ds(j * 4, 4), :]).then_inc(raw_ready[k], 16)
                else:
                    sp.dma_start(raw[:, k, :, :].rearrange("p a b -> p (a b)"),
                                 u_pe[bass.ds(j * P, P), k % 2 * 1024:k % 2 * 1024 + 1024]).then_inc(raw_ready[k], 16)

            def u_pair(i, own, part_a):
                for k in range(RAWS):
                    s, _, v = turned_at(k, i - 1, part_a)
                    sp.wait_ge(s, v)
                    u_half(i, k, own)

            def v_half(j, hf, slot):
                sp.dma_start(raw[:, slot, :, :].rearrange("p a b -> p (a b)"),
                             v_v[bass.ds(j * P, P), hf * 1024:hf * 1024 + 1024]).then_inc(raw_ready[slot], 16)

            sp.dma_start(small[:, :, :], small_tables).then_inc(small_in, 16)
            for n in range(4):
                sp.dma_start(x_piece(x_nat, n), x_piece(x.rearrange("a (b p) d -> (a p) b d", p=P), n)
                             ).then_inc(x_in[n], 16)
            dense(w_in_v, 0, 0, False)
            with sp.Fori(1, TABLE_PIECES + 1) as g:
                dense(w_in_v, 0, g, True)
                piece = bass.ds(g * PIECE - PIECE, PIECE)
                sp.dma_start(cst[:, piece], tables[:, piece]).then_inc(tab_in, 16)
            sp.dma_start(norm_w[:, 0:SBH * HD], sb_norm_w.partition_broadcast(P)).then_inc(norms_in, 16)
            sp.dma_start(norm_w[:, SBH * HD:D], ret_norm_w.partition_broadcast(P)).then_inc(norms_in, 16)
            with sp.Fori(TABLE_PIECES + 1, G_IN) as g:
                dense(w_in_v, 0, g, True)
            out_pair(0)
            sp.wait_ge(mixed_ready, TB)
            sp.dma_start(keys_nat[:, :, :], sub_keys.rearrange("l h c k d -> k (l h c) d")).then_inc(keys_in, 16)
            sp.dma_start(ln_w[:, :], ln1_w.partition_broadcast(P)).then_inc(ln1_in, 16)
            sp.dma_start(ln_b[:, :], ln1_b.partition_broadcast(P)).then_inc(ln1_in, 16)
            out_pair(1)
            by_rows(0, True)
            sp.wait_ge(x1_ready, TB)
            sp.dma_start(x1_dram, x_nat[:, :, :]).then_inc(x1_out, 16)
            with sp.Fori(1, G_PQ) as g:
                by_rows(g, True)
            for k in range(RAWS):
                sp.wait_ge(lo_ready, Q_U - 2 * RAWS + 2 * k + 2)
                u_half(0, k, DVE_A)
            with sp.Fori(1, PAIRS_A) as i:
                u_pair(i, DVE_A, True)
            u_pair(PAIRS_A, DVE_B, True)
            with sp.Fori(PAIRS_A + 1, PAIRS) as i:
                u_pair(i, DVE_B, False)
            for k in range(RAWS):
                s, _, v = turned_at(k, PAIRS - 1, False)
                sp.wait_ge(s, v)
                v_half(k // 2, k % 2, k)

            def v_pairs(first, end):
                with sp.Fori(first, end) as i:
                    for n in range(RAWS):
                        sp.wait_ge(lo_ready, i * 8 + (Q_V + 2 * n + 2 - 2 * RAWS))
                        v_half(i * 2 + n // 2, n % 2, n)

            v_pairs(1, 3)
            sp.wait_ge(split_free, Q_V + SPLITS)
            sp.dma_start(ln2w[:, :], ln2_w.partition_broadcast(P)).then_inc(ln2_in, 16)
            v_pairs(3, 5)
            sp.dma_start(ln2b[:, :], ln2_b.partition_broadcast(P)).then_inc(ln2_in, 16)
            sp.wait_ge(x1_out, 16)
            for b in range(TB):
                v_pairs(5 + 2 * b, 7 + 2 * b)
                sp.dma_start(x1_back[:, b, :], x1_dram[:, b, :]).then_inc(x1_in, 16)
            v_pairs(5 + 2 * TB, PAIRS)
            for n in range(4):
                sp.wait_ge(y_ready, n + 1)
                sp.dma_start(x_piece(out.rearrange("a (b p) d -> (a p) b d", p=P), n), x_piece(y_out, n)
                             ).then_inc(y_stored, 16)
            sp.wait_ge(y_stored, 16 * 4)

        @block.tensor
        def _(pe):
            pe.sem_inc(split_free, SPLITS)

            def turn(fill, sources):
                if fill >= 4:
                    pe.wait_ge(turn_done, fill - 3)
                for i, s in enumerate(sources):
                    last = nc.tensor.transpose(ps[:, 4 + fill % 4, i * P:(i + 1) * P], s, ident)
                last.then_inc(turned, 1)

            def three(acc, l_hi, l_lo, r_hi, r_lo, first, last):
                nc.tensor.matmul(acc, l_hi, r_hi, start=first, stop=False)
                nc.tensor.matmul(acc, l_hi, r_lo, start=False, stop=False)
                return nc.tensor.matmul(acc, l_lo, r_hi, start=False, stop=last)

            def dense(g, parity, after=None):
                pe.wait_ge(acc_free, g + 1)
                for k in range(KT):
                    pe.wait_ge(lo_ready, g * KT + (k + 1))
                    for b in range(TB):
                        c = slice(b * P, (b + 1) * P)
                        last = three(ps[:, 2 * parity + b, :], act_hi[:, k, c], act_lo[:, k, c],
                                     split_hi[:, k % SPLITS, :], split_lo[:, k % SPLITS, :], k == 0, k == KT - 1)
                    last.then_inc(split_free, 1)
                    if after:
                        after(k)

            pe.wait_ge(small_in, 16)
            for f in range(8):
                if f % 2 == 0:
                    pe.wait_ge(x_in[f // 2], 16)
                turn(F_X + f, [x_nat[:, f // 4, (f % 4 * 4 + i) * P:(f % 4 * 4 + i + 1) * P] for i in range(4)])
            pe.wait_ge(turn_done, F_X + 8)
            with pe.Fori(0, SB_GROUP // 2) as i:
                for s in range(2):
                    dense(i * 2 + s, s)

            def sb_head(it):
                def after(k):
                    if k == AT_TURN:
                        pe.wait_ge(staged, it + 1)
                        pe.wait_ge(qk_out, it)
                        for n in range(4):
                            last = nc.tensor.transpose(ps[:, 4, n * P:(n + 1) * P], stage[:, n // 2, n % 2, :], ident)
                        last.then_inc(qk_turned, 1)
                    if k == AT_Z:
                        pe.wait_ge(qk_out, it + 1)
                        pe.wait_ge(z_masked, it)
                        nc.tensor.matmul(ps[:, 5, 0:256], qk_t[:, 0, 1, 0:P], qk_t[:, 0, 0, :], start=True, stop=True)
                        nc.tensor.matmul(ps[:, 5, 256:384], qk_t[:, 0, 1, P:SEQ], qk_t[:, 0, 0, P:SEQ],
                                         start=True, stop=True).then_inc(z_ready, 1)
                    if k == AT_SUMS:
                        pe.wait_ge(spm_ready, it + 1)
                        pe.wait_ge(la_ready, it)
                        nc.tensor.matmul(ps[:, 6, 0:256], tri, soft_p[:, 0:256], start=True, stop=False)
                        nc.tensor.matmul(ps[:, 6, P:256], ones, soft_p[:, 256:384], start=False, stop=True)
                        nc.tensor.matmul(ps[:, 6, 256:384], tri, soft_p[:, 256:384], start=True, stop=True
                                         ).then_inc(c_ready, 1)
                    if k == AT_VALUES:
                        pe.wait_ge(a_ready, it + 1)
                        pe.wait_ge(o_out, it)
                        v = bass.ds(it * HD + 2 * SBH * HD, HD)
                        nc.tensor.matmul(ps[:, 7, 0:P], soft_a[:, 0, 0:P], proj[:, 0, v], start=True, stop=True)
                        nc.tensor.matmul(ps[:, 7, P:256], soft_a[:, 0, P:256], proj[:, 0, v], start=True, stop=False)
                        nc.tensor.matmul(ps[:, 7, P:256], soft_a[:, 0, 256:384], proj[:, 1, v], start=False, stop=True
                                         ).then_inc(o_ready, 1)
                return after

            pe.wait_ge(tab_in, 16 * TABLE_PIECES)
            with pe.Fori(SB_GROUP // 2, G_IN // 2) as i:
                for s in range(2):
                    dense(i * 2 + s, s, sb_head(i * 2 + (s - SB_GROUP)))

            pe.wait_ge(acc_free, G_IN + 2)
            pe.wait_ge(rot_ready, 2 * TB)

            def rt_cols(it, kind):
                first = (3 * SBH + kind * RTH + it) * HD
                return slice(first, first + HD)

            def banks(it):
                return (it % 2 * 4, it % 2 * 4 + 1, it % 2 * 4 + 3) if it < RT_FIRST else (4, 5, 7)

            def free_at(it):
                return max(it - 1, 0) if it < RT_FIRST else it

            def turn_qk(it):
                pe.wait_ge(qk_out, SBH)
                pe.wait_ge(q_out, free_at(it))
                pe.wait_ge(k_out, free_at(it))
                for n in range(4):
                    last = nc.tensor.transpose(ps[:, banks(it)[0], n * P:(n + 1) * P],
                                               proj[:, n % 2, rt_cols(it, n // 2)], ident)
                last.then_inc(qk_turned, 1)

            def z_product(it):
                bank, p = banks(it)[1], it % 2
                pe.wait_ge(q_out, it + 1)
                pe.wait_ge(k_out, it + 1)
                pe.wait_ge(z_masked, SBH)
                pe.wait_ge(a_ready, SBH + free_at(it))
                nc.tensor.matmul(ps[:, bank, 0:256], qk_t[:, p, 1, 0:P], qk_t[:, p, 0, :], start=True, stop=True)
                nc.tensor.matmul(ps[:, bank, 256:384], qk_t[:, p, 1, P:SEQ], qk_t[:, p, 0, P:SEQ],
                                 start=True, stop=True).then_inc(z_ready, 1)

            def values(it):
                bank, p = banks(it)[2], it % 2
                pe.wait_ge(a_ready, SBH + it + 1)
                pe.wait_ge(o_out, SBH + free_at(it))
                v = rt_cols(it, 2)
                nc.tensor.matmul(ps[:, bank, 0:P], soft_a[:, p, 0:P], proj[:, 0, v], start=True, stop=True)
                nc.tensor.matmul(ps[:, bank, P:256], soft_a[:, p, P:256], proj[:, 0, v], start=True, stop=False)
                nc.tensor.matmul(ps[:, bank, P:256], soft_a[:, p, 256:384], proj[:, 1, v], start=False, stop=True
                                 ).then_inc(o_ready, 1)

            for s in range(RT_FIRST + 2):
                if s < RT_FIRST:
                    turn_qk(s)
                if 0 <= s - 1 < RT_FIRST:
                    z_product(s - 1)
                if 0 <= s - 2 < RT_FIRST:
                    values(s - 2)

            def turn_mixed(kind):
                for f in range(4):
                    b, col = f // 2, (kind * HALF + f % 2 * 4) * P
                    pe.wait_ge(sb_ready, b + 1) if kind == 0 else pe.wait_ge(mixed_ready, b + 1)
                    turn(F_MIX + 4 * kind + f, [mixed[:, b, col + i * P:col + (i + 1) * P] for i in range(4)])
                pe.wait_ge(turn_done, F_MIX + 4 * kind + 4)

            def out_half(pair, kind, after=None):
                for s in range(2):
                    if kind == 0:
                        pe.wait_ge(acc_free, G_IN + 2 * pair + s + 1)
                    for kk in range(HALF):
                        k, n = kind * HALF + kk, s * HALF + kk
                        pe.wait_ge(lo_ready, Q_OUT + (2 * pair + kind) * 2 * HALF + n + 1)
                        for b in range(TB):
                            c = slice(b * P, (b + 1) * P)
                            last = three(ps[:, 2 * s + b, :], act_hi[:, k, c], act_lo[:, k, c],
                                         split_hi[:, n % SPLITS, :], split_lo[:, n % SPLITS, :], k == 0, k == KT - 1)
                        last.then_inc(split_free, 1)
                        if after:
                            after(n)

            def last_heads(n):
                it = RT_FIRST + n
                if RT_FIRST <= it - 2 < RTH:
                    values(it - 2)
                if RT_FIRST <= it - 1 < RTH:
                    z_product(it - 1)
                if it < RTH:
                    turn_qk(it)

            pe.wait_ge(q_out, RT_FIRST)
            pe.wait_ge(k_out, RT_FIRST)
            pe.wait_ge(a_ready, SBH + RT_FIRST)
            pe.wait_ge(o_out, SBH + RT_FIRST)
            turn_mixed(0)
            out_half(0, 0, last_heads)
            turn_mixed(1)
            out_half(0, 1)
            for kind in range(2):
                out_half(1, kind)

            pe.wait_ge(keys_in, 16)
            for f in range(4):
                for i in range(4):
                    last = nc.tensor.transpose(ps[:, 4 + f, i * P:(i + 1) * P], keys_nat[:, 4 * f + i, :], ident)
                last.then_inc(keys_turned, 1)
            pe.wait_ge(keys_out, 4)
            for f in range(8):
                if f % 4 == 0:
                    pe.wait_ge(x1_ready, f // 4 + 1)
                dims = x_nat[:, f // 4, :].rearrange("p (h m c) -> p h c m", h=2, c=8)
                turn(F_X1 + f, [dims[:, f % 4 // 2, f % 2 * 4 + i, :] for i in range(4)])
            pe.wait_ge(turn_done, F_X1 + 8)
            with pe.Fori(0, G_PQ // 2) as i:
                for s in range(2):
                    dense(i * 2 + (G_IN + G_OUT + s), s)
            pe.wait_ge(acc_free, G_IN + G_OUT + G_PQ + 2)
            for f in range(8):
                turn(F_Q + f, [q_nat[:, f // 4, (f % 4 * 4 + i) * P:(f % 4 * 4 + i + 1) * P] for i in range(4)])
            pe.wait_ge(turn_done, F_Q + 8)
            for f in range(8):
                if f >= 2:
                    pe.wait_ge(sc_out, f - 1)
                for i in range(4):
                    s, b = f % 4 * 4 + i, f // 4
                    last = nc.tensor.matmul(ps[:, 2 + f % 2, i * P:(i + 1) * P], q_t[:, s, b * P:(b + 1) * P],
                                            keys_t[:, s, :], start=True, stop=True)
                last.then_inc(sc_ready, 1)

            def turn_u(pair, q, own, part_a):
                k = q // 2
                if k in own:
                    return
                if q % 2 == 0:
                    pe.wait_ge(raw_ready[k], u_raw(k, pair, part_a))
                blocks = raw[:, k, :, :].rearrange("p a (m c) -> p c (a m)", c=8)
                for i in range(4):
                    last = nc.tensor.transpose(ps[:, 4 + q % 4, i * P:(i + 1) * P], blocks[:, q % 2 * 4 + i, :],
                                               ident)
                last.then_inc(pe_turned, 1)

            LEAD = 3

            def score_pair(pair, own, part_a, nxt=None, next_a=False, after=None):
                for q in range(8):
                    if q % 4 == 0:
                        pe.wait_ge(score_free, pair * 2 + (q // 4 + 1))
                    if q + LEAD < 8:
                        turn_u(pair, q + LEAD, own, part_a)
                    elif nxt is not None:
                        turn_u(pair + 1, q + LEAD - 8, nxt, next_a)
                    pe.wait_ge(lo_ready, pair * 8 + (Q_U + q + 1))
                    for i in range(4):
                        last = three(ps[:, q // 4, 0:SEQ], split_hi[:, q % SPLITS, i * P:(i + 1) * P],
                                     split_lo[:, q % SPLITS, i * P:(i + 1) * P], act_hi[:, q % 4 * 4 + i, :],
                                     act_lo[:, q % 4 * 4 + i, :], q % 4 == 0 and i == 0, q % 4 == 3 and i == 3)
                    last.then_inc(split_free, 1)
                    if after:
                        after(q)

            def picks_after(q):
                if q == 5:
                    pe.wait_ge(topk_done, 1)
                    for a, bank, col in ((0, 2, 0), (1, 3, 0), (2, 2, SEQ)):
                        for b in range(TB):
                            last = nc.tensor.transpose(ps[:, bank, col + b * P:col + (b + 1) * P],
                                                       pick_n[:, a, b, :], ident)
                    last.then_inc(picks_turned, 1)

            def gates_after(n0):
                def after(q):
                    if q % 4 == 1:
                        n, parity = n0 + q // 4, q // 4
                        pe.wait_ge(weighted, n + 1)
                        pe.wait_ge(gates_free, n + 1)
                        for i in range(4):
                            last = nc.tensor.matmul(ps[:, 2 + parity, i * P:(i + 1) * P], hot[:, parity, 1, i, :],
                                                    hot[:, parity, 0, i, :], start=True, stop=True)
                        last.then_inc(gate_ready, 1)
                return after

            for q in range(LEAD):
                turn_u(0, q, DVE_A, True)
            with pe.Fori(0, PAIRS_A - 1) as i:
                score_pair(i, DVE_A, True, DVE_A, True)
            score_pair(PAIRS_A - 1, DVE_A, True, DVE_B, False)
            score_pair(PICKS, DVE_B, False, DVE_B, False, picks_after)
            score_pair(PICKS + 1, DVE_B, False, DVE_B, False)
            with pe.Fori(GATE0, GATE0 + GATES // 2) as i:
                score_pair(i, DVE_B, False, DVE_B, False, gates_after(i * 2 - 2 * GATE0))
            with pe.Fori(GATE0 + GATES // 2, PAIRS - 1) as i:
                score_pair(i, DVE_B, False, DVE_B, False)
            score_pair(PAIRS - 1, DVE_B, False)

            def value_tile(n0, t, first, last_tile):
                pe.wait_ge(w_lo, (n0 // 4 + t + 1) if isinstance(n0, int) else n0 // 4 + (t + 1))
                for q in range(4 * t, 4 * t + 4):
                    if first and q < 2:
                        pe.wait_ge(score_free, NT + q + 1)
                    pe.wait_ge(lo_ready, n0 + (Q_V + q + 1))
                    for b in range(TB):
                        c = slice(b * P, (b + 1) * P)
                        last = three(ps[:, b * 4 + q % 4, :], whalf_hi[:, t, c], whalf_lo[:, t, c],
                                     split_hi[:, q % SPLITS, :], split_lo[:, q % SPLITS, :], first, last_tile)
                    last.then_inc(split_free, 1)

            def value_pair(n0, first):
                for t in range(2):
                    value_tile(n0, t, first and t == 0, False)

            pe.wait_ge(gates_free, GATES + 2)
            value_pair(0, True)
            with pe.Fori(1, NT // 2 - 1) as i:
                value_pair(i * 8, False)
            value_tile(NT * 4 - 8, 0, False, False)
            pe.wait_ge(w_lo, NT)
            pe.wait_ge(lo_ready, Q_V + NT * 4)
            for b in range(TB):
                c = slice(b * P, (b + 1) * P)
                for q in range(4):
                    last = three(ps[:, b * 4 + q, :], whalf_hi[:, 1, c], whalf_lo[:, 1, c], split_hi[:, q, :],
                                 split_lo[:, q, :], False, True)
                last.then_inc(values_ready, 1)

        @block.scalar
        def _(act):
            chain = Chain(act, a_chain)
            act.sem_inc(acc_free, 2)
            act.sem_inc(score_free, 2)

            def split(n, q, values=False):
                if q % 2 == 0:
                    start = (V_RAW[q // 2] - Q_V * DMA1 // 8) if values else 0
                    act.wait_ge(raw_ready[q // 2], n * (DMA1 // 8) + (start + DMA1))
                act.wait_ge(split_free, n + (q + 1))
                nc.scalar.activation(split_hi[:, q % SPLITS, :], raw[:, q // 2, q % 2, :], ACT.Copy
                                     ).then_inc(hi_ready, 1)

            def dense_group(g, parity, evacuate, after=None):
                for q in range(4, 20):
                    split(g * KT + q // 8 * 8, q % 8)
                    if after:
                        after(q)
                if evacuate:
                    evacuate(g, parity)

            def mixed_hi(kind):
                for f in range(4):
                    act.wait_ge(turned, F_MIX + 4 * kind + f + 1)
                    k = kind * HALF + f % 2 * 4
                    nc.scalar.activation(act_hi[:, k:k + 4, f // 2 * P:(f // 2 + 1) * P],
                                         ps[:, 4 + f, :].rearrange("p (k t) -> p k t", k=4), ACT.Copy
                                         ).then_inc(turn_hi, 1)

            def turned_hi(first):
                for f in range(first, first + 8):
                    act.wait_ge(turned, f + 1)
                    fb, k = (f - first) // 4, (f - first) % 4 * 4
                    nc.scalar.activation(act_hi[:, k:k + 4, fb * P:(fb + 1) * P],
                                         ps[:, 4 + f % 4, :].rearrange("p (k t) -> p k t", k=4), ACT.Copy
                                         ).then_inc(turn_hi, 1)

            turned_hi(F_X)
            for q in range(4):
                split(0, q)

            def to_proj(g, parity):
                act.wait_ge(split_free, g * KT + (KT + SPLITS))
                nc.scalar.activation(proj[:, :, bass.ds(g * COLS, COLS)], ps[:, 2 * parity:2 * parity + 2, :],
                                     ACT.Copy).then_inc(acc_free, 1)

            with act.Fori(0, SB_GROUP // 2) as i:
                for s in range(2):
                    dense_group(i * 2 + s, s, to_proj)

            def sb_head(it):
                def after(q):
                    if q == AT_TURN + 4:
                        act.wait_ge(qk_turned, it + 1)
                        act.wait_ge(z_ready, it)
                        nc.scalar.activation(qk_t[:, 0, :, :].rearrange("p a t -> p (a t)"), ps[:, 4, :], ACT.Copy
                                             ).then_inc(qk_out, 1)
                    if q == AT_Z + 4:
                        act.wait_ge(z_ready, it + 1)
                        act.wait_ge(spm_ready, it)
                        nc.scalar.activation(soft_l[:, :], ps[:, 5, 0:384], ACT.Abs).then_inc(soft_abs, 1)
                    if q == AT_Z + 5:
                        act.wait_ge(soft_abs, it + 1)
                        nc.scalar.activation(soft_l[:, :], soft_l[:, :], ACT.Exp, scale=-1.0).then_inc(soft_exp, 1)
                    if q == AT_Z + 6:
                        act.wait_ge(soft_exp, it + 1)
                        nc.scalar.activation(soft_l[:, :], soft_l[:, :], ACT.Ln, bias=1.0).then_inc(soft_ready, 1)
                    if q == AT_SUMS + 5:
                        act.wait_ge(la_ready, it + 1)
                        act.wait_ge(o_ready, it)
                        nc.scalar.activation(soft_a[:, 0, :], soft_p[:, :], ACT.Exp).then_inc(a_ready, 1)
                    if q == AT_VALUES + 4:
                        act.wait_ge(o_ready, it + 1)
                        nc.scalar.activation(mixed[:, :, bass.ds(it * HD, HD)],
                                             ps[:, 7, 0:256].rearrange("p (b d) -> p b d", b=TB), ACT.Copy
                                             ).then_inc(o_out, 1)
                return after

            nc.scalar.preload_act_table_set("natural_log_exp_and_others")
            with act.Fori(SB_GROUP // 2, G_IN // 2) as i:
                for s in range(2):
                    dense_group(i * 2 + s, s, to_proj, sb_head(i * 2 + (s - SB_GROUP)))

            act.wait_ge(acc_free, G_IN + 2)

            def queries_out(it):
                act.wait_ge(qk_turned, SBH + it + 1)
                act.wait_ge(z_ready, max(SBH, SBH + it - 1))
                bank = it % 2 * 4 if it < RT_FIRST else 4
                nc.scalar.activation(qk_t[:, it % 2, 0, :], ps[:, bank, 0:256], ACT.Copy).then_inc(q_out, 1)

            def result_out(it):
                act.wait_ge(o_ready, SBH + it + 1)
                bank = it % 2 * 4 + 3 if it < RT_FIRST else 7
                nc.scalar.activation(mixed[:, :, (SBH + it) * HD:(SBH + it + 1) * HD],
                                     ps[:, bank, 0:256].rearrange("p (b d) -> p b d", b=TB), ACT.Copy
                                     ).then_inc(o_out, 1)

            gate_cols = slice(INW - RTH * HD, INW)
            for s in range(RT_FIRST + 2):
                if s < RT_FIRST:
                    queries_out(s)
                if s == 1:
                    nc.scalar.activation(proj[:, :, gate_cols], proj[:, :, gate_cols], ACT.Silu).then_inc(gated, 1)
                if 0 <= s - 2 < RT_FIRST:
                    result_out(s - 2)

            mixed_hi(0)
            for n in range(4, 20):
                split(Q_OUT + n // 8 * 8, n % 8)
                it = RT_FIRST + n - 4
                if it < RTH:
                    queries_out(it)
                if RT_FIRST <= it - 2 < RTH:
                    result_out(it - 2)
            mixed_hi(1)
            for n in range(20, G_OUT * KT + 4):
                split(Q_OUT + n // 8 * 8, n % 8)

            for f in range(4):
                act.wait_ge(keys_turned, f + 1)
                nc.scalar.activation(keys_t[:, 4 * f:4 * f + 4, :].rearrange("p s k -> p (s k)"), ps[:, 4 + f, :],
                                     ACT.Copy).then_inc(keys_out, 1)
            turned_hi(F_X1)

            def to_q(g, parity):
                n = g - G_IN - G_OUT
                act.wait_ge(split_free, g * KT + KT + SPLITS)
                nc.scalar.activation(q_nat[:, :, n * COLS:(n + 1) * COLS], ps[:, 2 * parity:2 * parity + 2, :],
                                     ACT.Copy).then_inc(acc_free, 1)

            for g in range(G_IN + G_OUT, G_IN + G_OUT + G_PQ - 1):
                dense_group(g, g % 2, to_q)
            g = G_IN + G_OUT + G_PQ - 1
            for q in range(4, 16):
                split(g * KT + q // 8 * 8, q % 8)
            to_q(g, g % 2)
            for f in range(8):
                act.wait_ge(sc_ready, f + 1)
                nc.scalar.activation(scores[:, f // 4, f % 4 * 4:f % 4 * 4 + 4, :].rearrange("p s k -> p (s k)"),
                                     ps[:, 2 + f % 2, :], ACT.Copy).then_inc(sc_out, 1)

            def split_u(pair, q, part_a):
                semaphore, first, second = turned_at(q // 2, pair, part_a)
                act.wait_ge(semaphore, second if q % 2 else first)
                act.wait_ge(split_free, pair * 8 + (Q_U + q + 1))
                nc.scalar.activation(split_hi[:, q % SPLITS, :], ps[:, 4 + q % 4, :], ACT.Copy).then_inc(hi_ready, 1)

            def gelu(pair, t, is_late):
                act.wait_ge(split_free, pair * 8 + (Q_U + SPLITS + 4 * t + 4))
                if is_late:
                    act.wait_ge(late_used, pair * 2 + (t + 1 - LATE))
                    dst = late[:, t, :]
                else:
                    dst = wexp[:, bass.ds(pair * 2 + t, 1), :].rearrange("p a t -> p (a t)")
                nc.scalar.activation(dst, ps[:, t, 0:SEQ], ACT.Gelu).then_inc(score_free, 1)

            def hot_rows(n, parity):
                act.wait_ge(dist_ready, n + 1)
                d = hot[:, parity, :, :, :].rearrange("p a t k -> p (a t k)")
                nc.scalar.activation(d, d, ACT.Abs).then_inc(abs_ready, 1)
                act.wait_ge(abs_ready, n + 1)
                nc.scalar.activation(d, d, ACT.Relu, scale=-1.0, bias=1.0).then_inc(hot_ready, 1)

            def u_pair(pair, part_a, next_a, late_tiles=(), groups=None):
                for q in range(4, 8):
                    split_u(pair, q, part_a)
                gelu(pair, 0, 0 in late_tiles)
                split_u(pair + 1, 0, next_a)
                if groups is not None:
                    hot_rows(groups, 0)
                for q in range(1, 4):
                    split_u(pair + 1, q, next_a)
                gelu(pair, 1, 1 in late_tiles)
                if groups is not None:
                    hot_rows(groups + 1, 1)

            act.wait_ge(x1_out, 16)
            act.sem_inc(late_used, 2)
            nc.scalar.preload_act_table_set("gelu_and_others")
            for q in range(4):
                split_u(0, q, True)
            with act.Fori(0, PAIRS_A - 6) as i:
                u_pair(i, True, True)
            act.wait_ge(best_ready, 1)
            nc.scalar.activation(best[:, :, :], best[:, :, :], ACT.Exp).then_inc(exp_ready, 1)
            nc.scalar.preload_act_table_set("gelu_and_others")
            with act.Fori(PAIRS_A - 6, PAIRS_A - 1) as i:
                u_pair(i, True, True)
            u_pair(PAIRS_A - 1, True, False, (1,))
            u_pair(PICKS, False, False, (0, 1))
            with act.Fori(GATE0 - 1, GATE0 - 1 + GATES // 2) as i:
                u_pair(i, False, False, (0, 1), i * 2 - (2 * GATE0 - 2))
            with act.Fori(GATE0 - 1 + GATES // 2, PAIRS - 1) as i:
                u_pair(i, False, False, (0, 1))
            for q in range(4, 8):
                split_u(PAIRS - 1, q, False)

            def split_w(n, t, static=False):
                act.wait_ge(split_free, n + (Q_V + SPLITS + 4 * t - 4) if static or t > 0 else n + (Q_V + SPLITS - 4))
                nc.scalar.activation(whalf_hi[:, t % 2, :],
                                     wexp[:, bass.ds(n // 4 + t, 1), :].rearrange("p a t -> p (a t)"), ACT.Copy
                                     ).then_inc(w_hi, 1)

            act.wait_ge(gates_free, GATES + 2)
            split_w(0, 0)
            gelu(PAIRS - 1, 0, True)
            for q in range(3):
                split(Q_V, q, True)
            gelu(PAIRS - 1, 1, True)
            split(Q_V, 3, True)
            act.wait_ge(late_used, NT - LATE + 2)

            with act.Fori(0, NT // 2 - 1) as i:
                split_w(i * 8, 1)
                for q in range(4, 8):
                    split(i * 8 + Q_V, q, True)
                split_w(i * 8, 2)
                for q in range(4):
                    split(i * 8 + (Q_V + 8), q, True)
            n = NT * 4 - 8
            split_w(n, 1)
            for q in range(4, 8):
                split(n + Q_V, q, True)

        @block.vector
        def _(dve):
            chain = Chain(dve, v_chain)
            vec = nc.vector

            def split(n, q):
                dve.wait_ge(hi_ready, n + (q + 1))
                vec.tensor_tensor(split_lo[:, q % SPLITS, :], raw[:, q // 2, q % 2, :],
                                  split_hi[:, q % SPLITS, :].bitcast(f32), ALU.subtract).then_inc(lo_ready, 1)

            def dense_group(g, after=None):
                for q in range(4, 20):
                    split(g * KT + q // 8 * 8, q % 8)
                    if after:
                        after(q)

            def turned_lo(first, order):
                for f in range(first, first + 8):
                    dve.wait_ge(turn_hi, order * 8 + f - first + 1)
                    fb, k = (f - first) // 4, (f - first) % 4 * 4
                    vec.tensor_tensor(act_lo[:, k:k + 4, fb * P:(fb + 1) * P],
                                      ps[:, 4 + f % 4, :].rearrange("p (k t) -> p k t", k=4),
                                      act_hi[:, k:k + 4, fb * P:(fb + 1) * P].bitcast(f32), ALU.subtract
                                      ).then_inc(turn_done, 1)

            turned_lo(F_X, 0)
            for q in range(4):
                split(0, q)
            with dve.Fori(0, SB_GROUP) as i:
                dense_group(i)

            def sb_head(it):
                def after(q):
                    if q == AT_Z + 4:
                        dve.wait_ge(soft_abs, it + 1)
                        vec.tensor_tensor(z_sb[:, :], ps[:, 5, 0:384], masked, ALU.subtract).then_inc(z_masked, 1)
                    if q == AT_Z + 7:
                        dve.wait_ge(soft_ready, it + 1)
                        dve.wait_ge(a_ready, it)
                        dve.wait_ge(z_masked, it + 1)
                        vec.scalar_tensor_tensor(out=soft_p[:, :], in0=z_sb[:, :], scalar=0.0, in1=soft_l[:, :],
                                                 op0=ALU.max, op1=ALU.add).then_inc(soft_max, 1)
                        dve.wait_ge(soft_max, it + 1)
                        vec.tensor_tensor(soft_p[:, :], soft_p[:, :], causal, ALU.mult).then_inc(spm_ready, 1)
                    if q == AT_SUMS + 4:
                        dve.wait_ge(c_ready, it + 1)
                        vec.tensor_tensor(soft_p[:, :], z_sb[:, :], ps[:, 6, 0:384], ALU.subtract).then_inc(la_ready, 1)
                    if q == AT_VALUES + 6:
                        dve.wait_ge(o_out, it + 1)
                        for b in range(TB):
                            vec.bn_stats(bn_sb[:, b, bass.ds(it * 6, 6)], mixed[:, b, bass.ds(it * HD, HD)]
                                         ).then_inc(sb_bn_ready, 1)
                return after

            dve.wait_ge(tab_in, 16 * TABLE_PIECES)
            with dve.Fori(SB_GROUP, G_IN) as i:
                dense_group(i, sb_head(i - SB_GROUP))

            dve.wait_ge(acc_free, G_IN + 2)
            dve.wait_ge(o_out, SBH)
            dve.wait_ge(norms_in, 32)
            heads = SBH + RTH
            m4 = mixed[:, :, :].rearrange("p b (h d) -> p b h d", h=heads)
            sb = slice(0, SBH * HD)

            def keys_out(it):
                dve.wait_ge(q_out, it + 1)
                dve.wait_ge(z_ready, max(SBH, SBH + it - 1))
                bank = it % 2 * 4 if it < RT_FIRST else 4
                vec.tensor_copy(qk_t[:, it % 2, 1, :], ps[:, bank, 256:512]).then_inc(k_out, 1)

            def decayed(it):
                p = it % 2
                dve.wait_ge(z_ready, SBH + it + 1)
                dve.wait_ge(o_ready, max(SBH, SBH + it - 1))
                bank = p * 4 + 1 if it < RT_FIRST else 5
                vec.tensor_tensor(soft_a[:, p, :], ps[:, bank, 0:384], decay[:, it, :], ALU.mult
                                  ).then_inc(a_ready, 1)

            def sb_variances():
                dve.wait_ge(sb_bn_ready, SBH * TB)
                for b in range(TB):
                    for h in range(SBH):
                        chain.add(vec.bn_aggr(moments_sb[:, b, h, :], bn_sb[:, b, 6 * h:6 * h + 6]))
                dve.wait_ge(v_chain, chain.n)
                own = stats[:, VAR:VAR + TB * SBH].rearrange("p (b h) -> p b h", b=TB)
                mean, var = moments_sb[:, :, :, 0], moments_sb[:, :, :, 1]
                chain.step(vec.tensor_tensor(own, mean, mean, ALU.mult))
                vec.scalar_tensor_tensor(out=own, in0=own, scalar=NORM_EPS, in1=var, op0=ALU.add, op1=ALU.add
                                         ).then_inc(var_ready, 1)

            def sb_norm(b):
                dve.wait_ge(rstd_ready, 1)
                chain.step(vec.tensor_tensor(m4[:, b, 0:SBH, :], m4[:, b, 0:SBH, :],
                                             stats[:, RSTD + SBH * b:RSTD + SBH * (b + 1)].unsqueeze(2)
                                             .to_broadcast([P, SBH, HD]), ALU.mult))
                vec.tensor_tensor(mixed[:, b, sb], mixed[:, b, sb], norm_w[:, sb], ALU.mult).then_inc(sb_ready, 1)

            def head_stats(it):
                dve.wait_ge(o_out, SBH + it + 1)
                for b in range(TB):
                    chain.add(vec.bn_stats(bn[:, b, it, :], m4[:, b, SBH + it, :]))

            bn = stats[:, BN:BN + TB * RTH * 6].rearrange("p (b h s) -> p b h s", b=TB, h=RTH)
            between = {0: sb_variances, 2: lambda: sb_norm(0), 3: lambda: sb_norm(1)}
            for s in range(RT_FIRST + 3):
                if s < RT_FIRST:
                    keys_out(s)
                if 0 <= s - 1 < RT_FIRST:
                    decayed(s - 1)
                if s in between:
                    between[s]()
                if 0 <= s - 3 < RT_FIRST:
                    head_stats(s - 3)

            def head_moments(it):
                for b in range(TB):
                    chain.add(vec.bn_aggr(moments[:, b, it, :], bn[:, b, it, :]))

            def head_variances():
                dve.wait_ge(v_chain, chain.n)
                for it in range(RT_FIRST, RTH):
                    head_moments(it)
                dve.wait_ge(v_chain, chain.n)
                vec.tensor_scalar(stats[:, VAR:VAR + TB * RTH].rearrange("p (b h) -> p b h", b=TB),
                                  moments[:, :, :, 1], NORM_EPS, None, ALU.add).then_inc(var_ready, 1)

            NORM_STEPS = TB * 5

            def norm_step(step):
                b, part = step // 5, step % 5
                if part < 4:
                    if step == 0:
                        dve.wait_ge(rstd_ready, 2)
                    for it in (2 * part, 2 * part + 1):
                        r = RSTD + RTH * b + it
                        chain.add(vec.tensor_scalar(m4[:, b, SBH + it, :], m4[:, b, SBH + it, :],
                                                    moments[:, b, it, 0:1], stats[:, r:r + 1],
                                                    ALU.subtract, ALU.mult))
                else:
                    dve.wait_ge(v_chain, chain.n)
                    dve.wait_ge(gate_weighted, TB)
                    ret = slice(SBH * HD, D)
                    vec.tensor_tensor(mixed[:, b, ret], mixed[:, b, ret], proj[:, b, INW - RTH * HD:INW], ALU.mult
                                      ).then_inc(mixed_ready, 1)

            def mixed_lo(kind):
                for f in range(4):
                    dve.wait_ge(turn_hi, HALF + 4 * kind + f + 1)
                    k = kind * HALF + f % 2 * 4
                    part = act_hi[:, k:k + 4, f // 2 * P:(f // 2 + 1) * P]
                    vec.tensor_tensor(act_lo[:, k:k + 4, f // 2 * P:(f // 2 + 1) * P],
                                      ps[:, 4 + f, :].rearrange("p (k t) -> p k t", k=4), part.bitcast(f32),
                                      ALU.subtract).then_inc(turn_done, 1)

            mixed_lo(0)
            dve.wait_ge(v_chain, chain.n)
            for it in range(RT_FIRST):
                head_moments(it)
            for n in range(4, 20):
                split(Q_OUT + n // 8 * 8, n % 8)
                it = RT_FIRST + n - 4
                if it < RTH:
                    keys_out(it)
                if RT_FIRST <= it - 1 < RTH:
                    decayed(it - 1)
                if RT_FIRST <= it - 3 < RTH:
                    head_stats(it - 3)
                if it == RTH + 3:
                    head_variances()
                if it > RTH + 3 and it - RTH - 4 < NORM_STEPS:
                    norm_step(it - RTH - 4)
            for step in range(20 - 4 + RT_FIRST - RTH - 4, NORM_STEPS):
                norm_step(step)
            mixed_lo(1)

            def residual(g):
                dve.wait_ge(split_free, Q_OUT + g // 2 * 4 * HALF + (3 + g % 2) * HALF + SPLITS)
                s, part = g % 2, x_nat[:, :, g * COLS:(g + 1) * COLS]
                vec.scalar_tensor_tensor(out=part, in0=part, scalar=ALPHA, in1=ps[:, 2 * s:2 * s + 2, :],
                                         op0=ALU.mult, op1=ALU.add).then_inc(acc_free, 1)
                dve.wait_ge(acc_free, G_IN + g + 3)
                for b in range(TB):
                    at_g = BN + 24 * b + 6 * g
                    vec.bn_stats(stats[:, at_g:at_g + 6], x_nat[:, b, g * COLS:(g + 1) * COLS]).then_inc(bn_ready, 1)

            for n in range(20, G_OUT * KT + 4):
                split(Q_OUT + n // 8 * 8, n % 8)
                if n % 32 == 27:
                    residual(n // 32 * 2)
                if n % 32 == 3:
                    residual(n // 32 * 2 - 1)

            def row_stats(n):
                for b in range(TB):
                    chain.add(vec.bn_aggr(stats[:, MEAN + 2 * b:MEAN + 2 * b + 2], stats[:, BN + 24 * b:BN + 24 * b + 24]))
                dve.wait_ge(v_chain, chain.n)
                vec.tensor_scalar(stats[:, VAR:VAR + TB], stats[:, MEAN + 1:MEAN + 2 * TB:2], LN_EPS, None, ALU.add
                                  ).then_inc(var_ready, 1)
                dve.wait_ge(rstd_ready, n + 3)

            def layer_norm(buf, w, b_, blk, cols):
                part = buf[:, blk, cols]
                chain.step(vec.scalar_tensor_tensor(out=part, in0=part, scalar=stats[:, MEAN + 2 * blk:MEAN + 2 * blk + 1],
                                                    in1=w[:, cols], op0=ALU.subtract, op1=ALU.mult))
                return vec.scalar_tensor_tensor(out=part, in0=part, scalar=stats[:, RSTD + blk:RSTD + blk + 1],
                                                in1=b_[:, cols], op0=ALU.mult, op1=ALU.add)

            dve.wait_ge(bn_ready, G_OUT * TB)
            dve.wait_ge(ln1_in, 32)
            row_stats(0)
            for b in range(TB):
                layer_norm(x_nat, ln_w, ln_b, b, slice(0, D)).then_inc(x1_ready, 1)

            turned_lo(F_X1, 2)
            with dve.Fori(0, G_PQ - 1) as i:
                dense_group(i + (G_IN + G_OUT))
            g = G_IN + G_OUT + G_PQ - 1
            for q in range(4, 16):
                split(g * KT + q // 8 * 8, q % 8)
            for f in range(8):
                dve.wait_ge(turned, F_Q + f + 1)
                vec.tensor_copy(q_t[:, f % 4 * 4:f % 4 * 4 + 4, f // 4 * P:(f // 4 + 1) * P],
                                ps[:, 4 + f % 4, :].rearrange("p (k t) -> p k t", k=4)).then_inc(turn_done, 1)

            def split_u(pair, q):
                dve.wait_ge(hi_ready, pair * 8 + (Q_U + q + 1))
                vec.tensor_tensor(split_lo[:, q % SPLITS, :], ps[:, 4 + q % 4, :],
                                  split_hi[:, q % SPLITS, :].bitcast(f32), ALU.subtract).then_inc(lo_ready, 1)

            def turn_u(pair, k, own, part_a):
                if k not in own:
                    return
                dve.wait_ge(raw_ready[k], u_raw(k, pair, part_a))
                dve.wait_ge(lo_ready, pair * 8 + (Q_U + 2 * k - 2))
                bank = 4 + k % 2 * 2
                vec.transpose(ps[:, bank:bank + 2, :].rearrange("p a (c g i) -> p g (a c) i", g=4, i=32),
                              raw[:, k, :, :].rearrange("p a (b q c) -> p (a b) c q", b=2, q=32)
                              ).then_inc(dve_turned, 1)

            def split_turn(pair, k, own, part_a, nxt=None, next_a=False, between=None, behind=None):
                split_u(pair, 2 * k)
                if between:
                    between()
                split_u(pair, 2 * k + 1)
                if behind:
                    behind()
                if nxt is not None:
                    turn_u(pair + 1, k - 2, nxt, next_a)

            class LoopChain:

                def __init__(self, i, first, steps):
                    self.i, self.first, self.steps, self.n = i, first, steps, 0

                def add(self, instruction):
                    self.n += 1
                    instruction.then_inc(v_chain, 1)

                def step(self, instruction):
                    self.add(instruction)
                    dve.wait_ge(v_chain, self.i * self.steps + (self.first + self.n))
                    dve.sem_inc(carried, 1)

            def flat(ap, pattern="p a b -> p (a b)"):
                return ap.rearrange(pattern)

            sc3 = flat(scores[:, :, :, :], "p b s k -> p (b s) k")
            TOP_STEPS = 18
            dve.wait_ge(sc_out, 8)
            c0 = chain.n
            dve.wait_ge(turn_done, F_Q + 8)
            for k in range(2):
                turn_u(0, k, DVE_A, True)
            for k in range(2):
                split_u(0, 2 * k)
                split_u(0, 2 * k + 1)
                turn_u(0, k + 2, DVE_A, True)
            with dve.Fori(0, TB * PH) as i:
                lc = LoopChain(i, c0, TOP_STEPS)
                halves = range(2)
                half_rest = [rest[:, c * PKEYS:(c + 1) * PKEYS] for c in halves]

                def largest():
                    lc.step(vec.tensor_copy(head_s[:, :, :], sc3[:, bass.ds(i * 2, 2), :]))
                    lc.add(vec.max(top_v[:, 0, 0:8], head_s[:, 0, :]))
                    lc.step(vec.max(top_v[:, 1, 0:8], head_s[:, 1, :]))

                def their_places():
                    for c in halves:
                        lc.add(vec.max_index(head_i[:, c, 0:8], top_v[:, c, 0:8], head_s[:, c, :]))
                    lc.add(vec.match_replace(half_rest[0], top_v[:, 0, 0:8], head_s[:, 0, :], LOWEST))
                    lc.step(vec.match_replace(half_rest[1], top_v[:, 1, 0:8], head_s[:, 1, :], LOWEST))

                def next_largest():
                    lc.add(vec.max(top_v[:, 0, 8:16], half_rest[0]))
                    lc.step(vec.max(top_v[:, 1, 8:16], half_rest[1]))
                    for c in halves:
                        lc.add(vec.max_index(head_i[:, c, 8:16], top_v[:, c, 8:16], half_rest[c]))

                def candidates():
                    lc.step(vec.tensor_tensor(cand[:, :, :], top_v[:, 0, :].unsqueeze(2).to_broadcast([P, TOPK, TOPK]),
                                              top_v[:, 1, :].unsqueeze(1).to_broadcast([P, TOPK, TOPK]), ALU.add))
                    lc.step(vec.max(head_b[:, 0:8], flat(cand[:, :, :])))

                def their_sums():
                    lc.add(vec.max_index(head_p[:, 0:8], head_b[:, 0:8], flat(cand[:, :, :])))
                    lc.step(vec.match_replace(rest[:, :], head_b[:, 0:8], flat(cand[:, :, :]), LOWEST))
                    lc.step(vec.max(head_b[:, 8:16], rest[:, :]))
                    lc.step(vec.max_index(head_p[:, 8:16], head_b[:, 8:16], rest[:, :]))

                def keep_picks():
                    vec.tensor_copy(idx_u[:, bass.ds(i, 1), :, :].rearrange("p a c k -> p (a c) k"), head_i[:, :, :])
                    vec.tensor_copy(best[:, bass.ds(i, 1), :].rearrange("p a k -> p (a k)"), head_b[:, :])
                    lc.step(vec.tensor_copy(pos_u[:, bass.ds(i, 1), :].rearrange("p a k -> p (a k)"), head_p[:, :]))

                split_turn(i, 2, DVE_A, True, DVE_A, True, between=largest, behind=their_places)
                split_turn(i, 3, DVE_A, True, DVE_A, True, between=next_largest)
                split_turn(i, 4, DVE_A, True, DVE_A, True, between=candidates, behind=their_sums)
                split_turn(i, 5, DVE_A, True, DVE_A, True, between=keep_picks)
                assert lc.n == TOP_STEPS
            chain.n += TB * PH * TOP_STEPS

            def late_tile(pair, t):
                dve.wait_ge(score_free, pair * 2 + (t + 3))
                row = wexp[:, bass.ds(pair * 2 + t, 1), :].rearrange("p a t -> p (a t)")
                vec.tensor_tensor(row, row, late[:, t % 2, :], ALU.mult).then_inc(late_used, 1)

            def apply_gates(n, parity):
                dve.wait_ge(gate_ready, n + 1)
                part = wexp[:, :, bass.ds(n * 4, 4)]
                dve.wait_ge(late_used, n + (2 * GATE0 - LATE + 2))
                vec.tensor_tensor(part, part, ps[:, 2 + parity, :].rearrange("p (t j) -> p j t", t=4), ALU.mult
                                  ).then_inc(gates_free, 1)

            def u_pair(pair, own, part_a, nxt, next_a, late_tiles=False, groups=None, between=None):
                for k in (2, 3):
                    split_turn(pair, k, own, part_a, nxt, next_a)
                    if late_tiles and k == 2:
                        if groups is not None and not isinstance(groups, int):
                            dve.wait_ge(gates_free, groups + 2)
                        late_tile(pair, -1)
                if groups is not None:
                    apply_gates(groups, 0)
                for k in (4, 5):
                    split_turn(pair, k, own, part_a, nxt, next_a)
                    if late_tiles and k == 4:
                        if groups is not None:
                            dve.wait_ge(gates_free, groups + 3)
                        late_tile(pair, 0)
                if groups is not None:
                    apply_gates(groups + 1, 1)
                if between:
                    between()

            def softmax_start():
                chain.step(vec.tensor_copy(gsum[:, 0, :], best[:, :, 0]))
                vec.tensor_tensor(best[:, :, :], best[:, :, :], gsum[:, 0, :].unsqueeze(2)
                                  .to_broadcast([P, TB * PH, TOPK]), ALU.subtract).then_inc(best_ready, 1)
                chain.step(vec.tensor_scalar(pos_i[:, 0, :, :], pos_u[:, :, :], 4, None, ALU.logical_shift_right))
                chain.step(vec.tensor_scalar(pos_i[:, 1, :, :], pos_u[:, :, :], TOPK - 1, None, ALU.bitwise_and))
                chain.step(vec.tensor_copy(flat(pos_f[:, :, :, :], "p a b c -> p (a b c)"),
                                           flat(pos_i[:, :, :, :], "p a b c -> p (a b c)")))
                chain.step(vec.tensor_copy(flat(idx_f[:, :, :, :], "p a b c -> p (a b c)"),
                                           flat(idx_u[:, :, :, :], "p a b c -> p (a b c)")))

            u_pair(SOFT, DVE_A, True, DVE_A, True, between=softmax_start)

            DEC_STEPS = 6
            c1 = chain.n
            with dve.Fori(0, TB * PH // 2) as i:
                lc = LoopChain(i, c1, DEC_STEPS)
                o4 = onehot[:, :, :].rearrange("p (a k) j -> p a k j", a=2)

                def compare(h):
                    row = pos_f[:, h, bass.ds(i * 2, 2), :].rearrange("p a k -> p (a k)")
                    lc.step(vec.tensor_tensor(onehot[:, :, :], row.unsqueeze(2).to_broadcast([P, 2 * TOPK, TOPK]),
                                              iota[:, 0:TOPK].unsqueeze(1).to_broadcast([P, 2 * TOPK, TOPK]),
                                              ALU.is_equal))

                def select(h):
                    lc.step(vec.tensor_tensor(o4, o4, idx_f[:, bass.ds(i * 2, 2), h, :].unsqueeze(2)
                                              .to_broadcast([P, 2, TOPK, TOPK]), ALU.mult))

                def collect(h):
                    dst = pick_n[:, h, :, :].rearrange("p b k -> p (b k)")
                    lc.step(vec.tensor_reduce(dst[:, bass.ds(i * 2 * TOPK, 2 * TOPK)], onehot[:, :, :], AX.X, ALU.add))

                for h in range(2):
                    split_turn(i + (SOFT + 1), 2 + 2 * h, DVE_A, True, DVE_A, True,
                               between=lambda: compare(h), behind=lambda: select(h))
                    split_turn(i + (SOFT + 1), 3 + 2 * h, DVE_A, True, DVE_A, True, between=lambda: collect(h))
                assert lc.n == DEC_STEPS
            chain.n += TB * PH // 2 * DEC_STEPS

            def softmax_end():
                dve.wait_ge(exp_ready, 1)
                chain.step(vec.tensor_reduce(gsum[:, 0, :], best[:, :, :], AX.X, ALU.add))
                chain.step(vec.reciprocal(gsum[:, 1, :], gsum[:, 0, :]))
                vec.tensor_tensor(pick_n[:, 2, :, :].rearrange("p b (h k) -> p (b h) k", k=TOPK), best[:, :, :],
                                  gsum[:, 1, :].unsqueeze(2).to_broadcast([P, TB * PH, TOPK]), ALU.mult
                                  ).then_inc(topk_done, 1)

            assert SOFT + 1 + TB * PH // 2 == PAIRS_A - 1
            u_pair(PAIRS_A - 1, DVE_A, True, DVE_B, False, between=softmax_end)

            def picks_out():
                dve.wait_ge(picks_turned, 1)
                chain.step(vec.tensor_copy(picks_t[:, 0, :], ps[:, 2, 0:SEQ]))
                chain.step(vec.tensor_copy(picks_t[:, 1, :], ps[:, 3, 0:SEQ]))
                vec.tensor_copy(picks_t[:, 2, :], ps[:, 2, SEQ:2 * SEQ]).then_inc(picks_ready, 1)
                dve.sem_inc(gates_free, 2)

            dve.wait_ge(ones_ready, 1)
            u_pair(PICKS, DVE_B, False, DVE_B, False, True, between=picks_out)
            dve.wait_ge(ones_ready, 2)
            u_pair(PICKS + 1, DVE_B, False, DVE_B, False, True)
            with dve.Fori(GATE0, GATE0 + GATES // 2) as i:
                u_pair(i, DVE_B, False, DVE_B, False, True, i * 2 - 2 * GATE0)
            dve.wait_ge(gates_free, GATES + 2)
            with dve.Fori(GATE0 + GATES // 2, PAIRS - 1) as i:
                u_pair(i, DVE_B, False, DVE_B, False, True)
            split_turn(PAIRS - 1, 2, DVE_B, False)
            late_tile(PAIRS - 1, -1)
            split_turn(PAIRS - 1, 3, DVE_B, False)

            def split_w(n, t):
                dve.wait_ge(w_hi, (n // 4 + t + 1) if isinstance(n, int) else n // 4 + (t + 1))
                vec.tensor_tensor(whalf_lo[:, t % 2, :], wexp[:, bass.ds(n // 4 + t, 1), :].rearrange("p a t -> p (a t)"),
                                  whalf_hi[:, t % 2, :].bitcast(f32), ALU.subtract).then_inc(w_lo, 1)

            split_w(0, 0)
            for q in range(3):
                split(Q_V, q)
            late_tile(PAIRS - 1, 0)
            split(Q_V, 3)
            late_tile(PAIRS - 1, 1)
            with dve.Fori(0, NT // 2 - 1) as i:
                split_w(i * 8, 1)
                for q in range(4, 8):
                    split(i * 8 + Q_V, q)
                split_w(i * 8, 2)
                for q in range(4):
                    split(i * 8 + (Q_V + 8), q)
            n = NT * 4 - 8
            split_w(n, 1)
            for q in range(4, 8):
                split(n + Q_V, q)

            dve.wait_ge(x1_in, 16 * TB)
            dve.wait_ge(ln2_in, 32)
            for b in range(TB):
                dve.wait_ge(values_ready, b + 1)
                chain.step(vec.scalar_tensor_tensor(out=y_out[:, b, :], in0=x1_back[:, b, :], scalar=ALPHA,
                                                    in1=ps[:, 4 * b:4 * b + 4, :].rearrange("p n c -> p (n c)"),
                                                    op0=ALU.mult, op1=ALU.add))
                for c in range(4):
                    at_c = BN + 24 * b + 6 * c
                    chain.add(vec.bn_stats(stats[:, at_c:at_c + 6], y_out[:, b, c * COLS:(c + 1) * COLS]))
            dve.wait_ge(v_chain, chain.n)
            row_stats(1)
            for b in range(TB):
                for h in range(2):
                    layer_norm(y_out, ln2w, ln2b, b, slice(h * 1024, h * 1024 + 1024)).then_inc(y_ready, 1)

        @block.gpsimd
        def _(pool):
            chain = Chain(pool, g_chain)
            eng = nc.gpsimd
            eng.memset(stats[:, NHALF:NHALF + 32], -0.5).then_inc(halfexp, 1)

            eng.memset(scales[:, 0:1], SCALE).then_inc(scales_ready, 1)
            eng.memset(scales[:, 1:2], 1.0).then_inc(scales_ready, 1)

            def stage_head(it):
                pool.wait_ge(qk_turned, it)
                qk = proj[:, :, 0:2 * SBH * HD].rearrange("p b (a c) -> p a b c", a=2)
                eng.tensor_tensor(stage[:, :, :, :], qk[:, :, :, bass.ds(it * HD, HD)],
                                  scales[:, :].unsqueeze(2).unsqueeze(3).to_broadcast([P, 2, TB, HD]), ALU.mult
                                  ).then_inc(staged, 1)

            rot = mixed[:, :, SBH * HD:D].rearrange("p a (h d) -> p a h d", h=RTH)

            def rotary(kind):
                first_col = (3 * SBH + kind * RTH) * HD
                half = HD // 2
                for b in range(TB):
                    xs = proj[:, b, first_col:first_col + RTH * HD].rearrange("p (h d) -> p h d", h=RTH)
                    chain.add(eng.tensor_tensor(rot[:, 1, :, 0:half], xs[:, :, half:HD],
                                                sin_t[:, b:b + 1, 0:half].to_broadcast([P, RTH, half]), ALU.mult))
                    chain.add(eng.tensor_tensor(rot[:, 1, :, half:HD], xs[:, :, 0:half],
                                                sin_t[:, b:b + 1, half:HD].to_broadcast([P, RTH, half]), ALU.mult))
                    chain.step(eng.tensor_tensor(rot[:, 0, :, :], xs,
                                                 cos_t[:, b:b + 1, :].to_broadcast([P, RTH, HD]), ALU.mult))
                    eng.tensor_tensor(xs, rot[:, 0, :, :], rot[:, 1, :, :], ALU.add).then_inc(rot_ready, 1)
                    pool.wait_ge(rot_ready, TB * kind + b + 1)

            pool.wait_ge(scales_ready, 2)
            pool.wait_ge(acc_free, SB_GROUP + 2)
            with pool.Fori(0, 3) as i:
                stage_head(i)
            pool.wait_ge(tab_in, 16 * TABLE_PIECES)
            q_groups, k_groups = ((3 * SBH + n * RTH) * HD // COLS for n in (1, 2))
            pool.wait_ge(acc_free, q_groups + 2)
            rotary(0)
            with pool.Fori(3, 5) as i:
                stage_head(i)
            pool.wait_ge(acc_free, k_groups + 2)
            rotary(1)
            with pool.Fori(5, SBH) as i:
                stage_head(i)
            pool.wait_ge(halfexp, 1)
            for n in range(4):
                pool.wait_ge(var_ready, n + 1)
                w = 16 if n < 2 else TB
                eng.tensor_tensor(stats[:, RSTD:RSTD + w], stats[:, VAR:VAR + w],
                                  stats[:, NHALF:NHALF + w], ALU.pow).then_inc(rstd_ready, 1)
                if n == 0:
                    pool.wait_ge(gated, 1)
                    pool.wait_ge(norms_in, 32)
                    for b in range(TB):
                        cols = slice(INW - RTH * HD, INW)
                        eng.tensor_tensor(proj[:, b, cols], proj[:, b, cols], norm_w[:, SBH * HD:D], ALU.mult
                                          ).then_inc(gate_weighted, 1)
                if n == 2:
                    pool.wait_ge(x1_out, 16)
                    pool.wait_ge(sc_ready, 8)
                    top = 96
                    eng.memset(wexp[:, LATE:top, :], 1.0).then_inc(ones_ready, 1)
                    pool.wait_ge(topk_done, 1)
                    eng.memset(wexp[:, top:NT, :], 1.0).then_inc(ones_ready, 1)
                    pool.wait_ge(picks_ready, 1)

                    def distances(n, parity, wait):
                        if wait:
                            pool.wait_ge(gate_ready, n - 1)
                        eng.tensor_tensor(hot[:, parity, :, :, :],
                                          iota.unsqueeze(1).unsqueeze(1).to_broadcast([P, 2, 4, P]),
                                          picks_t[:, 0:2, bass.ds(n * 4, 4)].unsqueeze(3).to_broadcast([P, 2, 4, P]),
                                          ALU.subtract).then_inc(dist_ready, 1)

                    def weigh(n, parity):
                        pool.wait_ge(hot_ready, n + 1)
                        rows = hot[:, parity, 1, :, :]
                        eng.tensor_tensor(rows, rows, picks_t[:, 2, bass.ds(n * 4, 4)].unsqueeze(2)
                                          .to_broadcast([P, 4, P]), ALU.mult).then_inc(weighted, 1)

                    distances(0, 0, False)
                    distances(1, 1, False)
                    with pool.Fori(0, GATES // 2 - 1) as i:
                        for s in range(2):
                            weigh(i * 2 + s, s)
                            distances(i * 2 + (s + 2), s, True)
                    weigh(GATES - 2, 0)
                    weigh(GATES - 1, 1)


def constant_tables():
    inv = 10000.0 ** (-np.arange(0, HD, 2, dtype=np.float32) / HD)
    ang = np.arange(SEQ, dtype=np.float32)[:, None] * inv.astype(np.float32)[None, :]
    ang = np.concatenate([ang, ang], -1).astype(np.float32)
    cos, sin = np.cos(ang), np.sin(ang)
    sin[:, :HD // 2] *= -1
    by_block = lambda a: a.reshape(TB, P, HD).transpose(1, 0, 2).reshape(P, TB * HD)
    log_g = np.log1p(-(2.0 ** (-5.0 - np.arange(RTH, dtype=np.float64))))
    j, i = np.arange(P)[:, None], np.arange(SEQ)[None, :]
    seen = (i // CHUNK) >= (j // CHUNK)
    dist = np.abs(i - j)
    decay = np.where(seen[None], np.exp(log_g[:, None, None] * dist[None]), 0.0) * SCALE
    decay = np.concatenate([decay, decay[:, :, :P]], -1).transpose(1, 0, 2).reshape(P, RTH * 384)
    r, c = np.arange(P)[:, None], np.arange(P)[None, :]
    causal = np.concatenate([j < i, r < c], -1)
    cst = np.concatenate([by_block(cos), by_block(sin), decay, (r >= c), np.ones((P, P)), causal,
                          np.where(causal, 0.0, BIG)], -1).astype(np.float32)
    small = np.stack([np.eye(P), np.broadcast_to(np.arange(P), (P, P))], 1).astype(np.float32)
    return np.ascontiguousarray(cst), np.ascontiguousarray(small)


_INS = ["x", "w_in", "sb_norm_w", "ret_norm_w", "w_out", "ln1_w", "ln1_b", "w_pq", "sub_keys",
        "expert_u", "expert_v", "ln2_w", "ln2_b"]


def kernel(**inputs):
    import concourse.bacc as _bacc
    from concourse.bass_utils import run_bass_kernel_spmd as _run

    nc = _bacc.Bacc("TRN2", target_bir_lowering=False, num_devices=1)
    cst, small = constant_tables()
    arrays, args = {}, []
    named = [(n, np.ascontiguousarray(inputs[n])) for n in _INS] + [("tables", cst), ("small_tables", small)]
    for name, a in named:
        arrays[f"in_{name}"] = a
        args.append(nc.dram_tensor(f"in_{name}", a.shape, mybir.dt.from_np(a.dtype), kind="ExternalInput").ap())
    args.append(nc.dram_tensor("out_y", (1, SEQ, D), mybir.dt.float32, kind="ExternalOutput").ap())
    layer_kernel(nc, *args)
    r = _run(nc, [arrays], core_ids=[0])
    return r.results[0]["out_y"]
```
